# Optimizing a Trainium2 kernel written in Bass

```python
import math
import jax
import jax.numpy as jnp
from jax import lax
import numpy as np

D_MODEL = 1024
BATCH = 1
SEQ = 512
DEPTH = 1

N_META = 16
ROPE_THETA = 10000.0
EPS = 1e-6
A_HEAD_DIM = 64
A_HEADS = (D_MODEL // 2) // A_HEAD_DIM
A_WIDTH = A_HEADS * A_HEAD_DIM
KV_RANK = D_MODEL // 4
IDX_HEADS = 8
IDX_DIM = 64
INDEX_TOPK = 256
Q_BLOCK = 128
B_HEAD_DIM = 128
B_HEADS = (D_MODEL // 2) // B_HEAD_DIM
B_WIDTH = B_HEADS * B_HEAD_DIM
CONV_WIDTH = 4
CHUNK = 64
MIX_WIDTH = A_WIDTH + B_WIDTH
N_EXPERTS = 32
TOP_K = 4
D_FF = D_MODEL
SWIGLU_LIMIT = 7.0
SWIGLU_ALPHA = 1.702
MOE_BLOCK = 128
IN_SPLITS = (A_WIDTH, KV_RANK, IDX_HEADS * IDX_DIM, IDX_DIM, IDX_HEADS, 3 * B_WIDTH, B_WIDTH, B_HEADS, B_HEADS)
IN_COLS = A_WIDTH + KV_RANK + IDX_HEADS * IDX_DIM + IDX_DIM + IDX_HEADS + 4 * B_WIDTH + 2 * B_HEADS

kernel_name = "hybrid_dsa_gdn_moe_meta"

def rms_norm(x, w):
    xf = x.astype(jnp.float32)
    y = xf * lax.rsqrt(jnp.mean(xf * xf, axis=-1, keepdims=True) + EPS)
    return (y * w.astype(jnp.float32)).astype(x.dtype)

def l2_normalize(x):
    return x * lax.rsqrt(jnp.sum(x * x, axis=-1, keepdims=True) + EPS)

def rope_tables(n_pos, dim):
    inv_freq = ROPE_THETA ** (-jnp.arange(0, dim, 2, dtype=jnp.float32) / dim)
    ang = jnp.arange(n_pos, dtype=jnp.float32)[:, None] * inv_freq[None, :]
    return jnp.cos(ang), jnp.sin(ang)

def apply_rope(x, cos, sin):
    xf = x.astype(jnp.float32)
    x1, x2 = jnp.split(xf, 2, axis=-1)
    c = cos[:, None, :]
    s = sin[:, None, :]
    return jnp.concatenate([x1 * c - x2 * s, x2 * c + x1 * s], axis=-1).astype(x.dtype)

def sparse_index_attention(q, k, v, q_idx, k_idx, w_idx):
    B, T, H, hd = q.shape
    S = T - N_META
    scale = hd ** -0.5
    topk = min(INDEX_TOPK, S // 4)
    q_m, q_r = q[:, :N_META], q[:, N_META:]
    k_m, k_r = k[:, :N_META], k[:, N_META:]
    v_m, v_r = v[:, :N_META], v[:, N_META:]
    qi_r = q_idx[:, N_META:]
    ki_r = k_idx[:, N_META:]
    wi_r = w_idx[:, N_META:]
    causal_m = jnp.tril(jnp.ones((N_META, N_META), bool))
    s_mm = jnp.einsum('bqhd,bkhd->bhqk', q_m, k_m).astype(jnp.float32) * scale
    p_mm = jax.nn.softmax(jnp.where(causal_m, s_mm, -jnp.inf), axis=-1).astype(v.dtype)
    o_m = jnp.einsum('bhqk,bkhd->bqhd', p_mm, v_m)
    key_pos = jnp.arange(S)
    take = jax.vmap(lambda arr, idx: arr[idx])

    def query_block(j):
        start = j * Q_BLOCK
        qb = lax.dynamic_slice_in_dim(q_r, start, Q_BLOCK, axis=1)
        qib = lax.dynamic_slice_in_dim(qi_r, start, Q_BLOCK, axis=1)
        wb = lax.dynamic_slice_in_dim(wi_r, start, Q_BLOCK, axis=1)
        t_pos = start + jnp.arange(Q_BLOCK)
        rel = jax.nn.relu(jnp.einsum('bqhd,bsd->bqhs', qib, ki_r))
        iscore = jnp.einsum('bqhs,bqh->bqs', rel, wb).astype(jnp.float32)
        admissible = key_pos[None, :] <= t_pos[:, None]
        iscore = jnp.where(admissible[None], iscore, -jnp.inf)
        _, idx = lax.top_k(iscore, topk)
        valid = idx <= t_pos[None, :, None]
        kg = take(k_r, idx)
        vg = take(v_r, idx)
        s_sel = jnp.einsum('bqhd,bqkhd->bhqk', qb, kg).astype(jnp.float32) * scale
        s_sel = jnp.where(valid[:, None], s_sel, -jnp.inf)
        s_met = jnp.einsum('bqhd,bmhd->bhqm', qb, k_m).astype(jnp.float32) * scale
        p = jax.nn.softmax(jnp.concatenate([s_met, s_sel], axis=-1), axis=-1).astype(v.dtype)
        return (jnp.einsum('bhqm,bmhd->bqhd', p[..., :N_META], v_m)
                + jnp.einsum('bhqk,bqkhd->bqhd', p[..., N_META:], vg))

    o_r = lax.map(query_block, jnp.arange(S // Q_BLOCK))
    o_r = jnp.moveaxis(o_r, 0, 1).reshape(B, S, H, hd)
    return jnp.concatenate([o_m, o_r], axis=1)

def causal_depthwise_conv(x, w):
    C = x.shape[-1]
    return lax.conv_general_dilated(
        x, w[:, None, :].astype(x.dtype), window_strides=(1,),
        padding=((CONV_WIDTH - 1, 0),), dimension_numbers=('NWC', 'WIO', 'NWC'),
        feature_group_count=C)

def chunk_gated_delta_rule(q, k, v, g, beta):
    B, H, L, dk = q.shape
    dv = v.shape[-1]
    n = L // CHUNK
    q = q * dk ** -0.5
    k_beta = k * beta[..., None]
    v_beta = v * beta[..., None]

    def to_chunks(t):
        return t.reshape(B, H, n, CHUNK, t.shape[-1])

    q, k, k_beta, v_beta = to_chunks(q), to_chunks(k), to_chunks(k_beta), to_chunks(v_beta)
    g = jnp.cumsum(g.reshape(B, H, n, CHUNK), axis=-1)
    incl = jnp.tril(jnp.ones((CHUNK, CHUNK), bool))
    strict = jnp.tril(jnp.ones((CHUNK, CHUNK), bool), -1)
    decay = jnp.where(incl, jnp.exp(jnp.where(incl, g[..., :, None] - g[..., None, :], 0.0)), 0.0)
    a_mat = jnp.where(strict, jnp.einsum('bhncd,bhnsd->bhncs', k_beta, k) * decay, 0.0)
    eye = jnp.eye(CHUNK, dtype=jnp.float32)
    t_inv = lax.linalg.triangular_solve(a_mat + eye, jnp.broadcast_to(eye, a_mat.shape),
                                        left_side=True, lower=True, unit_diagonal=True)
    u = t_inv @ v_beta
    w = t_inv @ (k_beta * jnp.exp(g)[..., None])
    intra = jnp.where(incl, jnp.einsum('bhncd,bhnsd->bhncs', q, k) * decay, 0.0)

    def step(state, xs):
        q_c, k_c, u_c, w_c, g_c, intra_c = xs
        v_new = u_c - w_c @ state
        o_c = (q_c * jnp.exp(g_c)[..., None]) @ state + intra_c @ v_new
        g_last = g_c[..., -1:]
        state = state * jnp.exp(g_last)[..., None] + jnp.einsum(
            'bhcd,bhce->bhde', k_c * jnp.exp(g_last - g_c)[..., None], v_new)
        return state, o_c

    xs = tuple(jnp.moveaxis(t, 2, 0) for t in (q, k, u, w, g, intra))
    state0 = jnp.zeros((B, H, dk, dv), jnp.float32)
    _, o = lax.scan(step, state0, xs)
    return jnp.moveaxis(o, 0, 2).reshape(B, H, L, dv)

def gated_deltanet(qkv, z, beta_in, decay_in, conv_w, a_log, dt_bias, norm_w):
    B, T, _ = qkv.shape
    f32 = jnp.float32
    qkv = jax.nn.silu(causal_depthwise_conv(qkv, conv_w)).astype(f32)
    q, k, v = (t.reshape(B, T, B_HEADS, B_HEAD_DIM) for t in jnp.split(qkv, 3, axis=-1))
    q, k = l2_normalize(q), l2_normalize(k)
    beta = jax.nn.sigmoid(beta_in.astype(f32))
    g = -jnp.exp(a_log.astype(f32)) * jax.nn.softplus(decay_in.astype(f32) + dt_bias.astype(f32))
    n_pad = CHUNK - N_META

    def lead_pad(t):
        return jnp.pad(t, [(0, 0), (n_pad, 0)] + [(0, 0)] * (t.ndim - 2))

    q, k, v = (jnp.moveaxis(lead_pad(t), 1, 2) for t in (q, k, v))
    beta, g = (jnp.moveaxis(lead_pad(t), 1, 2) for t in (beta, g))
    o = chunk_gated_delta_rule(q, k, v, g, beta)
    o = jnp.moveaxis(o, 1, 2)[:, n_pad:]
    zf = z.astype(f32).reshape(B, T, B_HEADS, B_HEAD_DIM)
    o = rms_norm(o, norm_w) * jax.nn.silu(zf)
    return o.reshape(B, T, B_WIDTH).astype(z.dtype)

def moe_ffn(u, w_router, b_router, w_gate_up, b_gate_up, w_down, b_down):
    B, T, D = u.shape
    n_tok = B * T
    xt = u.reshape(n_tok, D)
    logits = (xt @ w_router + b_router).astype(jnp.float32)
    top_logit, top_e = lax.top_k(logits, TOP_K)
    gates = jax.nn.softmax(top_logit, axis=-1)
    n_assign = n_tok * TOP_K
    flat_e = top_e.reshape(-1)
    flat_tok = jnp.repeat(jnp.arange(n_tok, dtype=jnp.int32), TOP_K)
    flat_gate = gates.reshape(-1)
    order = jnp.argsort(flat_e)
    sorted_e = flat_e[order]
    counts = jnp.bincount(flat_e, length=N_EXPERTS)
    padded = (counts + MOE_BLOCK - 1) // MOE_BLOCK * MOE_BLOCK
    start = jnp.cumsum(counts) - counts
    pend = jnp.cumsum(padded)
    pstart = pend - padded
    dest = pstart[sorted_e] + jnp.arange(n_assign) - start[sorted_e]
    n_blocks = -(-(n_assign + N_EXPERTS * (MOE_BLOCK - 1)) // MOE_BLOCK)
    n_rows = n_blocks * MOE_BLOCK
    row_tok = jnp.full((n_rows,), n_tok, jnp.int32).at[dest].set(flat_tok[order])
    row_gate = jnp.zeros((n_rows,), jnp.float32).at[dest].set(flat_gate[order])
    block_e = jnp.minimum(jnp.searchsorted(pend, jnp.arange(n_blocks) * MOE_BLOCK, side='right'),
                          N_EXPERTS - 1)
    x_pad = jnp.concatenate([xt, jnp.zeros((1, D), xt.dtype)], axis=0)
    xb = x_pad[row_tok].reshape(n_blocks, MOE_BLOCK, D)

    def expert_block(args):
        xe, e = args
        gu = xe @ w_gate_up[e] + b_gate_up[e]
        gate = jnp.minimum(gu[:, 0::2], SWIGLU_LIMIT)
        up = jnp.clip(gu[:, 1::2], -SWIGLU_LIMIT, SWIGLU_LIMIT)
        glu = gate * jax.nn.sigmoid(gate * SWIGLU_ALPHA)
        return (glu * (up + 1.0)) @ w_down[e] + b_down[e]

    y = lax.map(expert_block, (xb, block_e)).reshape(n_rows, D)
    y = y * row_gate[:, None].astype(y.dtype)
    out = jnp.zeros((n_tok + 1, D), y.dtype).at[row_tok].add(y)[:n_tok]
    return out.reshape(B, T, D)

def hybrid_layer(h, norm_mix_w, w_in, q_norm_w, k_norm_w, kv_norm_w, w_kv_up, conv_w, a_log,
                 dt_bias, delta_norm_w, w_out, norm_ffn_w, w_router, b_router, w_gate_up,
                 b_gate_up, w_down, b_down):
    B, T, _ = h.shape
    u = rms_norm(h, norm_mix_w)
    points = np.cumsum(IN_SPLITS)[:-1].tolist()
    a_q, a_ckv, i_q, i_k, i_w, b_qkv, b_z, b_beta, b_a = jnp.split(u @ w_in, points, axis=-1)
    cos_a, sin_a = rope_tables(T, A_HEAD_DIM)
    cos_i, sin_i = rope_tables(T, IDX_DIM)
    q = apply_rope(rms_norm(a_q.reshape(B, T, A_HEADS, A_HEAD_DIM), q_norm_w), cos_a, sin_a)
    k, v = jnp.split(rms_norm(a_ckv, kv_norm_w) @ w_kv_up, 2, axis=-1)
    k = apply_rope(rms_norm(k.reshape(B, T, A_HEADS, A_HEAD_DIM), k_norm_w), cos_a, sin_a)
    v = v.reshape(B, T, A_HEADS, A_HEAD_DIM)
    q_idx = apply_rope(i_q.reshape(B, T, IDX_HEADS, IDX_DIM), cos_i, sin_i)
    k_idx = apply_rope(i_k[:, :, None, :], cos_i, sin_i)[:, :, 0]
    w_idx = i_w * (IDX_HEADS ** -0.5 * IDX_DIM ** -0.5)
    o_a = sparse_index_attention(q, k, v, q_idx, k_idx, w_idx).reshape(B, T, A_WIDTH)
    o_b = gated_deltanet(b_qkv, b_z, b_beta, b_a, conv_w, a_log, dt_bias, delta_norm_w)
    h = h + jnp.concatenate([o_a, o_b], axis=-1) @ w_out
    return h + moe_ffn(rms_norm(h, norm_ffn_w), w_router, b_router, w_gate_up, b_gate_up,
                       w_down, b_down)

def setup_inputs(seed: int = 0) -> dict:
    key = jax.random.key(seed)
    ks = jax.random.split(key, 20)
    f32 = jnp.float32

    def nrm(k, shape, scale):
        return jax.random.normal(k, shape, f32) * scale

    def gain(k, shape):
        return 1.0 + 0.02 * jax.random.normal(k, shape, f32)

    x = nrm(ks[0], (BATCH, SEQ, D_MODEL), 1.0)
    meta_tokens = nrm(ks[1], (N_META, D_MODEL), 1.0)
    norm_mix_w = gain(ks[2], (DEPTH, D_MODEL))
    w_in = nrm(ks[3], (DEPTH, D_MODEL, IN_COLS), D_MODEL ** -0.5)
    q_norm_w = gain(ks[4], (DEPTH, A_HEAD_DIM))
    k_norm_w = gain(ks[5], (DEPTH, A_HEAD_DIM))
    kv_norm_w = gain(ks[6], (DEPTH, KV_RANK))
    w_kv_up = nrm(ks[7], (DEPTH, KV_RANK, 2 * A_WIDTH), KV_RANK ** -0.5)
    conv_w = nrm(ks[8], (DEPTH, CONV_WIDTH, 3 * B_WIDTH), CONV_WIDTH ** -0.5)
    a_log = jnp.log(jax.random.uniform(ks[9], (DEPTH, B_HEADS), f32, 1.0, 16.0))
    dt = jnp.exp(jax.random.uniform(ks[10], (DEPTH, B_HEADS), f32, math.log(1e-3), math.log(0.1)))
    dt_bias = dt + jnp.log(-jnp.expm1(-dt))
    delta_norm_w = gain(ks[11], (DEPTH, B_HEAD_DIM))
    w_out = nrm(ks[12], (DEPTH, MIX_WIDTH, D_MODEL), MIX_WIDTH ** -0.5)
    norm_ffn_w = gain(ks[13], (DEPTH, D_MODEL))
    w_router = nrm(ks[14], (DEPTH, D_MODEL, N_EXPERTS), D_MODEL ** -0.5)
    b_router = nrm(ks[15], (DEPTH, N_EXPERTS), 0.01)
    w_gate_up = nrm(ks[16], (DEPTH, N_EXPERTS, D_MODEL, 2 * D_FF), D_MODEL ** -0.5)
    b_gate_up = nrm(ks[17], (DEPTH, N_EXPERTS, 2 * D_FF), 0.01)
    w_down = nrm(ks[18], (DEPTH, N_EXPERTS, D_FF, D_MODEL), D_FF ** -0.5)
    b_down = nrm(ks[19], (DEPTH, N_EXPERTS, D_MODEL), 0.01)
    return {"x": x, "meta_tokens": meta_tokens, "norm_mix_w": norm_mix_w, "w_in": w_in,
            "q_norm_w": q_norm_w, "k_norm_w": k_norm_w, "kv_norm_w": kv_norm_w,
            "w_kv_up": w_kv_up, "conv_w": conv_w, "a_log": a_log, "dt_bias": dt_bias,
            "delta_norm_w": delta_norm_w, "w_out": w_out, "norm_ffn_w": norm_ffn_w,
            "w_router": w_router, "b_router": b_router, "w_gate_up": w_gate_up,
            "b_gate_up": b_gate_up, "w_down": w_down, "b_down": b_down}

def reference(x, meta_tokens, norm_mix_w, w_in, q_norm_w, k_norm_w, kv_norm_w, w_kv_up, conv_w,
              a_log, dt_bias, delta_norm_w, w_out, norm_ffn_w, w_router, b_router, w_gate_up,
              b_gate_up, w_down, b_down):
    B = x.shape[0]
    meta = jnp.broadcast_to(meta_tokens.astype(x.dtype)[None], (B, N_META, x.shape[-1]))
    h = jnp.concatenate([meta, x], axis=1)
    for l in range(DEPTH):
        h = hybrid_layer(h, norm_mix_w[l], w_in[l], q_norm_w[l], k_norm_w[l], kv_norm_w[l],
                         w_kv_up[l], conv_w[l], a_log[l], dt_bias[l], delta_norm_w[l], w_out[l],
                         norm_ffn_w[l], w_router[l], b_router[l], w_gate_up[l], b_gate_up[l],
                         w_down[l], b_down[l])
    return h[:, N_META:]


_drawn_inputs = setup_inputs


def setup_inputs(seed=0):
    import zlib

    import numpy as np

    out = dict(_drawn_inputs(seed))
    spreads = {}
    factors = {'q_norm_w': 8.0,
     'k_norm_w': 3.676,
     'kv_norm_w': 3.119,
     'b_gate_up': 22.261,
     'b_down': 25.666,
     'delta_norm_w': 15.438,
     'b_router': 12.338,
     'norm_ffn_w': 3.411}
    for name, (base, spread) in spreads.items():
        noise = np.random.default_rng([zlib.crc32(name.encode()), seed]).standard_normal(out[name].shape)
        drawn = base * np.exp(spread * noise) if base else spread * noise
        out[name] = jnp.asarray(drawn.astype(out[name].dtype))
    for name, factor in factors.items():
        out[name] = (out[name] * factor).astype(out[name].dtype)
    return out
```

```python
from contextlib import ExitStack

import concourse.bass as bass
import numpy as np
from concourse import mybir

ALU = mybir.AluOpType
ACT = mybir.ActivationFunctionType
AX = mybir.AxisListType
F32 = mybir.dt.float32
I32 = mybir.dt.int32
U32 = mybir.dt.uint32

P = 128
D = 1024
KD = D // P
SEQ = 512
NT = SEQ // P
META = 16
T = META + SEQ
AH, AD = 8, 64
AW = AH * AD
RANK = 256
IH = 8
TOPK = 128
BH, BD = 4, 128
BW = BH * BD
CW = 4
PAD = CW - 1
NE = 32
TOPE = 4
FF = 1024
EPS = 1e-6
LIMIT = 7.0
ALPHA = 1.702
ITEMS = 48
INCOLS = 3408
C_Q, C_CKV, C_BQKV, C_Z, C_BETA = 0, 512, 1352, 2888, 3400
NPROJ = 336
LOW = -1.0e38
TAKEN = -3.0e38
HIDE = -1.0e30
LEVELS = 7
ROPE_H = 25

K_ID = 0
K_UI = K_ID + P
K_US = K_UI + P
K_LS = K_US + P
K_ONE = K_LS + P
K_LV = K_ONE + P
K_IOTA = K_LV + LEVELS * P
K_ADD = K_IOTA + P
K_LOW = K_ADD + P
K_LI = K_LOW + P
K_COS = K_LI + P
K_SIN = K_COS + NT * 32
K_MCOS = K_SIN + NT * 32
K_MSIN = K_MCOS + 32
KONST = K_MSIN + 32


def constants():
    k = np.zeros((P, KONST), np.float32)
    r, c = np.meshgrid(np.arange(P), np.arange(P), indexing="ij")
    k[:, K_ID:K_ID + P] = r == c
    k[:, K_UI:K_UI + P] = r <= c
    k[:, K_US:K_US + P] = r < c
    k[:, K_LS:K_LS + P] = r > c
    k[:, K_ONE:K_ONE + P] = 1
    for lv in range(LEVELS):
        at = K_LV + lv * P
        k[:, at:at + P] = (r > c) & (r >> (lv + 1) == c >> (lv + 1)) & (r >> lv != c >> lv)
    k[:, K_IOTA:K_IOTA + P] = c
    k[:, K_ADD:K_ADD + P] = np.where(c <= r, 0, HIDE)
    k[:, K_LOW:K_LOW + P] = np.where(c <= r, 0, LOW)
    k[:, K_LI:K_LI + P] = c <= r
    inv = np.float32(10000.0) ** (-np.arange(0, AD, 2, dtype=np.float32) / np.float32(AD))
    ang = np.arange(T, dtype=np.float32)[:, None] * inv[None, :]
    cos, sin = np.cos(ang).astype(np.float32), np.sin(ang).astype(np.float32)
    for t in range(NT):
        rows = slice(META + P * t, META + P * t + P)
        k[:, K_COS + 32 * t:K_COS + 32 * t + 32] = cos[rows]
        k[:, K_SIN + 32 * t:K_SIN + 32 * t + 32] = sin[rows]
    k[:META, K_MCOS:K_MCOS + 32] = cos[:META]
    k[:META, K_MSIN:K_MSIN + 32] = sin[:META]
    return k


def hybrid_layer(nc, konst, x, meta_tokens, norm_mix_w, w_in, q_norm_w, k_norm_w, kv_norm_w, w_kv_up, conv_w,
                 a_log, dt_bias, delta_norm_w, w_out, norm_ffn_w, w_router, b_router, w_gate_up, b_gate_up,
                 w_down, b_down, out):
    with ExitStack() as ctx:
        def sb(name, cols, dt=F32):
            return ctx.enter_context(nc.sbuf_tensor(name, [P, cols], dt))

        def sem(name):
            return ctx.enter_context(nc.semaphore(name))

        ps = [ctx.enter_context(nc.psum_tensor(f"bank{i}", [P, 512], F32)) for i in range(8)]

        ring = sb("ring", 6 * 4096)
        h = sb("h", NT * D)
        kc = sb("kc", KONST)
        ffnw = sb("ffnw", D)
        gains = sb("gains", 64 + 64 + BD + NE + 2 * BH)
        colw = sb("colw", 58)
        r1 = sb("r1", KD * T)
        r2 = sb("r2", 12 * (T + PAD))
        r3 = sb("r3", 8768)
        small = sb("small", 900)

        def slot(s, n=4096, at=0):
            return ring[:, 4096 * s + at:4096 * s + at + n]

        def konst_at(at, rows=P, n=P):
            return kc[0:rows, at:at + n]

        def ident(n=P):
            return kc[0:n, K_ID:K_ID + n]

        h_t = [h[:, D * t:D * t + D] for t in range(NT)]
        qn_w, kn_w = gains[:, 0:64], gains[:, 64:128]
        dn_w = gains[:, 128:256]
        br_w = gains[:, 256:288]
        alog, dtb = gains[:, 288:292], gains[:, 292:296]
        uT = r1[:, :].rearrange("p (k t) -> p k t", k=KD)
        oab = r1[:, 0:NT * D].rearrange("p (t d) -> p t d", t=NT)
        qkvT = r2[:, :].rearrange("p (m t) -> p m t", m=12)
        qT = r3[:, 0:2048].rearrange("p (a t) -> p a t", a=4)
        kT = r3[:, 2048:4160].rearrange("p (a t) -> p a t", a=4)
        vA = r3[:, 4160:6208].rearrange("p (t d) -> p t d", t=NT)
        vM = r3[0:META, 6208:6720]
        qiT = r3[:, 6720:8256].rearrange("p (a t) -> p a t", a=4)
        kiT = r3[:, 8256:8768]
        utmp = [r3[:, 0:1024], r3[:, 1024:2048]]
        metax = r3[0:META, 2048:3072]
        conv_a = [r3[:, 3072:3600], r3[:, 3600:4128]]
        wrow = r3[0:58, 4128:4256]
        sq = r3[:, 5056:6080]
        convsq = [r3[:, 6080:6608], r3[:, 6608:7136]]
        zs = slot(2, 2048).rearrange("p (t d) -> p t d", t=NT)
        rp = slot(2, 1664, 2048).rearrange("p (a d) -> p a d", a=26)
        pre = slot(1, 1600, 2048).rearrange("p (a d) -> p a d", a=ROPE_H)
        sqC = slot(5, 768, KD * NPROJ)
        ckv = slot(5, 256, KD * NPROJ + 768)
        square_out = r2[:, 4096:5120]
        sm_at = [0]

        def sm(n):
            sm_at[0] += n
            return small[:, sm_at[0] - n:sm_at[0]]

        ssqA, rsA = sm(5), sm(5)
        ba = sm(5 * 8).rearrange("p (t c) -> p t c", t=5)
        beta = sm(20).rearrange("p (t c) -> p t c", t=5)
        gg = sm(20).rearrange("p (t c) -> p t c", t=5)
        rqk = sm(40).rearrange("p (t c) -> p t c", t=5)
        wi = sm(NT * 8).rearrange("p (t c) -> p t c", t=NT)
        st1, st2, st3, st4 = sm(20), sm(20), sm(20), sm(20)
        ea = sm(4)
        ckvT = [sm(P), sm(P)]
        gcc, eg, el, ngk, br = sm(4), sm(4), sm(4), sm(4), sm(4)
        mx8 = sm(8)
        qmax, qsum, qinv = sm(8), sm(8), sm(8)
        ossq, orstd = sm(16), sm(16)

        konst_in, x_in, gains_in = sem("konst_in"), [sem(f"x_in{i}") for i in range(5)], sem("gains_in")
        slot_in = [sem(f"slot_in{s}") for s in range(6)]
        wkv_in, wr_in, bias_in = sem("wkv_in"), sem("wr_in"), sem("bias_in")
        colw_T, u_T, u_evac = sem("colw_T"), sem("u_T"), sem("u_evac")
        conv_ps, conv_evac, conv_silu, conv_sq, qk_ssq = (sem("conv_ps"), sem("conv_evac"), sem("conv_silu"),
                                                          sem("conv_sq"), sem("qk_ssq"))
        group_used = sem("group_used")
        proj_ps, ckv_T, kv_ps, rope_T = sem("proj_ps"), sem("ckv_T"), sem("kv_ps"), sem("rope_T")
        act_step = sem("act_step")
        dve_step = sem("dve_step")
        pool_step = sem("pool_step")
        d_u, d_colw, d_conv, d_ckv, d_ckvT, d_rope, d_ropeT = (sem("d_u"), sem("d_colw"), sem("d_conv"), sem("d_ckv"),
                                                               sem("d_ckvT"), sem("d_rope"), sem("d_ropeT"))
        d_ssqc = sem("d_ssqc")
        d_stat, a_stat, a_proj, a_z, a_ssq = sem("d_stat"), sem("a_stat"), sem("a_proj"), sem("a_z"), sem("a_ssq")
        f_in, f_ps, f_dd, f_exp, f_A, f_E, f_lv, f_lvps = (sem("f_in"), sem("f_ps"), sem("f_dd"), sem("f_exp"),
                                                           sem("f_A"), sem("f_E"), sem("f_lv"), sem("f_lvps"))
        f_ks, f_r, f_vn, f_vnc, f_o, f_oc, f_s, f_sc = (sem("f_ks"), sem("f_r"), sem("f_vn"), sem("f_vnc"), sem("f_o"),
                                                        sem("f_oc"), sem("f_s"), sem("f_sc"))
        i_ps, i_rel, i_add = sem("i_ps"), sem("i_rel"), sem("i_add")
        a_sc, a_msk, a_exp, a_pT, a_pTc, a_o, a_on = (sem("a_sc"), sem("a_msk"), sem("a_exp"), sem("a_pT"), sem("a_pTc"),
                                                      sem("a_o"), sem("a_on"))
        g_T, g_Tc, g_ps, g_h, g_xn, g_xT, g_xTc, g_lg, g_sel, g_rk, g_gt, g_gtc, g_bd, g_acc = (
            sem("g_T"), sem("g_Tc"), sem("g_ps"), sem("g_h"), sem("g_xn"), sem("g_xT"), sem("g_xTc"), sem("g_lg"),
            sem("g_sel"), sem("g_rk"), sem("g_gt"), sem("g_gtc"), sem("g_bd"), sem("g_acc"))
        table_ready = sem("table_ready")
        p_built, x_ps, xe_ready, gu_ready, gm_ready, sg_ready, act_ready = (
            sem("p_built"), sem("x_ps"), sem("xe_ready"), sem("gu_ready"), sem("gm_ready"), sem("sg_ready"), sem("act_ready"))
        pt_ps, pt_ready, actT_ps, actT_ready, y_ps, y_ready, scat_ps, acc_added, chunk_used, loop_step = (
            sem("pt_ps"), sem("pt_ready"), sem("actT_ps"), sem("actT_ready"), sem("y_ps"), sem("y_ready"),
            sem("scat_ps"), sem("acc_added"), sem("chunk_used"), sem("loop_step"))
        out_done = sem("out_done")

        fs = [slot(s, 512, 512 * i) for s in (0, 1, 3) for i in range(8)]

        def heads(ap):
            return ap.rearrange("p (h c) -> p h c", h=4)

        F_GB, F_RK, F_KD, F_VB, F_DN, F_DT, F_A, F_IT, F_D, F_Dt, F_Y, F_S, F_R, F_VN, F_O = [heads(a) for a in fs[0:15]]
        F_E = [heads(a) for a in fs[15:22]]
        isc = slot(0, 1536).rearrange("p (t c) -> p t c", t=3)
        rel = [slot(0, 512, 1536), slot(0, 512, 2048)]
        madd = slot(1, 1536).rearrange("p (t c) -> p t c", t=3)
        prob = [slot(3, T), slot(3, T, T)]
        pT = [slot(3, 640, 2 * T), slot(3, 640, 2 * T + 640)]
        oT = r3[:, 0:1024].rearrange("p (k c) -> p k c", k=KD)
        xT = r3[:, 1024:2048].rearrange("p (k c) -> p k c", k=KD)
        wr = r3[:, 2048:2304].rearrange("p (k e) -> p k e", k=KD)
        bgu = r3[:, 2304:4352]
        bdn = r3[0:NE, 4352:5376]
        lg = r3[:, 5376:5504].rearrange("p (t e) -> p t e", t=NT)
        selm = r3[:, 5504:5632].rearrange("p (t e) -> p t e", t=NT)
        gate = r3[:, 5632:5760]
        rankm = r3[:, 5760:5888]
        gtok = r3[:, 5888:5920]
        gT = r3[0:NE, 5920:6048]
        etab = r3[:, 6048:6048 + ITEMS]
        shift = r3[:, 6112:6112 + ITEMS]
        cnt, blocks, cum, tmpe = r3[:, 6176:6208], r3[:, 6208:6240], r3[:, 6240:6272], r3[:, 6272:6304]
        gcol = r3[:, 6304:6308]
        sel = r3[:, 6400:6528]
        onehot = r3[:, 6528:7040].rearrange("p (t c) -> p t c", t=NT)
        onehotT = r3[:, 7040:7552].rearrange("p (t c) -> p t c", t=NT)
        ybuf = r3[:, 7552:8576]
        xn = r2[:, 0:NT * D].rearrange("p (t d) -> p t d", t=NT)
        actT = r2[:, 4096:5120].rearrange("p (k c) -> p k c", k=KD)
        xe = r1[:, 0:1024].rearrange("p (k c) -> p k c", k=KD)
        gm, sg, act = r1[:, 1024:2048], r1[:, 2048:3072], r1[:, 3072:4096]
        eidx = ctx.enter_context(nc.sbuf_tensor("eidx", [P, 8 + 1], U32))
        etab_i = ctx.enter_context(nc.sbuf_tensor("etab_i", [P, ITEMS], I32))
        nitems_i = ctx.enter_context(nc.sbuf_tensor("nitems_i", [P, 1], I32))

        w_in0 = w_in[0].rearrange("(k p) n -> p k n", p=P)
        tok_cols = [(0, META)] + [(META + P * t, P) for t in range(NT)]

        def w_group(s, n=512):
            return slot(s, KD * n).rearrange("p (k n) -> p k n", k=KD)

        gC = w_group(5, NPROJ)
        wkv = slot(1, 2048).rearrange("p (k n) -> p k n", k=2)

        def expert_chunk(e, s):
            if s < 4:
                return w_gate_up[0, bass.ds(e, 1)].rearrange("o (k p) n -> p (o k) n", p=P)[:, :, 512 * s:512 * s + 512]
            return w_down[0, bass.ds(e, 1)].rearrange("o (k p) n -> p (o k) n", p=P)[:, :, 512 * (s - 4):512 * (s - 4) + 512]

        block = ctx.enter_context(nc.Block())

        @block.sync
        def _(sp):
            sp.dma_start(metax, meta_tokens).then_inc(x_in[0], 16)
            for t in range(NT):
                sp.dma_start(h_t[t], x[0, P * t:P * t + P, :]).then_inc(x_in[t + 1], 16)
            for s in range(3):
                sp.dma_start(w_group(s), w_in0[:, :, C_BQKV + 512 * s:C_BQKV + 512 * s + 512]).then_inc(slot_in[s], 16)
            sp.dma_start(w_group(3), w_in0[:, :, 0:512]).then_inc(slot_in[3], 16)
            sp.dma_start(w_group(4), w_in0[:, :, 512:1024]).then_inc(slot_in[4], 16)
            sp.dma_start(gC[:, :, 0:328], w_in0[:, :, 1024:1352]).then_inc(slot_in[5], 16)
            sp.dma_start(gC[:, :, 328:336], w_in0[:, :, C_BETA:C_BETA + 8]).then_inc(slot_in[5], 16)
            sp.wait_ge(group_used, 1)
            sp.dma_start(w_group(0), w_in0[:, :, C_Z:C_Z + 512]).then_inc(slot_in[0], 16)
            sp.wait_ge(group_used, 2)
            sp.dma_start(wkv, w_kv_up[0].rearrange("(k p) n -> p k n", p=P)).then_inc(wkv_in, 16)
            sp.wait_ge(group_used, 4)
            for n in range(2):
                sp.dma_start(w_group(4 + n), w_out[0].rearrange("(k p) n -> p k n", p=P)[:, :, 512 * n:512 * n + 512])\
                  .then_inc(slot_in[4 + n], 16)
            sp.wait_ge(a_on, NT)
            sp.dma_start(wr, w_router[0].rearrange("(k p) e -> p k e", p=P)).then_inc(wr_in, 16)
            sp.dma_start(bdn, b_down[0]).then_inc(bias_in, 16)
            sp.wait_ge(table_ready, 1)
            sp.dma_start(bgu[0:NE, :], b_gate_up[0]).then_inc(bias_in, 16)
            for s in range(4):
                sp.dma_start(w_group(s), expert_chunk(0, s)).then_inc(slot_in[s], 16)
            sp.wait_ge(g_ps, 2 * NT)
            for s in (4, 5):
                sp.dma_start(w_group(s), expert_chunk(0, s)).then_inc(slot_in[s], 16)
            with sp.Fori(1, NE) as e:
                for s in range(6):
                    sp.wait_ge(chunk_used, 6 * (e - 1) + s + 1)
                    sp.dma_start(w_group(s), expert_chunk(e, s)).then_inc(slot_in[s], 16)
            sp.wait_ge(table_ready, 2)
            items = sp.value_load(nitems_i[0:1, 0:1], min_val=NE, max_val=ITEMS - 1)
            with sp.If(items > NE):
                with sp.Fori(NE, items) as i:
                    e = sp.value_load(etab_i[0:1, bass.ds(i, 1)], min_val=0, max_val=NE - 1)
                    for s in range(6):
                        sp.wait_ge(chunk_used, 6 * (i - 1) + s + 1)
                        sp.dma_start(w_group(s), expert_chunk(e, s)).then_inc(slot_in[s], 16)
            sp.wait_ge(acc_added, 8 * items + 8)
            for t in range(NT):
                sp.dma_start(out[0, P * t:P * t + P, :], h_t[t]).then_inc(out_done, 16)
            sp.wait_ge(out_done, 16 * NT)

        @block.gpsimd
        def _(pool):
            pool.dma_start(kc[:, :], konst).then_inc(konst_in, 16)
            rows = [(norm_mix_w[0].rearrange("(k p) -> k p", p=P), 48, 56), (kv_norm_w[0].rearrange("(k p) -> k p", p=P), 56, 58)]
            for w in range(CW):
                pool.dma_start(wrow[12 * w:12 * w + 12, :], conv_w[0, w].rearrange("(m p) -> m p", p=P)).then_inc(gains_in, 16)
            for src, a, b in rows:
                pool.dma_start(wrow[a:b, :], src).then_inc(gains_in, 16)
            for dst, src in ((qn_w, q_norm_w), (kn_w, k_norm_w), (dn_w, delta_norm_w), (br_w, b_router), (alog, a_log),
                             (dtb, dt_bias), (ffnw[:, :], norm_ffn_w)):
                pool.dma_start(dst, src.partition_broadcast(P)).then_inc(gains_in, 16)
            for c in range(5):
                n = META if c == 0 else P
                pool.wait_ge(f_A, c + 1)
                for lv in range(1, 4 if c == 0 else LEVELS):
                    m = konst_at(K_LV + lv * P, n, n).unsqueeze(1).to_broadcast([n, 4, n])
                    nc.gpsimd.tensor_tensor(F_E[lv][0:n, :, 0:n], F_A[0:n, :, 0:n], m, ALU.mult).then_inc(f_E, 1)

        @block.scalar
        def _(act_e):
            n_act = [0]

            def own(ins):
                n_act[0] += 1
                ins.then_inc(act_step, 1)
                act_e.wait_ge(act_step, n_act[0])

            A = nc.scalar.activation
            act_e.wait_ge(d_colw, 1)
            for t in range(5):
                n = tok_cols[t][1]
                src = metax if t == 0 else h_t[t - 1]
                act_e.wait_ge(x_in[t], 16)
                A(sq[0:n, :], src, ACT.Square, accum_out=ssqA[0:n, t:t + 1]).then_inc(a_ssq, 1)
                act_e.wait_ge(a_ssq, t + 1)
            act_e.wait_ge(d_stat, 1)
            A(st1[:, 0:5], rsA, ACT.Sqrt).then_inc(a_stat, 1)
            for m in range(12):
                for half in range(2):
                    act_e.wait_ge(conv_ps, 2 * m + half + 1)
                    A(qkvT[:, m, PAD + 264 * half:PAD + 264 * half + 264], ps[4 + 2 * (m % 2) + half][:, 0:264], ACT.Copy)\
                        .then_inc(conv_evac, 1)
            for m in range(12):
                act_e.wait_ge(d_conv, m + 1)
                A(qkvT[:, m, PAD:], qkvT[:, m, PAD:], ACT.Silu).then_inc(conv_silu, 1)
                if m < 8:
                    act_e.wait_ge(conv_silu, m + 1)
                    if m >= 2:
                        act_e.wait_ge(qk_ssq, m - 1)
                    A(convsq[m % 2], qkvT[:, m, PAD:], ACT.Square).then_inc(conv_sq, 1)
            for t in range(5):
                n = tok_cols[t][1]
                act_e.wait_ge(proj_ps, 4 * t + 4)
                if t:
                    act_e.wait_ge(d_rope, t)
                    own(A(sqC[:, 0:512], ps[0][:, :], ACT.Square))
                own(A(sqC[0:n, 512:768], ps[1][0:n, 0:256], ACT.Square))
                if t:
                    own(A(pre[:, 16:20, :], ps[1][:, 256:512].rearrange("p (a d) -> p a d", a=4), ACT.Copy))
                    own(A(pre[:, 20:24, :], ps[2][:, 0:256].rearrange("p (a d) -> p a d", a=4), ACT.Copy))
                    own(A(pre[:, 24, :], ps[2][:, 256:320], ACT.Copy))
                    own(A(wi[:, t - 1, :], ps[2][:, 320:328], ACT.Copy, scale=float(IH ** -0.5 * 64 ** -0.5)))
                    own(A(zs[:, t - 1, :], ps[3][:, :], ACT.Copy))
                A(ba[0:n, t, :], ps[2][0:n, 328:336], ACT.Copy).then_inc(a_proj, 1)
                act_e.wait_ge(d_stat, 2 + 2 * t)
                A(st2[0:n, 0:9], st1[0:n, 0:9], ACT.Sqrt).then_inc(a_stat, 1)
                act_e.wait_ge(kv_ps, 2 * t + 2)
                own(A(sqC[0:n, 0:512], ps[5][0:n, :], ACT.Square))
                A(vM if t == 0 else vA[:, t - 1, :], ps[6][0:n, :], ACT.Copy).then_inc(a_proj, 1)
                act_e.wait_ge(d_stat, 3 + 2 * t)
                A(st2[0:n, 0:8], st1[0:n, 0:8], ACT.Sqrt).then_inc(a_stat, 1)
            act_e.wait_ge(d_stat, 12)
            A(rqk[:, :, :], rqk[:, :, :], ACT.Sqrt).then_inc(a_stat, 1)
            act_e.wait_ge(d_stat, 13)
            own(A(zs[:, :, :], zs[:, :, :], ACT.Silu))
            own(A(beta[:, :, :], ba[:, :, 0:4], ACT.Sigmoid))
            own(A(ea, alog, ACT.Exp))
            own(A(st1, st1, ACT.Exp, scale=-1.0))
            A(st3, st1, ACT.Ln, bias=1.0).then_inc(a_stat, 1)
            for c in range(5):
                n = META if c == 0 else P
                act_e.wait_ge(f_dd, c + 1)
                own(A(F_DN[0:n, :, 0:n], F_DN[0:n, :, 0:n], ACT.Exp, scale=-1.0))
                own(A(F_DT[0:n, :, 0:n], F_DT[0:n, :, 0:n], ACT.Exp))
                own(A(eg[0:n, :], gcc[0:n, :], ACT.Exp))
                A(el, el, ACT.Exp).then_inc(f_exp, 1)
                act_e.wait_ge(f_vn, c + 1)
                A(F_VN[0:n, :, :], heads(ps[1][0:n, :]), ACT.Copy).then_inc(f_vnc, 1)
                if c:
                    act_e.wait_ge(f_o, c)
                    A(F_O[:, :, :], heads(ps[3][:, :]), ACT.Copy).then_inc(f_oc, 1)
            act_e.wait_ge(d_stat, 14)
            A(orstd, ossq, ACT.Sqrt).then_inc(a_stat, 1)
            q = 0
            for j in range(1, NT):
                w = P * (j + 1)
                for hh in range(IH):
                    act_e.wait_ge(i_ps, q + 1)
                    if q >= 2:
                        act_e.wait_ge(i_add, q - 1)
                    A(rel[q % 2][:, 0:w], ps[q % 2][:, 0:w], ACT.Relu).then_inc(i_rel, 1)
                    q += 1
            for j in range(NT):
                w = META + P * (j + 1)
                for hh in range(AH):
                    q = AH * j + hh
                    act_e.wait_ge(a_msk, q + 1)
                    A(prob[q % 2][:, 0:w], prob[q % 2][:, 0:w], ACT.Exp, bias=qmax[:, hh:hh + 1],
                      accum_out=qsum[:, hh:hh + 1]).then_inc(a_exp, 1)
                    act_e.wait_ge(a_pT, q + 1)
                    own(A(pT[q % 2][:, 0:P * (j + 1)], ps[2 + q % 2][:, 0:P * (j + 1)], ACT.Copy))
                    A(pT[q % 2][0:META, 512:640], ps[5 + q % 2][0:META, P:2 * P], ACT.Copy).then_inc(a_pTc, 1)
            for t in range(NT):
                for half in range(2):
                    act_e.wait_ge(g_T, 2 * t + half + 1)
                    A(oT[:, 4 * half:4 * half + 4, :], ps[half][:, :].rearrange("p (k c) -> p k c", k=4), ACT.Copy)\
                        .then_inc(g_Tc, 1)
                act_e.wait_ge(g_h, t + 1)
                A(square_out, h_t[t], ACT.Square, accum_out=st1[:, t:t + 1]).then_inc(a_ssq, 1)
                act_e.wait_ge(d_stat, 15 + t)
                A(st3[:, t:t + 1], st2[:, t:t + 1], ACT.Sqrt).then_inc(a_stat, 1)
                for half in range(2):
                    act_e.wait_ge(g_xT, 2 * t + half + 1)
                    A(xT[:, 4 * half:4 * half + 4, :], ps[4 + half][:, :].rearrange("p (k c) -> p k c", k=4), ACT.Copy)\
                        .then_inc(g_xTc, 1)
            for t in range(NT):
                act_e.wait_ge(g_sel, t + 1)
                A(lg[:, t, :], lg[:, t, :], ACT.Exp).then_inc(a_stat, 1)
            act_e.wait_ge(g_rk, NT + 2)
            own(A(ybuf, kc[:, 0:1024], ACT.Copy, scale=0.0))
            A(onehotT[:, :, :], kc[:, 0:512].rearrange("p (t c) -> p t c", t=4), ACT.Copy, scale=0.0).then_inc(pt_ready, 1)

            def copy_xe(i):
                for half in range(2):
                    act_e.wait_ge(x_ps, 2 * i + half + 1)
                    A(xe[:, 4 * half:4 * half + 4, :], ps[6 + half][:, :].rearrange("p (k c) -> p k c", k=4), ACT.Copy)\
                        .then_inc(xe_ready, 1)

            copy_xe(0)
            act_e.wait_ge(table_ready, 2)
            items = act_e.value_load(nitems_i[0:1, 0:1], min_val=NE, max_val=ITEMS - 1)
            with act_e.Fori(0, items) as i:
                for n in range(4):
                    act_e.wait_ge(gm_ready, 4 * i + n + 1)
                    A(sg[:, 256 * n:256 * n + 256], gm[:, 256 * n:256 * n + 256], ACT.Sigmoid, scale=ALPHA).then_inc(sg_ready, 1)
                act_e.wait_ge(pt_ps, i + 1)
                A(onehotT[:, :, :], ps[2][:, :].rearrange("p (t c) -> p t c", t=4), ACT.Copy).then_inc(pt_ready, 1)
                for half in range(2):
                    act_e.wait_ge(actT_ps, 2 * i + half + 1)
                    A(actT[:, 4 * half:4 * half + 4, :], ps[half][:, :].rearrange("p (k c) -> p k c", k=4), ACT.Copy)\
                        .then_inc(actT_ready, 1)
                for half in range(2):
                    act_e.wait_ge(y_ps, 2 * i + half + 1)
                    A(ybuf[:, 512 * half:512 * half + 512], ps[4 + half][:, :], ACT.Copy).then_inc(y_ready, 1)
                copy_xe(i + 1)

        @block.vector
        def _(dve):
            V = nc.vector
            counts = {}

            def own(ins, signal=dve_step):
                counts[signal.num] = counts.get(signal.num, 0) + 1
                ins.then_inc(signal, 1)
                dve.wait_ge(signal, counts[signal.num])

            def bc(ap, shape):
                return ap.to_broadcast(shape)

            own(V.memset(small[:, :], 1.0), d_colw)
            own(V.memset(qkvT[:, :, 0:PAD], 0.0))
            dve.wait_ge(a_ssq, 5)
            own(V.tensor_scalar(rsA, ssqA, 1.0 / D, EPS, ALU.mult, ALU.add), d_stat)
            dve.wait_ge(konst_in, 16)
            dve.wait_ge(colw_T, 1)
            own(V.tensor_copy(colw[:, :], ps[7][:, 0:58]))
            dve.wait_ge(a_stat, 1)
            own(V.reciprocal(rsA, st1[:, 0:5]))
            for t in range(5):
                at, n = tok_cols[t]
                src = metax if t == 0 else h_t[t - 1]
                if t >= 2:
                    dve.wait_ge(u_T, 2 * (t - 1))
                own(V.tensor_scalar(utmp[t % 2][0:n, :], src, rsA[0:n, t:t + 1], None, ALU.mult), d_u)
                for half in range(2):
                    dve.wait_ge(u_T, 2 * t + half + 1)
                    own(V.tensor_tensor(uT[:, 4 * half:4 * half + 4, at:at + n],
                                    ps[2 * (t % 2) + half][:, :].rearrange("p (k c) -> p k c", k=4)[:, :, 0:n],
                                    bc(colw[:, 48 + 4 * half:52 + 4 * half].unsqueeze(2), [P, 4, n]), ALU.mult), u_evac)
            for m in range(12):
                dve.wait_ge(conv_evac, 2 * m + 2)
                own(V.tensor_scalar(conv_a[0], qkvT[:, m, 0:T], colw[:, m:m + 1], None, ALU.mult))
                for w in range(1, CW - 1):
                    own(V.scalar_tensor_tensor(out=conv_a[w % 2], in0=qkvT[:, m, w:w + T], scalar=colw[:, 12 * w + m:12 * w + m + 1],
                                               in1=conv_a[(w + 1) % 2], op0=ALU.mult, op1=ALU.add))
                w = CW - 1
                own(V.scalar_tensor_tensor(out=qkvT[:, m, PAD:], in0=qkvT[:, m, PAD:], scalar=colw[:, 12 * w + m:12 * w + m + 1],
                                       in1=conv_a[(w + 1) % 2], op0=ALU.mult, op1=ALU.add), d_conv)
            dve.wait_ge(qk_ssq, 8)
            own(V.tensor_copy(rqk[0:META, 0, :], ps[7][0:META, 0:8]))
            for t in range(1, 5):
                own(V.tensor_copy(rqk[:, t, :], ps[7][:, 8 * t:8 * t + 8]))
            own(V.tensor_scalar(gcc, gcc, 1.0, None, ALU.mult), d_ssqc)
            for t in range(5):
                at, n = tok_cols[t]
                dve.wait_ge(a_proj, 2 * t + 1)
                if t:
                    own(V.tensor_reduce(st1[:, 0:8], sqC[:, 0:512].rearrange("p (a d) -> p a d", a=8), AX.X, ALU.add))
                    own(V.tensor_scalar(st1[:, 0:8], st1[:, 0:8], 1.0 / AD, EPS, ALU.mult, ALU.add))
                own(V.tensor_reduce(st1[0:n, 8:9], sqC[0:n, 512:768], AX.X, ALU.add))
                own(V.tensor_scalar(st1[0:n, 8:9], st1[0:n, 8:9], 1.0 / RANK, EPS, ALU.mult, ALU.add), d_stat)
                dve.wait_ge(a_stat, 2 + 2 * t)
                own(V.reciprocal(st3[0:n, 0:9], st2[0:n, 0:9]))
                own(V.tensor_scalar(ckv[0:n, :], ps[1][0:n, 0:256], st3[0:n, 8:9], None, ALU.mult), d_ckv)
                if t:
                    own(V.tensor_tensor(pre[:, 0:8, :], ps[0][:, :].rearrange("p (a d) -> p a d", a=8),
                                        bc(st3[:, 0:8].unsqueeze(2), [P, 8, AD]), ALU.mult))
                    own(V.tensor_tensor(pre[:, 0:8, :], pre[:, 0:8, :], bc(qn_w.unsqueeze(1), [P, 8, AD]), ALU.mult))
                dve.wait_ge(ckv_T, t + 1)
                own(V.tensor_scalar(ckvT[0][:, 0:n], ps[4][:, 0:n], colw[:, 56:57], None, ALU.mult))
                own(V.tensor_scalar(ckvT[1][:, 0:n], ps[4][:, P:P + n], colw[:, 57:58], None, ALU.mult), d_ckvT)
                dve.wait_ge(a_proj, 2 * t + 2)
                own(V.tensor_reduce(st1[0:n, 0:8], sqC[0:n, 0:512].rearrange("p (a d) -> p a d", a=8), AX.X, ALU.add))
                own(V.tensor_scalar(st1[0:n, 0:8], st1[0:n, 0:8], 1.0 / AD, EPS, ALU.mult, ALU.add), d_stat)
                dve.wait_ge(a_stat, 3 + 2 * t)
                own(V.reciprocal(st3[0:n, 0:8], st2[0:n, 0:8]))
                own(V.tensor_tensor(pre[0:n, 8:16, :], ps[5][0:n, :].rearrange("p (a d) -> p a d", a=8),
                                    bc(st3[0:n, 0:8].unsqueeze(2), [n, 8, AD]), ALU.mult))
                own(V.tensor_tensor(pre[0:n, 8:16, :], pre[0:n, 8:16, :], bc(kn_w[0:n].unsqueeze(1), [n, 8, AD]), ALU.mult))
                a, b = (8, 16) if t == 0 else (0, ROPE_H)
                cs = K_MCOS if t == 0 else K_COS + 32 * (t - 1)
                sn = K_MSIN if t == 0 else K_SIN + 32 * (t - 1)
                cosb = bc(kc[0:n, cs:cs + 32].unsqueeze(1), [n, b - a, 32])
                sinb = bc(kc[0:n, sn:sn + 32].unsqueeze(1), [n, b - a, 32])
                x1, x2 = pre[0:n, a:b, 0:32], pre[0:n, a:b, 32:64]
                y1, y2 = rp[0:n, a:b, 0:32], rp[0:n, a:b, 32:64]
                if t:
                    dve.wait_ge(rope_T, 4 * t)
                own(V.tensor_tensor(y1, x1, cosb, ALU.mult))
                own(V.tensor_tensor(y2, x2, cosb, ALU.mult))
                own(V.tensor_tensor(x2, x2, sinb, ALU.mult))
                own(V.tensor_tensor(x1, x1, sinb, ALU.mult))
                own(V.tensor_tensor(y1, y1, x2, ALU.subtract))
                own(V.tensor_tensor(y2, y2, x1, ALU.add))
                if t:
                    own(V.tensor_copy(rp[:, 25, :], rp[:, 24, :]))
                own(V.memset(mx8, 0.0), d_rope)
                dve.wait_ge(rope_T, 4 * t + 4)
                if t:
                    own(V.tensor_copy(qT[:, :, P * (t - 1):P * t], heads(ps[7][:, :])))
                    own(V.tensor_copy(kT[:, :, at:at + P], heads(ps[4][:, :])))
                    if t >= 2:
                        own(V.tensor_copy(qiT[:, :, P * (t - 2):P * (t - 1)], heads(ps[5][:, :])))
                    own(V.tensor_copy(kiT[:, P * (t - 1):P * t], ps[6][:, 0:P]))
                else:
                    own(V.tensor_copy(kT[:, :, 0:META], heads(ps[4][:, :])[:, :, 0:META]))
                own(V.memset(mx8, 0.0), d_ropeT)
            own(V.tensor_scalar(rqk[:, :, :], rqk[:, :, :], EPS, None, ALU.add), d_stat)
            y = st4.rearrange("p (t c) -> p t c", t=5)
            own(V.tensor_tensor(y, ba[:, :, 4:8], bc(dtb.unsqueeze(1), [P, 5, 4]), ALU.add))
            own(V.tensor_scalar(st2, st4, -1.0, None, ALU.mult))
            own(V.tensor_tensor(st1, st4, st2, ALU.max), d_stat)
            dve.wait_ge(a_stat, 12)
            own(V.reciprocal(rqk[:, :, :], rqk[:, :, :]))
            dve.wait_ge(a_stat, 13)
            own(V.scalar_tensor_tensor(out=st4, in0=st4, scalar=0.0, in1=st3, op0=ALU.max, op1=ALU.add))
            own(V.tensor_scalar(ea, ea, -1.0, None, ALU.mult))
            own(V.tensor_tensor(gg[:, :, :], y, bc(ea.unsqueeze(1), [P, 5, 4]), ALU.mult))
            lvs = 0
            for c in range(5):
                n = META if c == 0 else P
                rk = rqk[0:n, c, 4:8]
                own(V.tensor_copy(F_GB[0:n, :, :], bc(gg[0:n, c, :].unsqueeze(2), [n, 4, P])))
                own(V.tensor_copy(F_RK[0:n, :, 0:n], bc(rk.unsqueeze(2), [n, 4, n])), f_in)
                dve.wait_ge(f_ps, c + 1)
                R, KK, QK, Kt, Vt, RK, GC = (heads(ps[b][:, :]) for b in (0, 1, 2, 3, 4, 5, 6))
                own(V.tensor_copy(gcc[0:n, :], ps[6][0:n, 0:4]))
                for hh in range(BH):
                    own(V.tensor_scalar(F_DT[0:n, hh, 0:n], R[0:n, hh, 0:n], gcc[0:n, hh:hh + 1], 0.0, ALU.subtract, ALU.min))
                    own(V.tensor_scalar(F_DN[0:n, hh, 0:n], R[0:n, hh, 0:n], gcc[0:n, hh:hh + 1], 0.0, ALU.subtract, ALU.max))
                own(V.tensor_copy(el.unsqueeze(2), R[:, :, n - 1:n]), f_dd)
                own(V.tensor_tensor(br[0:n, :], beta[0:n, c, :], rk, ALU.mult))
                dve.wait_ge(f_exp, c + 1)
                own(V.scalar_tensor_tensor(out=ngk[0:n, :], in0=eg[0:n, :], scalar=-1.0, in1=br[0:n, :], op0=ALU.mult, op1=ALU.mult))
                own(V.tensor_tensor(F_DN[0:n, :, 0:n], KK[0:n, :, 0:n], F_DN[0:n, :, 0:n], ALU.mult))
                own(V.tensor_tensor(F_DN[0:n, :, 0:n], RK[0:n, :, 0:n], F_DN[0:n, :, 0:n], ALU.mult))
                for hh in range(BH):
                    own(V.scalar_tensor_tensor(out=F_A[0:n, hh, 0:n], in0=F_DN[0:n, hh, 0:n], scalar=br[0:n, hh:hh + 1],
                                               in1=konst_at(K_LS, n, n), op0=ALU.mult, op1=ALU.mult))
                own(V.tensor_tensor(F_Y[0:n, :, 0:n], F_A[0:n, :, 0:n], bc(konst_at(K_LV, n, n).unsqueeze(1), [n, 4, n]), ALU.mult))
                own(V.tensor_tensor(F_D[0:n, :, 0:n], bc(ident(n).unsqueeze(1), [n, 4, n]), F_Y[0:n, :, 0:n], ALU.subtract), f_A)
                own(V.tensor_tensor(st2[0:n, 0:4].unsqueeze(2), F_DT[0:n, :, n - 1:n], rk.unsqueeze(2), ALU.mult))
                own(V.tensor_tensor(F_KD[0:n, :, :], Kt[0:n, :, :], bc(st2[0:n, 0:4].unsqueeze(2), [n, 4, P]), ALU.mult))
                own(V.tensor_tensor(F_VB[0:n, :, :], Vt[0:n, :, :], bc(beta[0:n, c, :].unsqueeze(2), [n, 4, P]), ALU.mult))
                if c:
                    own(V.tensor_tensor(F_DT[:, :, :], QK[:, :, :], F_DT[:, :, :], ALU.mult))
                    for hh in range(BH):
                        own(V.scalar_tensor_tensor(out=F_IT[:, hh, :], in0=F_DT[:, hh, :], scalar=rk[:, hh:hh + 1],
                                                   in1=konst_at(K_UI), op0=ALU.mult, op1=ALU.mult))
                dve.wait_ge(f_lvps, lvs + 1)
                own(V.tensor_tensor(F_Dt[0:n, :, 0:n], bc(ident(n).unsqueeze(1), [n, 4, n]), heads(ps[7][:, :])[0:n, :, 0:n],
                                ALU.subtract), f_lv)
                lvs += 1
                for lv in range(1, 4 if c == 0 else LEVELS):
                    dve.wait_ge(f_lvps, lvs + 1)
                    own(V.tensor_copy(F_Y[0:n, :, 0:n], heads(ps[7][:, :])[0:n, :, 0:n]), f_lv)
                    dve.wait_ge(f_lvps, lvs + 2)
                    own(V.tensor_tensor(F_D[0:n, :, 0:n], F_D[0:n, :, 0:n], heads(ps[5][:, :])[0:n, :, 0:n], ALU.subtract))
                    own(V.tensor_tensor(F_Dt[0:n, :, 0:n], F_Dt[0:n, :, 0:n], heads(ps[6][:, :])[0:n, :, 0:n], ALU.subtract), f_lv)
                    lvs += 2
                if c == 0:
                    own(V.tensor_copy(F_R[0:n, :, :], F_VB[0:n, :, :]), f_r)
                else:
                    dve.wait_ge(f_ks, c)
                    for hh in range(BH):
                        own(V.scalar_tensor_tensor(out=F_R[:, hh, :], in0=heads(ps[0][:, :])[:, hh, :], scalar=ngk[:, hh:hh + 1],
                                                   in1=F_VB[:, hh, :], op0=ALU.mult, op1=ALU.add))
                    own(V.memset(mx8, 0.0), f_r)
                    dve.wait_ge(f_oc, c)
                    own(V.tensor_scalar(st2[:, 0:4], rqk[:, c, 0:4], float(BD ** -0.5), None, ALU.mult))
                    for hh in range(BH):
                        own(V.scalar_tensor_tensor(out=F_O[:, hh, :], in0=heads(ps[2][:, :])[:, hh, :], scalar=eg[:, hh:hh + 1],
                                                   in1=F_O[:, hh, :], op0=ALU.mult, op1=ALU.add))
                    o = oab[:, c - 1, AW:].rearrange("p (h c) -> p h c", h=4)
                    own(V.tensor_tensor(o, F_O[:, :, :], bc(st2[:, 0:4].unsqueeze(2), [P, 4, P]), ALU.mult))
                    own(V.tensor_tensor(F_O[:, :, :], o, o, ALU.mult))
                    own(V.tensor_reduce(ossq[:, 4 * (c - 1):4 * c], F_O[:, :, :], AX.X, ALU.add))
                dve.wait_ge(f_s, c + 1)
                if c == 0:
                    own(V.tensor_copy(F_S[:, :, :], heads(ps[4][:, :])), f_sc)
                else:
                    for hh in range(BH):
                        own(V.scalar_tensor_tensor(out=F_S[:, hh, :], in0=F_S[:, hh, :], scalar=el[:, hh:hh + 1],
                                                   in1=heads(ps[4][:, :])[:, hh, :], op0=ALU.mult, op1=ALU.add))
                    own(V.memset(mx8, 0.0), f_sc)
            own(V.tensor_scalar(ossq, ossq, 1.0 / BD, EPS, ALU.mult, ALU.add), d_stat)
            dve.wait_ge(a_stat, 14)
            own(V.reciprocal(orstd, orstd))
            for t in range(NT):
                o = oab[:, t, AW:].rearrange("p (h c) -> p h c", h=4)
                own(V.tensor_tensor(o, o, bc(orstd[:, 4 * t:4 * t + 4].unsqueeze(2), [P, 4, P]), ALU.mult))
                own(V.tensor_tensor(o, o, bc(dn_w.unsqueeze(1), [P, 4, P]), ALU.mult))
                own(V.tensor_tensor(o, o, zs[:, t, :].rearrange("p (h c) -> p h c", h=4), ALU.mult))
            q = 0
            for j in range(1, NT):
                w = P * (j + 1)
                row = isc[:, j - 1, 0:w]
                for hh in range(IH):
                    dve.wait_ge(i_rel, q + 1)
                    if hh == 0:
                        own(V.tensor_scalar(row, rel[q % 2][:, 0:w], wi[:, j, 0:1], None, ALU.mult), i_add)
                    else:
                        own(V.scalar_tensor_tensor(out=row, in0=rel[q % 2][:, 0:w], scalar=wi[:, j, hh:hh + 1], in1=row,
                                               op0=ALU.mult, op1=ALU.add), i_add)
                    dve.wait_ge(i_add, q + 1)
                    q += 1
                diag = isc[:, j - 1, P * j:w]
                own(V.tensor_tensor(diag, diag, konst_at(K_LI), ALU.mult))
                own(V.tensor_tensor(diag, diag, konst_at(K_LOW), ALU.add))
                for _ in range(TOPK // 8):
                    own(V.max(mx8, row))
                    own(V.match_replace(row, mx8, row, TAKEN))
                own(V.tensor_scalar(madd[:, j - 1, 0:w], row, TAKEN, HIDE, ALU.not_equal, ALU.mult))
            for j in range(NT):
                w = META + P * (j + 1)
                for hh in range(AH):
                    q = AH * j + hh
                    pr = prob[q % 2]
                    dve.wait_ge(a_sc, q + 1)
                    own(V.tensor_scalar(pr[:, 0:META], ps[5 + q % 2][:, 0:META], AD ** -0.5, None, ALU.mult))
                    mask = konst_at(K_ADD) if j == 0 else madd[:, j - 1, 0:P * (j + 1)]
                    own(V.scalar_tensor_tensor(out=pr[:, META:w], in0=ps[q % 2][:, 0:P * (j + 1)], scalar=AD ** -0.5, in1=mask,
                                               op0=ALU.mult, op1=ALU.add))
                    own(V.tensor_reduce(mx8[:, 0:1], pr[:, 0:w], AX.X, ALU.max))
                    own(V.tensor_scalar(qmax[:, hh:hh + 1], mx8[:, 0:1], -1.0, None, ALU.mult), a_msk)
                dve.wait_ge(a_exp, AH * (j + 1))
                own(V.reciprocal(qinv, qsum))
                dve.wait_ge(a_o, j + 1)
                own(V.tensor_tensor(oab[:, j, 0:AW].rearrange("p (a d) -> p a d", a=AH), ps[7][:, :].rearrange("p (a d) -> p a d", a=AH),
                                bc(qinv.unsqueeze(2), [P, AH, AD]), ALU.mult), a_on)
                dve.wait_ge(a_on, j + 1)
            own(V.memset(bgu, 0.0), table_ready)
            for t in range(NT):
                for half in range(2):
                    dve.wait_ge(g_ps, 2 * t + half + 1)
                    hs = h[:, D * t + 512 * half:D * t + 512 * half + 512]
                    own(V.tensor_tensor(hs, hs, ps[2 + half][:, :], ALU.add))
                own(V.memset(mx8, 0.0), g_h)
                dve.wait_ge(a_ssq, 6 + t)
                own(V.tensor_scalar(st2[:, t:t + 1], st1[:, t:t + 1], 1.0 / D, EPS, ALU.mult, ALU.add), d_stat)
                dve.wait_ge(a_stat, 15 + t)
                own(V.reciprocal(st4[:, t:t + 1], st3[:, t:t + 1]))
                own(V.scalar_tensor_tensor(out=xn[:, t, :], in0=h_t[t], scalar=st4[:, t:t + 1], in1=ffnw[:, :], op0=ALU.mult,
                                       op1=ALU.mult), g_xn)
                dve.wait_ge(g_lg, t + 1)
                own(V.tensor_tensor(lg[:, t, :], ps[6][:, 0:NE], br_w, ALU.add))
                own(V.max(mx8, lg[:, t, :]))
                own(V.max_index(eidx[:, 0:8], mx8, lg[:, t, :]))
                own(V.tensor_copy(qsum, eidx[:, 0:8]))
                own(V.tensor_scalar(selm[:, t, :], konst_at(K_IOTA, P, NE), qsum[:, 0:1], None, ALU.is_equal))
                for k in range(1, TOPE):
                    own(V.scalar_tensor_tensor(out=selm[:, t, :], in0=konst_at(K_IOTA, P, NE), scalar=qsum[:, k:k + 1],
                                               in1=selm[:, t, :], op0=ALU.is_equal, op1=ALU.add))
                own(V.tensor_scalar(lg[:, t, :], lg[:, t, :], mx8[:, 0:1], None, ALU.subtract))
                own(V.memset(mx8, 0.0), g_sel)
            gate3 = gate.rearrange("p (e t) -> p e t", t=NT)
            rank3 = rankm.rearrange("p (e t) -> p e t", t=NT)
            for t in range(NT):
                dve.wait_ge(a_stat, 19 + t)
                own(V.tensor_tensor(lg[:, t, :], lg[:, t, :], selm[:, t, :], ALU.mult))
                own(V.tensor_reduce(st1[:, t:t + 1], lg[:, t, :], AX.X, ALU.add))
                own(V.reciprocal(st2[:, t:t + 1], st1[:, t:t + 1]))
                own(V.tensor_scalar(gate3[:, :, t], lg[:, t, :], st2[:, t:t + 1], None, ALU.mult))
                own(V.tensor_copy(gtok, gate3[:, :, t]), g_gt)
                dve.wait_ge(g_rk, t + 1)
                own(V.tensor_scalar(tmpe, ps[7][:, 32 * t:32 * t + 32], 1.0, None, ALU.add))
                own(V.tensor_tensor(tmpe, tmpe, selm[:, t, :], ALU.mult))
                own(V.tensor_scalar(rank3[:, :, t], tmpe, -1.0, None, ALU.add))
                dve.wait_ge(g_gtc, t + 1)
                own(V.tensor_copy(gT, ps[0][0:NE, 0:P]))
                own(V.memset(mx8, 0.0), g_bd)
                for half in range(2):
                    dve.wait_ge(g_acc, 2 * t + half + 1)
                    hs = h[:, D * t + 512 * half:D * t + 512 * half + 512]
                    own(V.tensor_tensor(hs, hs, ps[1 + half][:, :], ALU.add))
            dve.wait_ge(g_rk, NT + 1)
            own(V.tensor_copy(cnt, ps[7][:, 128:160]))
            own(V.tensor_scalar(blocks, cnt, float(P), None, ALU.is_gt))
            for b in range(2, NT):
                own(V.scalar_tensor_tensor(out=blocks, in0=cnt, scalar=float(P * b), in1=blocks, op0=ALU.is_gt, op1=ALU.add))
            own(V.tensor_tensor_scan(cum, konst_at(K_ONE, P, NE), blocks, 0.0, ALU.mult, ALU.add))
            own(V.tensor_copy(etab[:, 0:NE], konst_at(K_IOTA, P, NE)))
            own(V.memset(shift[:, 0:NE], 0.0))
            for i in range(ITEMS - NE):
                own(V.tensor_scalar(tmpe, cum, float(i), None, ALU.is_le))
                own(V.tensor_reduce(etab[:, NE + i:NE + i + 1], tmpe, AX.X, ALU.add))
                own(V.tensor_tensor(tmpe, tmpe, blocks, ALU.mult))
                own(V.tensor_reduce(mx8[:, 0:1], tmpe, AX.X, ALU.add))
                own(V.tensor_scalar(shift[:, NE + i:NE + i + 1], mx8[:, 0:1], -float(P), float(P * (i + 1)), ALU.mult, ALU.add))
            own(V.tensor_scalar(etab, etab, float(NE - 1), None, ALU.min))
            own(V.tensor_copy(etab_i[:, :], etab))
            own(V.tensor_scalar(nitems_i[:, :], cum[:, NE - 1:NE], float(NE), None, ALU.add))
            own(V.memset(gcol, 0.0), table_ready)
            dve.wait_ge(table_ready, 2)
            items = dve.value_load(nitems_i[0:1, 0:1], min_val=NE, max_val=ITEMS - 1)

            def build_onehot(e, i):
                for t in range(NT):
                    V.tensor_scalar(onehot[:, t, :], konst_at(K_IOTA), shift[:, bass.ds(i, 1)], rankm[:, bass.ds(4 * e + t, 1)],
                                    ALU.add, ALU.is_equal)
                V.tensor_copy(sel, kc[:, bass.ds(K_ID + e, 1)].to_broadcast([P, P])).then_inc(p_built, 1)

            def add_scattered(i):
                for q in range(2 * NT):
                    t, half = q // 2, q % 2
                    dve.wait_ge(scat_ps, 8 * i + q + 1)
                    hs = h[:, D * t + 512 * half:D * t + 512 * half + 512]
                    V.scalar_tensor_tensor(out=hs, in0=ps[6 + q % 2][:, :], scalar=gcol[:, t:t + 1], in1=hs, op0=ALU.mult,
                                           op1=ALU.add).then_inc(acc_added, 1)

            build_onehot(0, 0)
            with dve.Fori(0, items) as i:
                e = dve.value_load(etab_i[0:1, bass.ds(i, 1)], min_val=0, max_val=NE - 1)
                e_next = dve.value_load(etab_i[0:1, bass.ds(i + 1, 1)], min_val=0, max_val=NE - 1)
                for n in range(4):
                    c = slice(256 * n, 256 * n + 256)
                    gu = ps[n][:, :].rearrange("p (f two) -> p f two", two=2)
                    dve.wait_ge(gu_ready, 4 * i + n + 1)
                    V.tensor_scalar(gm[:, c], gu[:, :, 0], LIMIT, None, ALU.min).then_inc(gm_ready, 1)
                    V.tensor_scalar(act[:, c], gu[:, :, 1], LIMIT, -LIMIT, ALU.min, ALU.max).then_inc(loop_step, 1)
                    dve.wait_ge(loop_step, 8 * i + 2 * n + 1)
                    V.scalar_tensor_tensor(out=act[:, c], in0=act[:, c], scalar=1.0, in1=gm[:, c], op0=ALU.add, op1=ALU.mult)\
                        .then_inc(loop_step, 1)
                    dve.wait_ge(loop_step, 8 * i + 2 * n + 2)
                    dve.wait_ge(sg_ready, 4 * i + n + 1)
                    V.tensor_tensor(act[:, c], act[:, c], sg[:, c], ALU.mult).then_inc(act_ready, 1)
                add_scattered(i)
                dve.wait_ge(acc_added, 8 * i + 8)
                dve.wait_ge(pt_ps, i + 1)
                V.tensor_copy(gcol, gate[:, bass.ds(4 * e, 4)])
                build_onehot(e_next, i + 1)
                dve.wait_ge(p_built, i + 2)
            add_scattered(items)

        @block.tensor
        def _(pe):
            M = nc.tensor.matmul
            TR = nc.tensor.transpose
            pe.wait_ge(konst_in, 16)
            pe.wait_ge(gains_in, 16 * 13)
            TR(ps[7][:, 0:58], wrow, ident(58)).then_inc(colw_T, 1)
            for t in range(5):
                n = tok_cols[t][1]
                pe.wait_ge(d_u, t + 1)
                if t >= 2:
                    pe.wait_ge(u_evac, 2 * (t - 1))
                for k in range(KD):
                    i = TR(ps[2 * (t % 2) + k // 4][:, P * (k % 4):P * (k % 4) + n], utmp[t % 2][0:n, P * k:P * k + P], ident(n))
                    if k % 4 == 3:
                        i.then_inc(u_T, 1)
            pe.wait_ge(u_evac, 10)
            for m in range(12):
                s = m // 4
                pe.wait_ge(slot_in[s], 16)
                if m >= 2:
                    pe.wait_ge(conv_evac, 2 * (m - 1))
                for half in range(2):
                    for k in range(KD):
                        i = M(ps[4 + 2 * (m % 2) + half][:, 0:264], w_group(s)[:, k, P * (m % 4):P * (m % 4) + P],
                              uT[:, k, 264 * half:264 * half + 264], start=(k == 0), stop=(k == KD - 1))
                    i.then_inc(conv_ps, 1)
                if m % 4 == 3:
                    pe.wait_ge(conv_ps, 2 * m + 2)
                    pe.sem_inc(group_used, 1)
            pe.wait_ge(conv_evac, 24)
            for m in range(8):
                pe.wait_ge(conv_sq, m + 1)
                for t, (at, n) in enumerate(tok_cols):
                    i = M(ps[7][0:n, 8 * t + m:8 * t + m + 1], convsq[m % 2][:, at:at + n], konst_at(K_ONE)[:, 0:1], start=True, stop=True)
                i.then_inc(qk_ssq, 1)
            for s in (3, 4):
                pe.wait_ge(slot_in[s], 16)
            pe.wait_ge(slot_in[5], 32)
            pe.wait_ge(slot_in[0], 32)
            pe.wait_ge(wkv_in, 16)
            for t, (at, n) in enumerate(tok_cols):
                if t:
                    pe.wait_ge(d_ropeT, t)
                for b, (w, c0, c1) in enumerate(((w_group(3), 0, 512), (w_group(4), 0, 512), (gC, 0, NPROJ), (w_group(0), 0, 512))):
                    if t == 0 and b in (0, 3):
                        pe.sem_inc(proj_ps, 1)
                        continue
                    if t == 0:
                        c0, c1 = (0, 256) if b == 1 else (328, 336)
                    for k in range(KD):
                        i = M(ps[b][0:n, c0:c1], uT[:, k, at:at + n], w[:, k, c0:c1], start=(k == 0), stop=(k == KD - 1))
                    i.then_inc(proj_ps, 1)
                pe.wait_ge(d_ckv, t + 1)
                for k in range(2):
                    i = TR(ps[4][:, P * k:P * k + n], ckv[0:n, P * k:P * k + P], ident(n))
                i.then_inc(ckv_T, 1)
                pe.wait_ge(d_ckvT, t + 1)
                for b in range(2):
                    for k in range(2):
                        i = M(ps[5 + b][0:n, :], ckvT[k][:, 0:n], wkv[:, k, 512 * b:512 * b + 512], start=(k == 0), stop=(k == 1))
                    i.then_inc(kv_ps, 1)
                pe.wait_ge(d_rope, t + 1)
                pe.wait_ge(a_proj, 2 * t + 2)
                if t == 0:
                    pe.wait_ge(d_ssqc, 1)
                for bank, a in ((7, 0), (4, 8), (5, 16), (6, 24)):
                    pairs = 1 if bank == 6 else 4
                    if t == 0 and bank != 4:
                        pe.sem_inc(rope_T, 1)
                        continue
                    for p in range(pairs):
                        src = rp[0:n, a + 2 * p:a + 2 * p + 2, :].rearrange("p a d -> p (a d)")
                        i = TR(ps[bank][:, P * p:P * p + n], src, ident(n))
                    i.then_inc(rope_T, 1)
            pe.wait_ge(rope_T, 20)
            pe.sem_inc(group_used, 1)
            pe.wait_ge(d_ropeT, 5)
            lvs, es = 0, 0
            for c, (at, n) in enumerate(tok_cols):
                cols = slice(PAD + at, PAD + at + n)
                pe.wait_ge(conv_silu, 12)
                pe.wait_ge(f_in, c + 1)
                if c:
                    pe.wait_ge(f_sc, c)
                for hh in range(BH):
                    q_, k_, v_ = qkvT[:, hh, cols], qkvT[:, 4 + hh, cols], qkvT[:, 8 + hh, cols]
                    hb = slice(P * hh, P * hh + n)
                    M(ps[0][:, hb], F_GB[0:n, hh, :], konst_at(K_UI, n, n), start=True, stop=True)
                    M(ps[1][0:n, hb], k_, k_, start=True, stop=True)
                    if c:
                        M(ps[2][0:n, hb], k_, q_, start=True, stop=True)
                    TR(ps[3][0:n, P * hh:P * hh + P], k_, ident())
                    TR(ps[4][0:n, P * hh:P * hh + P], v_, ident())
                    M(ps[5][0:n, hb], F_RK[0:n, hh, 0:n], ident(n), start=True, stop=True)
                M(ps[6][0:n, 0:4], konst_at(K_UI, n, n), gg[0:n, c, :], start=True, stop=True).then_inc(f_ps, 1)
                pe.wait_ge(f_A, c + 1)
                for hh in range(BH):
                    i = TR(ps[7][0:n, P * hh:P * hh + n], F_Y[0:n, hh, 0:n], ident(n))
                i.then_inc(f_lvps, 1)
                lvs += 1
                for lv in range(1, 4 if c == 0 else LEVELS):
                    pe.wait_ge(f_lv, lvs)
                    es += 1
                    pe.wait_ge(f_E, es)
                    for hh in range(BH):
                        i = M(ps[7][0:n, P * hh:P * hh + n], F_E[lv][0:n, hh, 0:n], F_Dt[0:n, hh, 0:n], start=True, stop=True)
                    i.then_inc(f_lvps, 1)
                    pe.wait_ge(f_lv, lvs + 1)
                    for hh in range(BH):
                        M(ps[5][0:n, P * hh:P * hh + n], F_Y[0:n, hh, 0:n], F_D[0:n, hh, 0:n], start=True, stop=True)
                        i = M(ps[6][0:n, P * hh:P * hh + n], F_D[0:n, hh, 0:n], F_Y[0:n, hh, 0:n], start=True, stop=True)
                    i.then_inc(f_lvps, 1)
                    lvs += 2
                pe.wait_ge(f_lv, lvs)
                if c:
                    for hh in range(BH):
                        i = M(ps[0][:, P * hh:P * hh + P], qkvT[:, 4 + hh, cols], F_S[:, hh, :], start=True, stop=True)
                    i.then_inc(f_ks, 1)
                pe.wait_ge(f_r, c + 1)
                for hh in range(BH):
                    i = M(ps[1][0:n, P * hh:P * hh + P], F_Dt[0:n, hh, 0:n], F_R[0:n, hh, :], start=True, stop=True)
                i.then_inc(f_vn, 1)
                if c:
                    for hh in range(BH):
                        M(ps[2][:, P * hh:P * hh + P], qkvT[:, hh, cols], F_S[:, hh, :], start=True, stop=True)
                pe.wait_ge(f_vnc, c + 1)
                if c:
                    for hh in range(BH):
                        i = M(ps[3][:, P * hh:P * hh + P], F_IT[:, hh, :], F_VN[:, hh, :], start=True, stop=True)
                    i.then_inc(f_o, 1)
                for hh in range(BH):
                    i = M(ps[4][:, P * hh:P * hh + P], F_KD[0:n, hh, :], F_VN[0:n, hh, :], start=True, stop=True)
                i.then_inc(f_s, 1)
            pe.wait_ge(f_sc, 5)
            q = 0
            for j in range(1, NT):
                for hh in range(IH):
                    rows = slice(64 * (hh % 2), 64 * (hh % 2) + 64)
                    if q >= 2:
                        pe.wait_ge(i_rel, q - 1)
                    M(ps[q % 2][:, 0:P * (j + 1)], qiT[rows, hh // 2, P * (j - 1):P * j], kiT[rows, 0:P * (j + 1)],
                      start=True, stop=True).then_inc(i_ps, 1)
                    q += 1
            pe.wait_ge(i_rel, q)

            def attn_scores(q):
                j, hh = q // AH, q % AH
                rows = slice(64 * (hh % 2), 64 * (hh % 2) + 64)
                if q >= 2:
                    pe.wait_ge(a_pT, q - 1)
                lhs = qT[rows, hh // 2, P * j:P * j + P]
                M(ps[5 + q % 2][:, 0:META], lhs, kT[rows, hh // 2, 0:META], start=True, stop=True)
                M(ps[q % 2][:, 0:P * (j + 1)], lhs, kT[rows, hh // 2, META:META + P * (j + 1)], start=True, stop=True)\
                    .then_inc(a_sc, 1)

            attn_scores(0)
            for q in range(NT * AH):
                j, hh = q // AH, q % AH
                if q + 1 < NT * AH:
                    attn_scores(q + 1)
                pe.wait_ge(a_exp, q + 1)
                if q >= 2:
                    pe.wait_ge(a_pTc, q - 1)
                for b in range(j + 1):
                    TR(ps[2 + q % 2][:, P * b:P * b + P], prob[q % 2][:, META + P * b:META + P * b + P], ident())
                TR(ps[5 + q % 2][0:META, P:2 * P], prob[q % 2][:, 0:META], ident()).then_inc(a_pT, 1)
                pe.wait_ge(a_pTc, q + 1)
                if hh == 0 and j:
                    pe.wait_ge(a_on, j)
                o = ps[7][:, AD * hh:AD * hh + AD]
                for b in range(j + 1):
                    M(o, pT[q % 2][:, P * b:P * b + P], vA[:, b, AD * hh:AD * hh + AD], start=(b == 0), stop=False)
                i = M(o, pT[q % 2][0:META, 512:640], vM[:, AD * hh:AD * hh + AD], start=False, stop=True)
                if hh == AH - 1:
                    i.then_inc(a_o, 1)
            pe.wait_ge(a_on, NT)
            pe.wait_ge(slot_in[4], 32)
            pe.wait_ge(slot_in[5], 48)
            pe.wait_ge(wr_in, 16)
            for t in range(NT):
                for k in range(KD):
                    if t and k % 4 == 0:
                        pe.wait_ge(g_Tc, 2 * (t - 1) + k // 4 + 1)
                    i = TR(ps[k // 4][:, P * (k % 4):P * (k % 4) + P], oab[:, t, P * k:P * k + P], ident())
                    if k % 4 == 3:
                        i.then_inc(g_T, 1)
                pe.wait_ge(g_Tc, 2 * t + 2)
                if t:
                    pe.wait_ge(g_h, t)
                for half in range(2):
                    for k in range(KD):
                        i = M(ps[2 + half][:, :], oT[:, k, :], w_group(4 + half)[:, k, :], start=(k == 0), stop=(k == KD - 1))
                    i.then_inc(g_ps, 1)
                pe.wait_ge(g_xn, t + 1)
                for k in range(KD):
                    i = TR(ps[4 + k // 4][:, P * (k % 4):P * (k % 4) + P], xn[:, t, P * k:P * k + P], ident())
                    if k % 4 == 3:
                        i.then_inc(g_xT, 1)
                pe.wait_ge(g_xTc, 2 * t + 2)
                if t:
                    pe.wait_ge(g_sel, t)
                for k in range(KD):
                    i = M(ps[6][:, 0:NE], xT[:, k, :], wr[:, k, :], start=(k == 0), stop=(k == KD - 1))
                i.then_inc(g_lg, 1)
            pe.wait_ge(g_sel, NT)
            for t in range(NT + 1):
                o = ps[7][:, 32 * t:32 * t + 32]
                for s in range(min(t, NT)):
                    i = M(o, konst_at(K_ONE), selm[:, s, :], start=(s == 0), stop=(t == NT and s == NT - 1))
                if t < NT:
                    i = M(o, konst_at(K_US), selm[:, t, :], start=(t == 0), stop=True)
            i.then_inc(g_rk, NT + 1)
            pe.wait_ge(bias_in, 32)
            for t in range(NT):
                pe.wait_ge(g_gt, t + 1)
                if t:
                    pe.wait_ge(g_bd, t)
                TR(ps[0][0:NE, 0:P], gtok, ident()).then_inc(g_gtc, 1)
                pe.wait_ge(g_bd, t + 1)
                for half in range(2):
                    M(ps[1 + half][:, :], gT, bdn[:, 512 * half:512 * half + 512], start=True, stop=True).then_inc(g_acc, 1)
            pe.sem_inc(g_rk, 1)

            def gather(i):
                pe.wait_ge(p_built, i + 1)
                for k in range(KD):
                    for t in range(NT):
                        ins = M(ps[6 + k // 4][:, P * (k % 4):P * (k % 4) + P], xn[:, t, P * k:P * k + P], onehot[:, t, :],
                                start=(t == 0), stop=(t == NT - 1))
                    if k % 4 == 3:
                        ins.then_inc(x_ps, 1)

            def scatter(i):
                for q in range(2 * NT):
                    t, half = q // 2, q % 2
                    if q >= 2:
                        pe.wait_ge(acc_added, 8 * i + q - 1)
                    M(ps[6 + q % 2][:, :], onehotT[:, t, :], ybuf[:, 512 * half:512 * half + 512], start=True, stop=True)\
                        .then_inc(scat_ps, 1)

            gather(0)
            pe.wait_ge(table_ready, 2)
            items = pe.value_load(nitems_i[0:1, 0:1], min_val=NE, max_val=ITEMS - 1)
            with pe.Fori(0, items) as i:
                pe.wait_ge(xe_ready, 2 * i + 2)
                pe.wait_ge(pt_ready, i + 1)
                for n in range(4):
                    pe.wait_ge(slot_in[n], 16 * i + 16 * (1 + PHASE1[n]))
                    M(ps[n][:, :], sel, bgu[:, 512 * n:512 * n + 512], start=True, stop=False)
                    for k in range(KD):
                        ins = M(ps[n][:, :], xe[:, k, :], w_group(n)[:, k, :], start=False, stop=(k == KD - 1))
                    ins.then_inc(gu_ready, 1)
                pe.wait_ge(gu_ready, 4 * i + 4)
                pe.sem_inc(chunk_used, 4)
                scatter(i)
                pe.wait_ge(act_ready, 4 * i + 4)
                for t in range(NT):
                    ins = TR(ps[2][:, P * t:P * t + P], onehot[:, t, :], ident())
                ins.then_inc(pt_ps, 1)
                for k in range(KD):
                    ins = TR(ps[k // 4][:, P * (k % 4):P * (k % 4) + P], act[:, P * k:P * k + P], ident())
                    if k % 4 == 3:
                        ins.then_inc(actT_ps, 1)
                pe.wait_ge(actT_ready, 2 * i + 2)
                for half in range(2):
                    pe.wait_ge(slot_in[4 + half], 16 * i + 16 * (1 + PHASE1[4 + half]))
                    for k in range(KD):
                        ins = M(ps[4 + half][:, :], actT[:, k, :], w_group(4 + half)[:, k, :], start=(k == 0), stop=(k == KD - 1))
                    ins.then_inc(y_ps, 1)
                pe.wait_ge(y_ps, 2 * i + 2)
                pe.sem_inc(chunk_used, 2)
                pe.wait_ge(acc_added, 8 * i + 8)
                gather(i + 1)
                pe.wait_ge(y_ready, 2 * i + 2)
            pe.wait_ge(pt_ready, items + 1)
            pe.wait_ge(xe_ready, 2 * items + 2)
            scatter(items)


PHASE1 = (2, 1, 1, 1, 2, 3)

_INS = ['x', 'meta_tokens', 'norm_mix_w', 'w_in', 'q_norm_w', 'k_norm_w', 'kv_norm_w', 'w_kv_up', 'conv_w', 'a_log',
        'dt_bias', 'delta_norm_w', 'w_out', 'norm_ffn_w', 'w_router', 'b_router', 'w_gate_up', 'b_gate_up', 'w_down', 'b_down']


def kernel(**inputs):
    import numpy as _np
    import concourse.bacc as _bacc
    from concourse import mybir as _mybir
    from concourse.bass_utils import run_bass_kernel_spmd as _run

    nc = _bacc.Bacc("TRN2", target_bir_lowering=False, num_devices=1)
    arrays = {"in_konst": constants()}
    args = [nc.dram_tensor("in_konst", (P, KONST), F32, kind="ExternalInput").ap()]
    for name in _INS:
        a = _np.ascontiguousarray(inputs[name])
        arrays[f"in_{name}"] = a
        args.append(nc.dram_tensor(f"in_{name}", a.shape, _mybir.dt.from_np(a.dtype), kind="ExternalInput").ap())
    args.append(nc.dram_tensor("out_0", (1, SEQ, D), F32, kind="ExternalOutput").ap())
    hybrid_layer(nc, *args)
    r = _run(nc, [arrays], core_ids=[0])
    return r.results[0]["out_0"]
```

```python
from contextlib import ExitStack

import concourse.bass as bass
import numpy as np
from concourse import mybir

ALU = mybir.AluOpType
ACT = mybir.ActivationFunctionType
AX = mybir.AxisListType
F32 = mybir.dt.float32
I32 = mybir.dt.int32
U32 = mybir.dt.uint32
F32R = mybir.dt.float32r
BF16 = mybir.dt.bfloat16
RING = 5
SCATTER_AT = ((0, 0), (0, 1), (0, 2), (1, 0), (1, 1), (1, 2), (2, 0), (2, 1))
PIECES = 20
FIRST = (0, 3, 6, 9, 12, 16)

P = 128
D = 1024
KD = D // P
SEQ = 512
NT = SEQ // P
META = 16
T = META + SEQ
AH, AD = 8, 64
AW = AH * AD
RANK = 256
IH = 8
TOPK = 128
BH, BD = 4, 128
BW = BH * BD
CW = 4
PAD = CW - 1
NE = 32
TOPE = 4
FF = 1024
EPS = 1e-6
LIMIT = 7.0
ALPHA = 1.702
ITEMS = 48
INCOLS = 3408
C_Q, C_CKV, C_BQKV, C_Z, C_BETA = 0, 512, 1352, 2888, 3400
NPROJ = 336
LOW = -1.0e38
TAKEN = -3.0e38
HIDE = -1.0e30
LEVELS = 7
ROPE_H = 25

K_ID = 0
K_UI = K_ID + P
K_US = K_UI + P
K_LS = K_US + P
K_ONE = K_LS + P
K_LV = K_ONE + P
K_IOTA = K_LV + LEVELS * P
K_ADD = K_IOTA + P
K_LOW = K_ADD + P
K_LI = K_LOW + P
K_TWO = K_LI + P
K_COS = K_TWO + 2 * 32
K_SIN = K_COS + NT * 32
K_MCOS = K_SIN + NT * 32
K_MSIN = K_MCOS + 32
KONST = K_MSIN + 32


def constants():
    k = np.zeros((P, KONST), np.float32)
    r, c = np.meshgrid(np.arange(P), np.arange(P), indexing="ij")
    k[:, K_ID:K_ID + P] = r == c
    k[:, K_UI:K_UI + P] = r <= c
    k[:, K_US:K_US + P] = r < c
    k[:, K_LS:K_LS + P] = r > c
    k[:, K_ONE:K_ONE + P] = 1
    for lv in range(LEVELS):
        at = K_LV + lv * P
        k[:, at:at + P] = (r > c) & (r >> (lv + 1) == c >> (lv + 1)) & (r >> lv != c >> lv)
    k[:, K_IOTA:K_IOTA + P] = c
    k[:, K_ADD:K_ADD + P] = np.where(c <= r, 0, HIDE)
    k[:, K_LOW:K_LOW + P] = np.where(c <= r, 0, LOW)
    k[:, K_LI:K_LI + P] = c <= r
    for half in range(2):
        k[:, K_TWO + NE * half:K_TWO + NE * half + NE] = (r - 64 * half == c)[:, :NE] | (r - 64 * half - NE == c)[:, :NE]
    inv = np.float32(10000.0) ** (-np.arange(0, AD, 2, dtype=np.float32) / np.float32(AD))
    ang = np.arange(T, dtype=np.float32)[:, None] * inv[None, :]
    cos, sin = np.cos(ang).astype(np.float32), np.sin(ang).astype(np.float32)
    for t in range(NT):
        rows = slice(META + P * t, META + P * t + P)
        k[:, K_COS + 32 * t:K_COS + 32 * t + 32] = cos[rows]
        k[:, K_SIN + 32 * t:K_SIN + 32 * t + 32] = sin[rows]
    k[:META, K_MCOS:K_MCOS + 32] = cos[:META]
    k[:META, K_MSIN:K_MSIN + 32] = sin[:META]
    return k


def hybrid_layer(nc, konst, x, meta_tokens, norm_mix_w, w_in, q_norm_w, k_norm_w, kv_norm_w, w_kv_up, conv_w,
                 a_log, dt_bias, delta_norm_w, w_out, norm_ffn_w, w_router, b_router, w_gate_up, b_gate_up,
                 w_down, b_down, out):
    with ExitStack() as ctx:
        def sb(name, cols, dt=F32):
            return ctx.enter_context(nc.sbuf_tensor(name, [P, cols], dt))

        def sem(name):
            return ctx.enter_context(nc.semaphore(name))

        ps = [ctx.enter_context(nc.psum_tensor(f"bank{i}", [P, 512], F32)) for i in range(8)]

        h = sb("h", NT * D)
        kc = sb("kc", KONST)
        ffnw = sb("ffnw", D)
        gains = sb("gains", 64 + 64 + BD + NE + 2 * BH)
        colw = sb("colw", 58)
        small = sb("small", 900)
        N_RING, N_R1, N_R2, N_R3 = 6 * 4096, KD * T, 12 * (T + PAD), 8768
        AT_R1, AT_R2, AT_R3 = N_RING, N_RING + N_R1, N_RING + N_R1 + N_R2 + 4
        arena_tensor = sb("arena", AT_R3 + N_R3)
        arena = nc.lookup_mloc(arena_tensor).addr

        def place(name, where, cols, dt=F32):
            return nc.alloc_sbuf_tensor_at(name, [P, cols], dt, offset=arena + 4 * where)

        ring = place("ring", 0, N_RING)
        r1 = place("r1", AT_R1, N_R1)
        r2 = place("r2", AT_R2, N_R2)
        r3 = place("r3", AT_R3, N_R3)
        xn = [place("xn_b0", 3 * 4096, 4096, BF16), place("xn_b1", 3 * 4096 + 2048, 4096, BF16),
              place("xn_b2", AT_R2, 4096, BF16)]
        w_hi = [place(f"w_hi{b}", 4 * 4096 + 1024 * b if b < 4 else AT_R2 + 2048, 1024, F32R) for b in range(RING)]
        w_lo = [place(f"w_lo{b}", 5 * 4096 + 1024 * b if b < 4 else AT_R2 + 3072, 1024, F32R) for b in range(RING)]
        xe = place("xe", AT_R1 + 3072, 256)
        xe_hi = place("xe_hi", AT_R1 + 3328, 768, F32R)
        x_rest = place("x_rest", AT_R2 + 2048, 1024)
        xe_lo = place("xe_lo", AT_R2 + 5120, 768, F32R)
        actT_hi, actT_lo = place("actT_hi", AT_R3, 1024, F32R), place("actT_lo", AT_R3 + 1024, 1024, F32R)
        y_hi, y_lo = place("y_hi", AT_R3 + 2304, 1024, F32R), place("y_lo", AT_R3 + 3328, 1024, F32R)
        sel = [place("sel0", AT_R3 + 4352, P, F32R), place("sel1", AT_R3 + 6400, P, F32R)]
        onehot_t, onehotT_t = place("onehot", AT_R3 + 6528, 512, BF16), place("onehotT", AT_R3 + 7040, 512, F32R)
        bias2 = place("bias2", AT_R3 + 7552, 1024, F32R)

        def slot(s, n=4096, at=0):
            return ring[:, 4096 * s + at:4096 * s + at + n]

        def konst_at(at, rows=P, n=P):
            return kc[0:rows, at:at + n]

        def ident(n=P):
            return kc[0:n, K_ID:K_ID + n]

        h_t = [h[:, D * t:D * t + D] for t in range(NT)]
        qn_w, kn_w = gains[:, 0:64], gains[:, 64:128]
        dn_w = gains[:, 128:256]
        br_w = gains[:, 256:288]
        alog, dtb = gains[:, 288:292], gains[:, 292:296]
        uT = r1[:, :].rearrange("p (k t) -> p k t", k=KD)
        oab = r1[:, 0:NT * D].rearrange("p (t d) -> p t d", t=NT)
        qkvT = r2[:, :].rearrange("p (m t) -> p m t", m=12)
        qT = r3[:, 0:2048].rearrange("p (a t) -> p a t", a=4)
        kT = r3[:, 2048:4160].rearrange("p (a t) -> p a t", a=4)
        vA = r3[:, 4160:6208].rearrange("p (t d) -> p t d", t=NT)
        vM = r3[0:META, 6208:6720]
        qiT = r3[:, 6720:8256].rearrange("p (a t) -> p a t", a=4)
        kiT = r3[:, 8256:8768]
        utmp = [r3[:, 0:1024], r3[:, 1024:2048]]
        metax = r3[0:META, 2048:3072]
        conv_a = [r3[:, 3072:3600], r3[:, 3600:4128]]
        wrow = r3[0:58, 4128:4256]
        sq = r3[:, 5056:6080]
        convsq = [r3[:, 6080:6608], r3[:, 6608:7136]]
        zs = slot(2, 2048).rearrange("p (t d) -> p t d", t=NT)
        rp = slot(2, 1664, 2048).rearrange("p (a d) -> p a d", a=26)
        pre = slot(1, 1600, 2048).rearrange("p (a d) -> p a d", a=ROPE_H)
        sqC = slot(5, 768, KD * NPROJ)
        ckv = slot(5, 256, KD * NPROJ + 768)
        square_out = r2[:, 5120:6144]
        sm_at = [0]

        def sm(n):
            sm_at[0] += n
            return small[:, sm_at[0] - n:sm_at[0]]

        ssqA, rsA = sm(5), sm(5)
        ba = sm(5 * 8).rearrange("p (t c) -> p t c", t=5)
        beta = sm(20).rearrange("p (t c) -> p t c", t=5)
        gg = sm(20).rearrange("p (t c) -> p t c", t=5)
        rqk = sm(40).rearrange("p (t c) -> p t c", t=5)
        wi = sm(NT * 8).rearrange("p (t c) -> p t c", t=NT)
        st1, st2, st3, st4 = sm(20), sm(20), sm(20), sm(20)
        ea = sm(4)
        ckvT = [sm(P), sm(P)]
        gcc, eg, el, ngk, br = sm(4), sm(4), sm(4), sm(4), sm(4)
        mx8 = sm(8)
        qmax, qsum, qinv = sm(8), sm(8), sm(8)
        ossq, orstd = sm(16), sm(16)

        konst_in, x_in, gains_in, wrow_in = sem("konst_in"), [sem(f"x_in{i}") for i in range(5)], sem("gains_in"), sem("wrow_in")
        slot_in = [sem(f"slot_in{s}") for s in range(6)]
        wkv_in, wr_in, bias_in = sem("wkv_in"), sem("wr_in"), sem("bias_in")
        colw_T, u_T, u_evac = sem("colw_T"), sem("u_T"), sem("u_evac")
        conv_ps, conv_evac, conv_silu, conv_sq, qk_ssq = (sem("conv_ps"), sem("conv_evac"), sem("conv_silu"),
                                                          sem("conv_sq"), sem("qk_ssq"))
        group_used = sem("group_used")
        proj_ps, ckv_T, kv_ps, rope_T = sem("proj_ps"), sem("ckv_T"), sem("kv_ps"), sem("rope_T")
        act_step = sem("act_step")
        dve_step = sem("dve_step")
        pool_step = sem("pool_step")
        d_u, d_colw, d_conv, d_ckv, d_ckvT, d_rope, d_ropeT = (sem("d_u"), sem("d_colw"), sem("d_conv"), sem("d_ckv"),
                                                               sem("d_ckvT"), sem("d_rope"), sem("d_ropeT"))
        d_ssqc = sem("d_ssqc")
        d_stat, a_stat, a_proj, a_z, a_ssq = sem("d_stat"), sem("a_stat"), sem("a_proj"), sem("a_z"), sem("a_ssq")
        f_in, f_ps, f_dd, f_exp, f_A, f_E, f_lv, f_lvps = (sem("f_in"), sem("f_ps"), sem("f_dd"), sem("f_exp"),
                                                           sem("f_A"), sem("f_E"), sem("f_lv"), sem("f_lvps"))
        f_ks, f_r, f_vn, f_vnc, f_o, f_oc, f_s, f_sc = (sem("f_ks"), sem("f_r"), sem("f_vn"), sem("f_vnc"), sem("f_o"),
                                                        sem("f_oc"), sem("f_s"), sem("f_sc"))
        i_ps, i_rel, i_add = sem("i_ps"), sem("i_rel"), sem("i_add")
        a_sc, a_msk, a_exp, a_pT, a_pTc, a_o, a_on = (sem("a_sc"), sem("a_msk"), sem("a_exp"), sem("a_pT"), sem("a_pTc"),
                                                      sem("a_o"), sem("a_on"))
        g_T, g_Tc, g_ps, g_h, g_xn, g_xT, g_xTc, g_lg, g_sel, g_rk, g_gt, g_gtc, g_bd, g_acc = (
            sem("g_T"), sem("g_Tc"), sem("g_ps"), sem("g_h"), sem("g_xn"), sem("g_xT"), sem("g_xTc"), sem("g_lg"),
            sem("g_sel"), sem("g_rk"), sem("g_gt"), sem("g_gtc"), sem("g_bd"), sem("g_acc"))
        table_ready = sem("table_ready")
        p_built, x_ps, xe_ready, gm_ready, sg_ready, act_ready = (
            sem("p_built"), sem("x_ps"), sem("xe_ready"), sem("gm_ready"), sem("sg_ready"), sem("act_ready"))
        pt_ps, pt_ready, actT_ps, actT_ready, y_ready, scat_ps, acc_added, loop_step = (
            sem("pt_ps"), sem("pt_ready"), sem("actT_ps"), sem("actT_ready"), sem("y_ready"),
            sem("scat_ps"), sem("acc_added"), sem("loop_step"))
        out_done = sem("out_done")
        raw_in = [sem(f"raw_in{r}") for r in range(3)]
        w_hi_ready, w_lo_ready, piece_used = sem("w_hi_ready"), sem("w_lo_ready"), sem("piece_used")
        plain_used = sem("plain_used")
        actT_hi_ready, y_hi_ready, xe_hi_ready = sem("actT_hi_ready"), sem("y_hi_ready"), sem("xe_hi_ready")
        xe_whole_ready, table_loaded = sem("xe_whole_ready"), sem("table_loaded")

        fs = [slot(s, 512, 512 * i) for s in (0, 1, 3) for i in range(8)]

        def heads(ap):
            return ap.rearrange("p (h c) -> p h c", h=4)

        F_GB, F_RK, F_KD, F_VB, F_DN, F_DT, F_A, F_IT, F_D, F_Dt, F_Y, F_S, F_R, F_VN, F_O = [heads(a) for a in fs[0:15]]
        F_E = [heads(a) for a in fs[15:22]]
        isc = slot(0, 1536).rearrange("p (t c) -> p t c", t=3)
        rel = [slot(0, 512, 1536), slot(0, 512, 2048)]
        madd = slot(1, 1536).rearrange("p (t c) -> p t c", t=3)
        prob = [slot(3, T), slot(3, T, T)]
        pT = [slot(3, 640, 2 * T), slot(3, 640, 2 * T + 640)]
        oT = r3[:, 0:1024].rearrange("p (k c) -> p k c", k=KD)
        xT = r3[:, 1024:2048].rearrange("p (k c) -> p k c", k=KD)
        wr = r3[:, 2048:2304].rearrange("p (k e) -> p k e", k=KD)
        bias_raw = r3[:, 2304:3328]
        bdn = r3[0:NE, 4352:5376]
        lg = r3[:, 5376:5504].rearrange("p (t e) -> p t e", t=NT)
        selm = r3[:, 5504:5632].rearrange("p (t e) -> p t e", t=NT)
        gate = r3[:, 5632:5760]
        rankm = r3[:, 5760:5888]
        gtok = r3[:, 5888:5920]
        gT = r3[0:NE, 5920:6048]
        etab = r3[:, 6048:6048 + ITEMS]
        shift = r3[:, 6112:6112 + ITEMS]
        cnt, blocks, cum, tmpe = r3[:, 6176:6208], r3[:, 6208:6240], r3[:, 6240:6272], r3[:, 6272:6304]
        gcol = r3[:, 6304:6308]
        onehot = onehot_t[:, :].rearrange("p (t c) -> p t c", t=NT)
        ident_b = place("ident_b", AT_R3 + 6784, P, BF16)
        onehotT = onehotT_t[:, :].rearrange("p (t c) -> p t c", t=NT)
        xraw = r2[:, 4096:5120]
        gm, sg, act = r1[:, 0:1024], r1[:, 1024:2048], r1[:, 2048:3072]

        def f32(ap):
            return ap.bitcast(F32)

        def raw_piece(n):
            s, j = (n // 3, 1 + n % 3) if n < 12 else (n // 4 + 1, n % 4)
            return piece(slot(s % 3), j)

        def piece(t, j):
            return t[:, 1024 * j:1024 * j + 1024]
        eidx = ctx.enter_context(nc.sbuf_tensor("eidx", [P, 8 + 1], U32))
        etab_i = ctx.enter_context(nc.sbuf_tensor("etab_i", [P, ITEMS], I32))
        nitems_i = ctx.enter_context(nc.sbuf_tensor("nitems_i", [P, 1], I32))

        w_in0 = w_in[0].rearrange("(k p) n -> p k n", p=P)
        tok_cols = [(0, META)] + [(META + P * t, P) for t in range(NT)]

        def w_group(s, n=512):
            return slot(s, KD * n).rearrange("p (k n) -> p k n", k=KD)

        gC = w_group(5, NPROJ)
        wkv = slot(1, 2048).rearrange("p (k n) -> p k n", k=2)

        def expert_chunk(e, s):
            if s < 4:
                return w_gate_up[0, bass.ds(e, 1)].rearrange("o (k p) n -> p (o k) n", p=P)[:, :, 512 * s:512 * s + 512]
            return w_down[0, bass.ds(e, 1)].rearrange("o (k p) n -> p (o k) n", p=P)[:, :, 512 * (s - 4):512 * (s - 4) + 512]

        block = ctx.enter_context(nc.Block())

        @block.sync
        def _(sp):
            sp.dma_start(metax, meta_tokens).then_inc(x_in[0], 16)
            for t in range(NT):
                sp.dma_start(h_t[t], x[0, P * t:P * t + P, :]).then_inc(x_in[t + 1], 16)
            sp.dma_start(kc[:, :], konst).then_inc(konst_in, 16)
            for s in range(3):
                sp.dma_start(w_group(s), w_in0[:, :, C_BQKV + 512 * s:C_BQKV + 512 * s + 512]).then_inc(slot_in[s], 16)
            sp.dma_start(w_group(3), w_in0[:, :, 0:512]).then_inc(slot_in[3], 16)
            sp.dma_start(w_group(4), w_in0[:, :, 512:1024]).then_inc(slot_in[4], 16)
            sp.dma_start(gC[:, :, 0:328], w_in0[:, :, 1024:1352]).then_inc(slot_in[5], 16)
            sp.dma_start(gC[:, :, 328:336], w_in0[:, :, C_BETA:C_BETA + 8]).then_inc(slot_in[5], 16)
            sp.wait_ge(group_used, 1)
            sp.dma_start(w_group(0), w_in0[:, :, C_Z:C_Z + 512]).then_inc(slot_in[0], 16)
            sp.wait_ge(group_used, 2)
            sp.dma_start(wkv, w_kv_up[0].rearrange("(k p) n -> p k n", p=P)).then_inc(wkv_in, 16)
            sp.wait_ge(group_used, 4)
            for n in range(2):
                sp.dma_start(w_group(4 + n), w_out[0].rearrange("(k p) n -> p k n", p=P)[:, :, 512 * n:512 * n + 512])\
                  .then_inc(slot_in[4 + n], 16)
            sp.wait_ge(a_on, NT)
            sp.dma_start(wr, w_router[0].rearrange("(k p) e -> p k e", p=P)).then_inc(wr_in, 16)
            sp.dma_start(bdn, b_down[0]).then_inc(bias_in, 16)
            for row in range(4):
                sp.dma_start(bias_raw[NE * row:NE * row + NE, :], b_gate_up[0, :, 1024 * (row // 2):1024 * (row // 2) + 1024])\
                  .then_inc(bias_in, 16)

            def load(e, i, s):
                if s in (1, 2):
                    sp.wait_ge(w_lo_ready, PIECES * i + 4 * s - 8)
                else:
                    sp.wait_ge(plain_used, 4 * i + max(0, s - 2))
                sp.dma_start(w_group(s % 3), expert_chunk(e, s)).then_inc(raw_in[s % 3], 16)

            def load_item(e, e_next, i):
                for s in range(2, 6):
                    load(e, i, s)
                for s in range(2):
                    load(e_next, i + 1, s)

            for s in range(3):
                sp.dma_start(w_group(s), expert_chunk(0, s)).then_inc(raw_in[s], 16)
            for s in range(3, 6):
                load(0, 0, s)
            load(1, 1, 0)
            load(1, 1, 1)
            with sp.Fori(1, NE - 1) as e:
                load_item(e, e + 1, e)
            items = sp.value_load(nitems_i[0:1, 0:1], min_val=NE, max_val=ITEMS - 1)
            with sp.Fori(NE - 1, items) as i:
                e = sp.value_load(etab_i[0:1, bass.ds(i, 1)], min_val=0, max_val=NE - 1)
                e_next = sp.value_load(etab_i[0:1, bass.ds(i + 1, 1)], min_val=0, max_val=NE - 1)
                load_item(e, e_next, i)
            for r in range(2):
                sp.wait_ge(raw_in[r], 32 * items + 16)
            sp.wait_ge(acc_added, 8 * items + 8)
            for t in range(NT):
                sp.dma_start(out[0, P * t:P * t + P, :], h_t[t]).then_inc(out_done, 16)
            sp.wait_ge(out_done, 16 * NT)

        @block.gpsimd
        def _(pool):
            for dst, src in ((qn_w, q_norm_w), (kn_w, k_norm_w), (dn_w, delta_norm_w), (br_w, b_router), (alog, a_log),
                             (dtb, dt_bias), (ffnw[:, :], norm_ffn_w)):
                pool.dma_start(dst, src.partition_broadcast(P)).then_inc(gains_in, 16)
            for c in range(5):
                n = META if c == 0 else P
                pool.wait_ge(f_A, c + 1)
                for lv in range(1, 4 if c == 0 else LEVELS):
                    m = konst_at(K_LV + lv * P, n, n).unsqueeze(1).to_broadcast([n, 4, n])
                    nc.gpsimd.tensor_tensor(F_E[lv][0:n, :, 0:n], F_A[0:n, :, 0:n], m, ALU.mult).then_inc(f_E, 1)

        @block.scalar
        def _(act_e):
            n_act = [0]

            def own(ins):
                n_act[0] += 1
                ins.then_inc(act_step, 1)
                act_e.wait_ge(act_step, n_act[0])

            A = nc.scalar.activation
            rows = [(norm_mix_w[0].rearrange("(k p) -> k p", p=P), 48, 56), (kv_norm_w[0].rearrange("(k p) -> k p", p=P), 56, 58)]
            for w in range(CW):
                act_e.dma_start(wrow[12 * w:12 * w + 12, :], conv_w[0, w].rearrange("(m p) -> m p", p=P)).then_inc(wrow_in, 16)
            for src, a, b in rows:
                act_e.dma_start(wrow[a:b, :], src).then_inc(wrow_in, 16)
            act_e.wait_ge(d_colw, 1)
            for t in range(5):
                n = tok_cols[t][1]
                src = metax if t == 0 else h_t[t - 1]
                act_e.wait_ge(x_in[t], 16)
                A(sq[0:n, :], src, ACT.Square, accum_out=ssqA[0:n, t:t + 1]).then_inc(a_ssq, 1)
                act_e.wait_ge(a_ssq, t + 1)
            act_e.wait_ge(d_stat, 1)
            A(st1[:, 0:5], rsA, ACT.Sqrt).then_inc(a_stat, 1)
            for m in range(12):
                for half in range(2):
                    act_e.wait_ge(conv_ps, 2 * m + half + 1)
                    A(qkvT[:, m, PAD + 264 * half:PAD + 264 * half + 264], ps[4 + 2 * (m % 2) + half][:, 0:264], ACT.Copy)\
                        .then_inc(conv_evac, 1)
            for m in range(12):
                act_e.wait_ge(d_conv, m + 1)
                A(qkvT[:, m, PAD:], qkvT[:, m, PAD:], ACT.Silu).then_inc(conv_silu, 1)
                if m < 8:
                    act_e.wait_ge(conv_silu, m + 1)
                    if m >= 2:
                        act_e.wait_ge(qk_ssq, m - 1)
                    A(convsq[m % 2], qkvT[:, m, PAD:], ACT.Square).then_inc(conv_sq, 1)
            for t in range(5):
                n = tok_cols[t][1]
                act_e.wait_ge(proj_ps, 4 * t + 4)
                if t:
                    act_e.wait_ge(d_rope, t)
                    own(A(sqC[:, 0:512], ps[0][:, :], ACT.Square))
                own(A(sqC[0:n, 512:768], ps[1][0:n, 0:256], ACT.Square))
                if t:
                    own(A(pre[:, 16:20, :], ps[1][:, 256:512].rearrange("p (a d) -> p a d", a=4), ACT.Copy))
                    own(A(pre[:, 20:24, :], ps[2][:, 0:256].rearrange("p (a d) -> p a d", a=4), ACT.Copy))
                    own(A(pre[:, 24, :], ps[2][:, 256:320], ACT.Copy))
                    own(A(wi[:, t - 1, :], ps[2][:, 320:328], ACT.Copy, scale=float(IH ** -0.5 * 64 ** -0.5)))
                    own(A(zs[:, t - 1, :], ps[3][:, :], ACT.Copy))
                A(ba[0:n, t, :], ps[2][0:n, 328:336], ACT.Copy).then_inc(a_proj, 1)
                act_e.wait_ge(d_stat, 2 + 2 * t)
                A(st2[0:n, 0:9], st1[0:n, 0:9], ACT.Sqrt).then_inc(a_stat, 1)
                act_e.wait_ge(kv_ps, 2 * t + 2)
                own(A(sqC[0:n, 0:512], ps[5][0:n, :], ACT.Square))
                A(vM if t == 0 else vA[:, t - 1, :], ps[6][0:n, :], ACT.Copy).then_inc(a_proj, 1)
                act_e.wait_ge(d_stat, 3 + 2 * t)
                A(st2[0:n, 0:8], st1[0:n, 0:8], ACT.Sqrt).then_inc(a_stat, 1)
            act_e.wait_ge(d_stat, 12)
            A(rqk[:, :, :], rqk[:, :, :], ACT.Sqrt).then_inc(a_stat, 1)
            act_e.wait_ge(d_stat, 13)
            own(A(zs[:, :, :], zs[:, :, :], ACT.Silu))
            own(A(beta[:, :, :], ba[:, :, 0:4], ACT.Sigmoid))
            own(A(ea, alog, ACT.Exp))
            own(A(st1, st1, ACT.Exp, scale=-1.0))
            A(st3, st1, ACT.Ln, bias=1.0).then_inc(a_stat, 1)
            for c in range(5):
                n = META if c == 0 else P
                act_e.wait_ge(f_dd, c + 1)
                own(A(F_DN[0:n, :, 0:n], F_DN[0:n, :, 0:n], ACT.Exp, scale=-1.0))
                own(A(F_DT[0:n, :, 0:n], F_DT[0:n, :, 0:n], ACT.Exp))
                own(A(eg[0:n, :], gcc[0:n, :], ACT.Exp))
                A(el, el, ACT.Exp).then_inc(f_exp, 1)
                act_e.wait_ge(f_vn, c + 1)
                A(F_VN[0:n, :, :], heads(ps[1][0:n, :]), ACT.Copy).then_inc(f_vnc, 1)
                if c:
                    act_e.wait_ge(f_o, c)
                    A(F_O[:, :, :], heads(ps[3][:, :]), ACT.Copy).then_inc(f_oc, 1)
            act_e.wait_ge(d_stat, 14)
            A(orstd, ossq, ACT.Sqrt).then_inc(a_stat, 1)
            q = 0
            for j in range(1, NT):
                w = P * (j + 1)
                for hh in range(IH):
                    act_e.wait_ge(i_ps, q + 1)
                    if q >= 2:
                        act_e.wait_ge(i_add, q - 1)
                    A(rel[q % 2][:, 0:w], ps[q % 2][:, 0:w], ACT.Relu).then_inc(i_rel, 1)
                    q += 1
            for j in range(NT):
                w = META + P * (j + 1)
                for hh in range(AH):
                    q = AH * j + hh
                    act_e.wait_ge(a_msk, q + 1)
                    A(prob[q % 2][:, 0:w], prob[q % 2][:, 0:w], ACT.Exp, bias=qmax[:, hh:hh + 1],
                      accum_out=qsum[:, hh:hh + 1]).then_inc(a_exp, 1)
                    act_e.wait_ge(a_pT, q + 1)
                    own(A(pT[q % 2][:, 0:P * (j + 1)], ps[2 + q % 2][:, 0:P * (j + 1)], ACT.Copy))
                    A(pT[q % 2][0:META, 512:640], ps[4][0:META, 0:P], ACT.Copy).then_inc(a_pTc, 1)

            def copy_oT(t):
                for half in range(2):
                    act_e.wait_ge(g_T, 2 * t + half + 1)
                    if t:
                        act_e.wait_ge(g_ps, 2 * t)
                    A(oT[:, 4 * half:4 * half + 4, :], ps[half][:, :].rearrange("p (k c) -> p k c", k=4), ACT.Copy)\
                        .then_inc(g_Tc, 1)

            copy_oT(0)
            for t in range(NT):
                if t + 1 < NT:
                    copy_oT(t + 1)
                act_e.wait_ge(g_h, t + 1)
                A(square_out, h_t[t], ACT.Square, accum_out=st1[:, t:t + 1]).then_inc(a_ssq, 1)
                act_e.wait_ge(d_stat, 15 + t)
                A(st3[:, t:t + 1], st2[:, t:t + 1], ACT.Sqrt).then_inc(a_stat, 1)
                for half in range(2):
                    act_e.wait_ge(g_xT, 2 * t + half + 1)
                    A(xT[:, 4 * half:4 * half + 4, :], ps[4 + half][:, :].rearrange("p (k c) -> p k c", k=4), ACT.Copy)\
                        .then_inc(g_xTc, 1)
            for t in range(NT):
                act_e.wait_ge(g_sel, t + 1)
                A(lg[:, t, :], lg[:, t, :], ACT.Exp).then_inc(a_stat, 1)
            act_e.wait_ge(g_rk, NT + 2)
            A(onehotT, kc[:, 0:512].rearrange("p (t c) -> p t c", t=4), ACT.Copy, scale=0.0).then_inc(pt_ready, 1)

            def round_piece(i, n):
                if n in FIRST:
                    s = FIRST.index(n)
                    act_e.wait_ge(raw_in[s % 3], 32 * i + (16 if s < 3 else 32))
                act_e.wait_ge(piece_used, PIECES * i + n + 1)
                A(w_hi[n % RING][:, :], raw_piece(n), ACT.Copy).then_inc(w_hi_ready, 1)

            def sigmoid(i, n):
                act_e.wait_ge(gm_ready, 4 * i + n + 1)
                A(sg[:, 256 * n:256 * n + 256], gm[:, 256 * n:256 * n + 256], ACT.Sigmoid, scale=ALPHA).then_inc(sg_ready, 1)

            def copy_xe(i):
                act_e.wait_ge(x_ps, 2 * i + 1)
                A(xe[:, :], ps[6][:, 0:256], ACT.Copy).then_inc(xe_whole_ready, 1)
                A(xe_hi[:, 0:256], ps[6][:, 256:512], ACT.Copy).then_inc(xe_hi_ready, 1)
                act_e.wait_ge(x_ps, 2 * i + 2)
                A(xe_hi[:, 256:768], ps[7][:, :], ACT.Copy).then_inc(xe_hi_ready, 1)

            def copy_actT(i, half):
                act_e.wait_ge(actT_ps, 2 * i + half + 1)
                A(actT_hi[:, 512 * half:512 * half + 512], ps[half][:, :], ACT.Copy).then_inc(actT_hi_ready, 1)

            def copy_y(i, half):
                act_e.wait_ge(piece_used, PIECES * i + RING + 16 + 4 * half)
                A(y_hi[:, 512 * half:512 * half + 512], ps[4 + half][:, :], ACT.Copy).then_inc(y_hi_ready, 1)

            copy_xe(0)
            for n in range(4):
                round_piece(0, n)
            act_e.wait_ge(table_ready, 1)
            items = act_e.value_load(nitems_i[0:1, 0:1], min_val=NE, max_val=ITEMS - 1)
            with act_e.Fori(0, items) as i:
                A(sg[:, 0:1], konst_at(K_ONE, P, 1), ACT.Sigmoid).then_inc(table_loaded, 1)
                for s in range(1, 4):
                    for j in range(3):
                        round_piece(i, 3 * s + 1 + j)
                        if j == 1 and s > 1:
                            if s == 2:
                                act_e.wait_ge(table_loaded, i + 1)
                            sigmoid(i, s - 2)
                round_piece(i, 13)
                act_e.wait_ge(pt_ps, i + 1)
                A(onehotT, ps[6][:, :].rearrange("p (t c) -> p t c", t=4), ACT.Copy).then_inc(pt_ready, 1)
                sigmoid(i, 2)
                round_piece(i, 14)
                round_piece(i, 15)
                copy_actT(i, 0)
                sigmoid(i, 3)
                round_piece(i, 16)
                copy_xe(i + 1)
                copy_actT(i, 1)
                for n in range(17, 20):
                    round_piece(i, n)
                round_piece(i + 1, 0)
                copy_y(i, 0)
                for n in range(1, 4):
                    round_piece(i + 1, n)
                copy_y(i, 1)

        @block.vector
        def _(dve):
            V = nc.vector
            counts = {}

            def own(ins, signal=dve_step):
                counts[signal.num] = counts.get(signal.num, 0) + 1
                ins.then_inc(signal, 1)
                dve.wait_ge(signal, counts[signal.num])

            def bc(ap, shape):
                return ap.to_broadcast(shape)

            own(V.memset(small[:, :], 1.0), d_colw)
            own(V.memset(qkvT[:, :, 0:PAD], 0.0))
            dve.wait_ge(a_ssq, 5)
            own(V.tensor_scalar(rsA, ssqA, 1.0 / D, EPS, ALU.mult, ALU.add), d_stat)
            dve.wait_ge(konst_in, 16)
            dve.wait_ge(colw_T, 1)
            own(V.tensor_copy(colw[:, :], ps[7][:, 0:58]))
            dve.wait_ge(a_stat, 1)
            own(V.reciprocal(rsA, st1[:, 0:5]))
            for t in range(5):
                at, n = tok_cols[t]
                src = metax if t == 0 else h_t[t - 1]
                if t >= 2:
                    dve.wait_ge(u_T, 2 * (t - 1))
                own(V.tensor_scalar(utmp[t % 2][0:n, :], src, rsA[0:n, t:t + 1], None, ALU.mult), d_u)
                for half in range(2):
                    dve.wait_ge(u_T, 2 * t + half + 1)
                    own(V.tensor_tensor(uT[:, 4 * half:4 * half + 4, at:at + n],
                                    ps[2 * (t % 2) + half][:, :].rearrange("p (k c) -> p k c", k=4)[:, :, 0:n],
                                    bc(colw[:, 48 + 4 * half:52 + 4 * half].unsqueeze(2), [P, 4, n]), ALU.mult), u_evac)
            for m in range(12):
                dve.wait_ge(conv_evac, 2 * m + 2)
                own(V.tensor_scalar(conv_a[0], qkvT[:, m, 0:T], colw[:, m:m + 1], None, ALU.mult))
                for w in range(1, CW - 1):
                    own(V.scalar_tensor_tensor(out=conv_a[w % 2], in0=qkvT[:, m, w:w + T], scalar=colw[:, 12 * w + m:12 * w + m + 1],
                                               in1=conv_a[(w + 1) % 2], op0=ALU.mult, op1=ALU.add))
                w = CW - 1
                own(V.scalar_tensor_tensor(out=qkvT[:, m, PAD:], in0=qkvT[:, m, PAD:], scalar=colw[:, 12 * w + m:12 * w + m + 1],
                                       in1=conv_a[(w + 1) % 2], op0=ALU.mult, op1=ALU.add), d_conv)
            dve.wait_ge(gains_in, 16 * 7)
            dve.wait_ge(qk_ssq, 8)
            own(V.tensor_copy(rqk[0:META, 0, :], ps[7][0:META, 0:8]))
            for t in range(1, 5):
                own(V.tensor_copy(rqk[:, t, :], ps[7][:, 8 * t:8 * t + 8]))
            own(V.tensor_scalar(gcc, gcc, 1.0, None, ALU.mult), d_ssqc)
            for t in range(5):
                at, n = tok_cols[t]
                dve.wait_ge(a_proj, 2 * t + 1)
                if t:
                    own(V.tensor_reduce(st1[:, 0:8], sqC[:, 0:512].rearrange("p (a d) -> p a d", a=8), AX.X, ALU.add))
                    own(V.tensor_scalar(st1[:, 0:8], st1[:, 0:8], 1.0 / AD, EPS, ALU.mult, ALU.add))
                own(V.tensor_reduce(st1[0:n, 8:9], sqC[0:n, 512:768], AX.X, ALU.add))
                own(V.tensor_scalar(st1[0:n, 8:9], st1[0:n, 8:9], 1.0 / RANK, EPS, ALU.mult, ALU.add), d_stat)
                dve.wait_ge(a_stat, 2 + 2 * t)
                own(V.reciprocal(st3[0:n, 0:9], st2[0:n, 0:9]))
                own(V.tensor_scalar(ckv[0:n, :], ps[1][0:n, 0:256], st3[0:n, 8:9], None, ALU.mult), d_ckv)
                if t:
                    own(V.tensor_tensor(pre[:, 0:8, :], ps[0][:, :].rearrange("p (a d) -> p a d", a=8),
                                        bc(st3[:, 0:8].unsqueeze(2), [P, 8, AD]), ALU.mult))
                    own(V.tensor_tensor(pre[:, 0:8, :], pre[:, 0:8, :], bc(qn_w.unsqueeze(1), [P, 8, AD]), ALU.mult))
                dve.wait_ge(ckv_T, t + 1)
                own(V.tensor_scalar(ckvT[0][:, 0:n], ps[4][:, 0:n], colw[:, 56:57], None, ALU.mult))
                own(V.tensor_scalar(ckvT[1][:, 0:n], ps[4][:, P:P + n], colw[:, 57:58], None, ALU.mult), d_ckvT)
                dve.wait_ge(a_proj, 2 * t + 2)
                own(V.tensor_reduce(st1[0:n, 0:8], sqC[0:n, 0:512].rearrange("p (a d) -> p a d", a=8), AX.X, ALU.add))
                own(V.tensor_scalar(st1[0:n, 0:8], st1[0:n, 0:8], 1.0 / AD, EPS, ALU.mult, ALU.add), d_stat)
                dve.wait_ge(a_stat, 3 + 2 * t)
                own(V.reciprocal(st3[0:n, 0:8], st2[0:n, 0:8]))
                own(V.tensor_tensor(pre[0:n, 8:16, :], ps[5][0:n, :].rearrange("p (a d) -> p a d", a=8),
                                    bc(st3[0:n, 0:8].unsqueeze(2), [n, 8, AD]), ALU.mult))
                own(V.tensor_tensor(pre[0:n, 8:16, :], pre[0:n, 8:16, :], bc(kn_w[0:n].unsqueeze(1), [n, 8, AD]), ALU.mult))
                a, b = (8, 16) if t == 0 else (0, ROPE_H)
                cs = K_MCOS if t == 0 else K_COS + 32 * (t - 1)
                sn = K_MSIN if t == 0 else K_SIN + 32 * (t - 1)
                cosb = bc(kc[0:n, cs:cs + 32].unsqueeze(1), [n, b - a, 32])
                sinb = bc(kc[0:n, sn:sn + 32].unsqueeze(1), [n, b - a, 32])
                x1, x2 = pre[0:n, a:b, 0:32], pre[0:n, a:b, 32:64]
                y1, y2 = rp[0:n, a:b, 0:32], rp[0:n, a:b, 32:64]
                if t:
                    dve.wait_ge(rope_T, 4 * t)
                own(V.tensor_tensor(y1, x1, cosb, ALU.mult))
                own(V.tensor_tensor(y2, x2, cosb, ALU.mult))
                own(V.tensor_tensor(x2, x2, sinb, ALU.mult))
                own(V.tensor_tensor(x1, x1, sinb, ALU.mult))
                own(V.tensor_tensor(y1, y1, x2, ALU.subtract))
                own(V.tensor_tensor(y2, y2, x1, ALU.add))
                if t:
                    own(V.tensor_copy(rp[:, 25, :], rp[:, 24, :]))
                own(V.memset(mx8, 0.0), d_rope)
                dve.wait_ge(rope_T, 4 * t + 4)
                if t:
                    own(V.tensor_copy(qT[:, :, P * (t - 1):P * t], heads(ps[7][:, :])))
                    own(V.tensor_copy(kT[:, :, at:at + P], heads(ps[4][:, :])))
                    if t >= 2:
                        own(V.tensor_copy(qiT[:, :, P * (t - 2):P * (t - 1)], heads(ps[5][:, :])))
                    own(V.tensor_copy(kiT[:, P * (t - 1):P * t], ps[6][:, 0:P]))
                else:
                    own(V.tensor_copy(kT[:, :, 0:META], heads(ps[4][:, :])[:, :, 0:META]))
                own(V.memset(mx8, 0.0), d_ropeT)
            own(V.tensor_scalar(rqk[:, :, :], rqk[:, :, :], EPS, None, ALU.add), d_stat)
            y = st4.rearrange("p (t c) -> p t c", t=5)
            own(V.tensor_tensor(y, ba[:, :, 4:8], bc(dtb.unsqueeze(1), [P, 5, 4]), ALU.add))
            own(V.tensor_scalar(st2, st4, -1.0, None, ALU.mult))
            own(V.tensor_tensor(st1, st4, st2, ALU.max), d_stat)
            dve.wait_ge(a_stat, 12)
            own(V.reciprocal(rqk[:, :, :], rqk[:, :, :]))
            dve.wait_ge(a_stat, 13)
            own(V.scalar_tensor_tensor(out=st4, in0=st4, scalar=0.0, in1=st3, op0=ALU.max, op1=ALU.add))
            own(V.tensor_scalar(ea, ea, -1.0, None, ALU.mult))
            own(V.tensor_tensor(gg[:, :, :], y, bc(ea.unsqueeze(1), [P, 5, 4]), ALU.mult))
            lvs = 0
            for c in range(5):
                n = META if c == 0 else P
                rk = rqk[0:n, c, 4:8]
                own(V.tensor_copy(F_GB[0:n, :, :], bc(gg[0:n, c, :].unsqueeze(2), [n, 4, P])))
                own(V.tensor_copy(F_RK[0:n, :, 0:n], bc(rk.unsqueeze(2), [n, 4, n])), f_in)
                dve.wait_ge(f_ps, c + 1)
                R, KK, QK, Kt, Vt, RK, GC = (heads(ps[b][:, :]) for b in (0, 1, 2, 3, 4, 5, 6))
                own(V.tensor_copy(gcc[0:n, :], ps[6][0:n, 0:4]))
                for hh in range(BH):
                    own(V.tensor_scalar(F_DT[0:n, hh, 0:n], R[0:n, hh, 0:n], gcc[0:n, hh:hh + 1], 0.0, ALU.subtract, ALU.min))
                    own(V.tensor_scalar(F_DN[0:n, hh, 0:n], R[0:n, hh, 0:n], gcc[0:n, hh:hh + 1], 0.0, ALU.subtract, ALU.max))
                own(V.tensor_copy(el.unsqueeze(2), R[:, :, n - 1:n]), f_dd)
                own(V.tensor_tensor(br[0:n, :], beta[0:n, c, :], rk, ALU.mult))
                dve.wait_ge(f_exp, c + 1)
                own(V.scalar_tensor_tensor(out=ngk[0:n, :], in0=eg[0:n, :], scalar=-1.0, in1=br[0:n, :], op0=ALU.mult, op1=ALU.mult))
                own(V.tensor_tensor(F_DN[0:n, :, 0:n], KK[0:n, :, 0:n], F_DN[0:n, :, 0:n], ALU.mult))
                own(V.tensor_tensor(F_DN[0:n, :, 0:n], RK[0:n, :, 0:n], F_DN[0:n, :, 0:n], ALU.mult))
                for hh in range(BH):
                    own(V.scalar_tensor_tensor(out=F_A[0:n, hh, 0:n], in0=F_DN[0:n, hh, 0:n], scalar=br[0:n, hh:hh + 1],
                                               in1=konst_at(K_LS, n, n), op0=ALU.mult, op1=ALU.mult))
                own(V.tensor_tensor(F_Y[0:n, :, 0:n], F_A[0:n, :, 0:n], bc(konst_at(K_LV, n, n).unsqueeze(1), [n, 4, n]), ALU.mult))
                own(V.tensor_tensor(F_D[0:n, :, 0:n], bc(ident(n).unsqueeze(1), [n, 4, n]), F_Y[0:n, :, 0:n], ALU.subtract), f_A)
                own(V.tensor_tensor(st2[0:n, 0:4].unsqueeze(2), F_DT[0:n, :, n - 1:n], rk.unsqueeze(2), ALU.mult))
                own(V.tensor_tensor(F_KD[0:n, :, :], Kt[0:n, :, :], bc(st2[0:n, 0:4].unsqueeze(2), [n, 4, P]), ALU.mult))
                own(V.tensor_tensor(F_VB[0:n, :, :], Vt[0:n, :, :], bc(beta[0:n, c, :].unsqueeze(2), [n, 4, P]), ALU.mult))
                if c:
                    own(V.tensor_tensor(F_DT[:, :, :], QK[:, :, :], F_DT[:, :, :], ALU.mult))
                    for hh in range(BH):
                        own(V.scalar_tensor_tensor(out=F_IT[:, hh, :], in0=F_DT[:, hh, :], scalar=rk[:, hh:hh + 1],
                                                   in1=konst_at(K_UI), op0=ALU.mult, op1=ALU.mult))
                dve.wait_ge(f_lvps, lvs + 1)
                own(V.tensor_tensor(F_Dt[0:n, :, 0:n], bc(ident(n).unsqueeze(1), [n, 4, n]), heads(ps[7][:, :])[0:n, :, 0:n],
                                ALU.subtract), f_lv)
                lvs += 1
                for lv in range(1, 4 if c == 0 else LEVELS):
                    dve.wait_ge(f_lvps, lvs + 1)
                    own(V.tensor_copy(F_Y[0:n, :, 0:n], heads(ps[7][:, :])[0:n, :, 0:n]), f_lv)
                    dve.wait_ge(f_lvps, lvs + 2)
                    own(V.tensor_tensor(F_D[0:n, :, 0:n], F_D[0:n, :, 0:n], heads(ps[5][:, :])[0:n, :, 0:n], ALU.subtract))
                    own(V.tensor_tensor(F_Dt[0:n, :, 0:n], F_Dt[0:n, :, 0:n], heads(ps[6][:, :])[0:n, :, 0:n], ALU.subtract), f_lv)
                    lvs += 2
                if c == 0:
                    own(V.tensor_copy(F_R[0:n, :, :], F_VB[0:n, :, :]), f_r)
                else:
                    dve.wait_ge(f_ks, c)
                    for hh in range(BH):
                        own(V.scalar_tensor_tensor(out=F_R[:, hh, :], in0=heads(ps[0][:, :])[:, hh, :], scalar=ngk[:, hh:hh + 1],
                                                   in1=F_VB[:, hh, :], op0=ALU.mult, op1=ALU.add))
                    own(V.memset(mx8, 0.0), f_r)
                    dve.wait_ge(f_oc, c)
                    own(V.tensor_scalar(st2[:, 0:4], rqk[:, c, 0:4], float(BD ** -0.5), None, ALU.mult))
                    for hh in range(BH):
                        own(V.scalar_tensor_tensor(out=F_O[:, hh, :], in0=heads(ps[2][:, :])[:, hh, :], scalar=eg[:, hh:hh + 1],
                                                   in1=F_O[:, hh, :], op0=ALU.mult, op1=ALU.add))
                    o = oab[:, c - 1, AW:].rearrange("p (h c) -> p h c", h=4)
                    own(V.tensor_tensor(o, F_O[:, :, :], bc(st2[:, 0:4].unsqueeze(2), [P, 4, P]), ALU.mult))
                    own(V.tensor_tensor(F_O[:, :, :], o, o, ALU.mult))
                    own(V.tensor_reduce(ossq[:, 4 * (c - 1):4 * c], F_O[:, :, :], AX.X, ALU.add))
                dve.wait_ge(f_s, c + 1)
                if c == 0:
                    own(V.tensor_copy(F_S[:, :, :], heads(ps[4][:, :])), f_sc)
                else:
                    for hh in range(BH):
                        own(V.scalar_tensor_tensor(out=F_S[:, hh, :], in0=F_S[:, hh, :], scalar=el[:, hh:hh + 1],
                                                   in1=heads(ps[4][:, :])[:, hh, :], op0=ALU.mult, op1=ALU.add))
                    own(V.memset(mx8, 0.0), f_sc)
            own(V.tensor_scalar(ossq, ossq, 1.0 / BD, EPS, ALU.mult, ALU.add), d_stat)
            dve.wait_ge(a_stat, 14)
            own(V.reciprocal(orstd, orstd))
            for t in range(NT):
                o = oab[:, t, AW:].rearrange("p (h c) -> p h c", h=4)
                own(V.tensor_tensor(o, o, bc(orstd[:, 4 * t:4 * t + 4].unsqueeze(2), [P, 4, P]), ALU.mult))
                own(V.tensor_tensor(o, o, bc(dn_w.unsqueeze(1), [P, 4, P]), ALU.mult))
                own(V.tensor_tensor(o, o, zs[:, t, :].rearrange("p (h c) -> p h c", h=4), ALU.mult))
            q = 0
            for j in range(1, NT):
                w = P * (j + 1)
                row = isc[:, j - 1, 0:w]
                for hh in range(IH):
                    dve.wait_ge(i_rel, q + 1)
                    if hh == 0:
                        own(V.tensor_scalar(row, rel[q % 2][:, 0:w], wi[:, j, 0:1], None, ALU.mult), i_add)
                    else:
                        own(V.scalar_tensor_tensor(out=row, in0=rel[q % 2][:, 0:w], scalar=wi[:, j, hh:hh + 1], in1=row,
                                               op0=ALU.mult, op1=ALU.add), i_add)
                    dve.wait_ge(i_add, q + 1)
                    q += 1
                diag = isc[:, j - 1, P * j:w]
                own(V.tensor_tensor(diag, diag, konst_at(K_LI), ALU.mult))
                own(V.tensor_tensor(diag, diag, konst_at(K_LOW), ALU.add))
                for _ in range(TOPK // 8):
                    own(V.max(mx8, row))
                    own(V.match_replace(row, mx8, row, TAKEN))
                own(V.tensor_scalar(madd[:, j - 1, 0:w], row, TAKEN, HIDE, ALU.not_equal, ALU.mult))
            def normalize(j):
                dve.wait_ge(a_o, j + 1)
                own(V.tensor_tensor(oab[:, j, 0:AW].rearrange("p (a d) -> p a d", a=AH), ps[7][:, :].rearrange("p (a d) -> p a d", a=AH),
                                bc(qinv.unsqueeze(2), [P, AH, AD]), ALU.mult), a_on)

            for j in range(NT):
                w = META + P * (j + 1)
                for hh in range(AH):
                    q = AH * j + hh
                    pr = prob[q % 2]
                    dve.wait_ge(a_sc, q + 1)
                    own(V.tensor_scalar(pr[:, 0:META], ps[5 + q % 2][:, 0:META], AD ** -0.5, None, ALU.mult))
                    mask = konst_at(K_ADD) if j == 0 else madd[:, j - 1, 0:P * (j + 1)]
                    own(V.scalar_tensor_tensor(out=pr[:, META:w], in0=ps[q % 2][:, 0:P * (j + 1)], scalar=AD ** -0.5, in1=mask,
                                               op0=ALU.mult, op1=ALU.add))
                    own(V.tensor_reduce(mx8[:, 0:1], pr[:, 0:w], AX.X, ALU.max))
                    own(V.tensor_scalar(qmax[:, hh:hh + 1], mx8[:, 0:1], -1.0, None, ALU.mult), a_msk)
                    if j and hh == 0:
                        normalize(j - 1)
                dve.wait_ge(a_exp, AH * (j + 1))
                own(V.reciprocal(qinv, qsum))
            normalize(NT - 1)

            def add_mixer(t):
                for half in range(2):
                    dve.wait_ge(g_ps, 2 * t + half + 1)
                    hs = h[:, D * t + 512 * half:D * t + 512 * half + 512]
                    own(V.tensor_tensor(hs, hs, ps[2 + half][:, :], ALU.add))
                own(V.memset(mx8, 0.0), g_h)

            add_mixer(0)
            for t in range(NT):
                dve.wait_ge(a_ssq, 6 + t)
                own(V.tensor_scalar(st2[:, t:t + 1], st1[:, t:t + 1], 1.0 / D, EPS, ALU.mult, ALU.add), d_stat)
                dve.wait_ge(a_stat, 15 + t)
                own(V.reciprocal(st4[:, t:t + 1], st3[:, t:t + 1]))
                own(V.scalar_tensor_tensor(out=xraw, in0=h_t[t], scalar=st4[:, t:t + 1], in1=ffnw[:, :], op0=ALU.mult,
                                           op1=ALU.mult), g_xn)
                own(V.tensor_copy(piece(xn[0], t), xraw))
                own(V.tensor_tensor(x_rest[:, :], xraw, piece(xn[0], t), ALU.subtract))
                own(V.tensor_copy(piece(xn[1], t), x_rest[:, :]))
                own(V.tensor_tensor(piece(xn[2], t), x_rest[:, :], piece(xn[1], t), ALU.subtract))
                if t + 1 < NT:
                    add_mixer(t + 1)
                dve.wait_ge(g_lg, t + 1)
                own(V.tensor_tensor(lg[:, t, :], ps[6][:, 0:NE], br_w, ALU.add))
                own(V.max(mx8, lg[:, t, :]))
                own(V.max_index(eidx[:, 0:8], mx8, lg[:, t, :]))
                own(V.tensor_copy(qsum, eidx[:, 0:8]))
                own(V.tensor_scalar(selm[:, t, :], konst_at(K_IOTA, P, NE), qsum[:, 0:1], None, ALU.is_equal))
                for k in range(1, TOPE):
                    own(V.scalar_tensor_tensor(out=selm[:, t, :], in0=konst_at(K_IOTA, P, NE), scalar=qsum[:, k:k + 1],
                                               in1=selm[:, t, :], op0=ALU.is_equal, op1=ALU.add))
                own(V.tensor_scalar(lg[:, t, :], lg[:, t, :], mx8[:, 0:1], None, ALU.subtract))
                own(V.memset(mx8, 0.0), g_sel)
            gate3 = gate.rearrange("p (e t) -> p e t", t=NT)
            rank3 = rankm.rearrange("p (e t) -> p e t", t=NT)
            for t in range(NT):
                dve.wait_ge(a_stat, 19 + t)
                own(V.tensor_tensor(lg[:, t, :], lg[:, t, :], selm[:, t, :], ALU.mult))
                own(V.tensor_reduce(st1[:, t:t + 1], lg[:, t, :], AX.X, ALU.add))
                own(V.reciprocal(st2[:, t:t + 1], st1[:, t:t + 1]))
                own(V.tensor_scalar(gate3[:, :, t], lg[:, t, :], st2[:, t:t + 1], None, ALU.mult))
                own(V.tensor_copy(gtok, gate3[:, :, t]), g_gt)
                dve.wait_ge(g_rk, t + 1)
                own(V.tensor_scalar(tmpe, ps[7][:, 32 * t:32 * t + 32], 1.0, None, ALU.add))
                own(V.tensor_tensor(tmpe, tmpe, selm[:, t, :], ALU.mult))
                own(V.tensor_scalar(rank3[:, :, t], tmpe, -1.0, None, ALU.add))
                dve.wait_ge(g_gtc, t + 1)
                own(V.tensor_copy(gT, ps[0][0:NE, 0:P]))
                own(V.memset(mx8, 0.0), g_bd)
                for half in range(2):
                    dve.wait_ge(g_acc, 2 * t + half + 1)
                    hs = h[:, D * t + 512 * half:D * t + 512 * half + 512]
                    own(V.tensor_tensor(hs, hs, ps[1 + half][:, :], ALU.add))
            dve.wait_ge(g_rk, NT + 1)
            own(V.tensor_copy(cnt, ps[7][:, 128:160]))
            own(V.tensor_scalar(blocks, cnt, float(P), None, ALU.is_gt))
            for b in range(2, NT):
                own(V.scalar_tensor_tensor(out=blocks, in0=cnt, scalar=float(P * b), in1=blocks, op0=ALU.is_gt, op1=ALU.add))
            own(V.tensor_tensor_scan(cum, konst_at(K_ONE, P, NE), blocks, 0.0, ALU.mult, ALU.add))
            own(V.tensor_copy(etab[:, 0:NE], konst_at(K_IOTA, P, NE)))
            own(V.memset(shift[:, 0:NE], 0.0))
            over = [ITEMS - NE, NE]
            ended = xraw[:, 0:over[0] * NE].rearrange("p (i e) -> p i e", i=over[0])
            own(V.tensor_tensor(ended, bc(cum.unsqueeze(1), [P] + over), bc(konst_at(K_IOTA, P, over[0]).unsqueeze(2), [P] + over),
                                ALU.is_le))
            own(V.tensor_reduce(etab[:, NE:ITEMS], ended, AX.X, ALU.add))
            own(V.tensor_tensor(ended, ended, bc(blocks.unsqueeze(1), [P] + over), ALU.mult))
            own(V.tensor_reduce(shift[:, NE:ITEMS], ended, AX.X, ALU.add))
            own(V.scalar_tensor_tensor(out=shift[:, NE:ITEMS], in0=konst_at(K_IOTA, P, over[0]), scalar=1.0, in1=shift[:, NE:ITEMS],
                                       op0=ALU.add, op1=ALU.subtract))
            own(V.tensor_scalar(shift[:, NE:ITEMS], shift[:, NE:ITEMS], float(P), None, ALU.mult))
            own(V.tensor_scalar(etab, etab, float(NE - 1), None, ALU.min))
            own(V.tensor_copy(etab_i[:, :], etab))
            own(V.tensor_scalar(nitems_i[:, :], cum[:, NE - 1:NE], float(NE), None, ALU.add))
            own(V.tensor_copy(ident_b[:, :], ident()))
            dve.wait_ge(bias_in, 16 * 5)
            own(V.tensor_copy(bias2[:, :], bias_raw))
            for row in (1, 3):
                r = slice(NE * row, NE * row + NE)
                own(V.tensor_tensor(bias2[r, :], bias_raw[r, :], f32(bias2[r, :]), ALU.subtract))
            own(V.memset(f32(y_hi[:, :]), 0.0), y_ready)
            own(V.memset(f32(y_lo[:, :]), 0.0), y_ready)
            own(V.memset(gcol, 0.0), table_ready)
            items = dve.value_load(nitems_i[0:1, 0:1], min_val=NE, max_val=ITEMS - 1)

            def build_onehot(e, i):
                for t in range(NT):
                    V.tensor_scalar(onehot[:, t, :], konst_at(K_IOTA), shift[:, bass.ds(i, 1)], rankm[:, bass.ds(4 * e + t, 1)],
                                    ALU.add, ALU.is_equal)
                for half in range(2):
                    ins = V.tensor_copy(sel[half][:, :], kc[:, bass.ds(K_TWO + NE * half + e, 1)].to_broadcast([P, P]))
                ins.then_inc(p_built, 1)

            def split_piece(i, n):
                dve.wait_ge(w_hi_ready, PIECES * i + n + 1)
                V.tensor_tensor(w_lo[n % RING][:, :], raw_piece(n), f32(w_hi[n % RING][:, :]), ALU.subtract).then_inc(w_lo_ready, 1)

            def add_scattered(i, q):
                half, t = q // 4, q % 4
                dve.wait_ge(scat_ps, 8 * i + q + 1)
                hs = h[:, D * t + 512 * half:D * t + 512 * half + 512]
                V.scalar_tensor_tensor(out=hs, in0=ps[6 + q % 2][:, :], scalar=gcol[:, t:t + 1], in1=hs, op0=ALU.mult,
                                       op1=ALU.add).then_inc(acc_added, 1)

            def clamp(i, n):
                c = slice(256 * n, 256 * n + 256)
                gu = ps[n][:, :].rearrange("p (f two) -> p f two", two=2)
                dve.wait_ge(piece_used, PIECES * i + RING + 3 * n + 3)
                V.tensor_scalar(gm[:, c], gu[:, :, 0], LIMIT, None, ALU.min).then_inc(gm_ready, 1)
                V.tensor_scalar(act[:, c], gu[:, :, 1], LIMIT, -LIMIT, ALU.min, ALU.max).then_inc(loop_step, 1)
                dve.wait_ge(loop_step, 8 * i + 2 * n + 1)
                V.scalar_tensor_tensor(out=act[:, c], in0=act[:, c], scalar=1.0, in1=gm[:, c], op0=ALU.add, op1=ALU.mult)\
                    .then_inc(loop_step, 1)

            def times_sigmoid(i, n):
                c = slice(256 * n, 256 * n + 256)
                dve.wait_ge(loop_step, 8 * i + 2 * n + 2)
                dve.wait_ge(sg_ready, 4 * i + n + 1)
                V.tensor_tensor(act[:, c], act[:, c], sg[:, c], ALU.mult).then_inc(act_ready, 1)

            def low_xe(i):
                for half, c in ((0, slice(0, 256)), (1, slice(256, 768))):
                    dve.wait_ge(xe_hi_ready, 2 * i + half + 1)
                    V.tensor_tensor(xe_lo[:, c], ps[6 + half][:, 256 - 256 * half:512], f32(xe_hi[:, c]), ALU.subtract)\
                        .then_inc(xe_ready, 1)

            def low_actT(i, half):
                c = slice(512 * half, 512 * half + 512)
                dve.wait_ge(actT_hi_ready, 2 * i + half + 1)
                V.tensor_tensor(actT_lo[:, c], ps[half][:, :], f32(actT_hi[:, c]), ALU.subtract).then_inc(actT_ready, 1)

            def low_y(i, half):
                c = slice(512 * half, 512 * half + 512)
                dve.wait_ge(y_hi_ready, 2 * i + half + 1)
                V.tensor_tensor(y_lo[:, c], ps[4 + half][:, :], f32(y_hi[:, c]), ALU.subtract).then_inc(y_ready, 1)

            build_onehot(0, 0)
            dve.wait_ge(p_built, 1)
            low_xe(0)
            for n in range(4):
                split_piece(0, n)
            with dve.Fori(0, items) as i:
                e = dve.value_load(etab_i[0:1, bass.ds(i, 1)], min_val=0, max_val=NE - 1)
                e_next = dve.value_load(etab_i[0:1, bass.ds(i + 1, 1)], min_val=0, max_val=NE - 1)
                for s in range(1, 4):
                    for j in range(3):
                        split_piece(i, 3 * s + 1 + j)
                        if (s - 1, j) in SCATTER_AT:
                            add_scattered(i, SCATTER_AT.index((s - 1, j)))
                        if s > 1 and j == 0:
                            clamp(i, s - 2)
                        if s > 1 and j == 1:
                            times_sigmoid(i, s - 2)
                dve.wait_ge(acc_added, 8 * i + 8)
                V.tensor_copy(gcol, gate[:, bass.ds(4 * e, 4)])
                split_piece(i, 13)
                clamp(i, 2)
                dve.wait_ge(pt_ps, i + 1)
                dve.wait_ge(piece_used, PIECES * i + RING + 10)
                build_onehot(e_next, i + 1)
                dve.wait_ge(p_built, i + 2)
                split_piece(i, 14)
                times_sigmoid(i, 2)
                split_piece(i, 15)
                clamp(i, 3)
                low_actT(i, 0)
                split_piece(i, 16)
                times_sigmoid(i, 3)
                low_xe(i + 1)
                low_actT(i, 1)
                for n in range(17, 20):
                    split_piece(i, n)
                split_piece(i + 1, 0)
                low_y(i, 0)
                for n in range(1, 4):
                    split_piece(i + 1, n)
                low_y(i, 1)
            for q in range(2 * NT):
                add_scattered(items, q)

        @block.tensor
        def _(pe):
            M = nc.tensor.matmul
            TR = nc.tensor.transpose
            pe.wait_ge(konst_in, 16)
            pe.wait_ge(wrow_in, 16 * 6)
            TR(ps[7][:, 0:58], wrow, ident(58)).then_inc(colw_T, 1)
            for t in range(5):
                n = tok_cols[t][1]
                pe.wait_ge(d_u, t + 1)
                if t >= 2:
                    pe.wait_ge(u_evac, 2 * (t - 1))
                for k in range(KD):
                    i = TR(ps[2 * (t % 2) + k // 4][:, P * (k % 4):P * (k % 4) + n], utmp[t % 2][0:n, P * k:P * k + P], ident(n))
                    if k % 4 == 3:
                        i.then_inc(u_T, 1)
            pe.wait_ge(u_evac, 10)
            for m in range(12):
                s = m // 4
                pe.wait_ge(slot_in[s], 16)
                if m >= 2:
                    pe.wait_ge(conv_evac, 2 * (m - 1))
                for half in range(2):
                    for k in range(KD):
                        i = M(ps[4 + 2 * (m % 2) + half][:, 0:264], w_group(s)[:, k, P * (m % 4):P * (m % 4) + P],
                              uT[:, k, 264 * half:264 * half + 264], start=(k == 0), stop=(k == KD - 1))
                    i.then_inc(conv_ps, 1)
                if m % 4 == 3:
                    pe.wait_ge(conv_ps, 2 * m + 2)
                    pe.sem_inc(group_used, 1)
            pe.wait_ge(conv_evac, 24)
            for m in range(8):
                pe.wait_ge(conv_sq, m + 1)
                for t, (at, n) in enumerate(tok_cols):
                    i = M(ps[7][0:n, 8 * t + m:8 * t + m + 1], convsq[m % 2][:, at:at + n], konst_at(K_ONE)[:, 0:1], start=True, stop=True)
                i.then_inc(qk_ssq, 1)
            for s in (3, 4):
                pe.wait_ge(slot_in[s], 16)
            pe.wait_ge(slot_in[5], 32)
            pe.wait_ge(slot_in[0], 32)
            pe.wait_ge(wkv_in, 16)

            def project(t):
                at, n = tok_cols[t]
                if t:
                    pe.wait_ge(a_proj, 2 * t - 1)
                    pe.wait_ge(d_ckvT, t)
                for b, (w, c0, c1) in enumerate(((w_group(3), 0, 512), (w_group(4), 0, 512), (gC, 0, NPROJ), (w_group(0), 0, 512))):
                    if t == 0 and b in (0, 3):
                        pe.sem_inc(proj_ps, 1)
                        continue
                    if t == 0:
                        c0, c1 = (0, 256) if b == 1 else (328, 336)
                    for k in range(KD):
                        i = M(ps[b][0:n, c0:c1], uT[:, k, at:at + n], w[:, k, c0:c1], start=(k == 0), stop=(k == KD - 1))
                    i.then_inc(proj_ps, 1)

            project(0)
            for t, (at, n) in enumerate(tok_cols):
                pe.wait_ge(d_ckv, t + 1)
                if t:
                    pe.wait_ge(d_ropeT, t)
                for k in range(2):
                    i = TR(ps[4][:, P * k:P * k + n], ckv[0:n, P * k:P * k + P], ident(n))
                i.then_inc(ckv_T, 1)
                pe.wait_ge(d_ckvT, t + 1)
                for b in range(2):
                    for k in range(2):
                        i = M(ps[5 + b][0:n, :], ckvT[k][:, 0:n], wkv[:, k, 512 * b:512 * b + 512], start=(k == 0), stop=(k == 1))
                    i.then_inc(kv_ps, 1)
                if t < NT:
                    project(t + 1)
                pe.wait_ge(d_rope, t + 1)
                pe.wait_ge(a_proj, 2 * t + 2)
                if t == 0:
                    pe.wait_ge(d_ssqc, 1)
                for bank, a in ((7, 0), (4, 8), (5, 16), (6, 24)):
                    pairs = 1 if bank == 6 else 4
                    if t == 0 and bank != 4:
                        pe.sem_inc(rope_T, 1)
                        continue
                    for p in range(pairs):
                        src = rp[0:n, a + 2 * p:a + 2 * p + 2, :].rearrange("p a d -> p (a d)")
                        i = TR(ps[bank][:, P * p:P * p + n], src, ident(n))
                    i.then_inc(rope_T, 1)
            pe.wait_ge(rope_T, 20)
            pe.sem_inc(group_used, 1)
            pe.wait_ge(d_ropeT, 5)
            lvs, es = 0, 0
            for c, (at, n) in enumerate(tok_cols):
                cols = slice(PAD + at, PAD + at + n)
                pe.wait_ge(conv_silu, 12)
                pe.wait_ge(f_in, c + 1)
                if c:
                    pe.wait_ge(f_sc, c)
                for hh in range(BH):
                    q_, k_, v_ = qkvT[:, hh, cols], qkvT[:, 4 + hh, cols], qkvT[:, 8 + hh, cols]
                    hb = slice(P * hh, P * hh + n)
                    M(ps[0][:, hb], F_GB[0:n, hh, :], konst_at(K_UI, n, n), start=True, stop=True)
                    M(ps[1][0:n, hb], k_, k_, start=True, stop=True)
                    if c:
                        M(ps[2][0:n, hb], k_, q_, start=True, stop=True)
                    TR(ps[3][0:n, P * hh:P * hh + P], k_, ident())
                    TR(ps[4][0:n, P * hh:P * hh + P], v_, ident())
                    M(ps[5][0:n, hb], F_RK[0:n, hh, 0:n], ident(n), start=True, stop=True)
                M(ps[6][0:n, 0:4], konst_at(K_UI, n, n), gg[0:n, c, :], start=True, stop=True).then_inc(f_ps, 1)
                pe.wait_ge(f_A, c + 1)
                for hh in range(BH):
                    i = TR(ps[7][0:n, P * hh:P * hh + n], F_Y[0:n, hh, 0:n], ident(n))
                i.then_inc(f_lvps, 1)
                lvs += 1
                for lv in range(1, 4 if c == 0 else LEVELS):
                    pe.wait_ge(f_lv, lvs)
                    es += 1
                    pe.wait_ge(f_E, es)
                    for hh in range(BH):
                        i = M(ps[7][0:n, P * hh:P * hh + n], F_E[lv][0:n, hh, 0:n], F_Dt[0:n, hh, 0:n], start=True, stop=True)
                    i.then_inc(f_lvps, 1)
                    pe.wait_ge(f_lv, lvs + 1)
                    for hh in range(BH):
                        M(ps[5][0:n, P * hh:P * hh + n], F_Y[0:n, hh, 0:n], F_D[0:n, hh, 0:n], start=True, stop=True)
                        i = M(ps[6][0:n, P * hh:P * hh + n], F_D[0:n, hh, 0:n], F_Y[0:n, hh, 0:n], start=True, stop=True)
                    i.then_inc(f_lvps, 1)
                    lvs += 2
                pe.wait_ge(f_lv, lvs)
                if c:
                    for hh in range(BH):
                        i = M(ps[0][:, P * hh:P * hh + P], qkvT[:, 4 + hh, cols], F_S[:, hh, :], start=True, stop=True)
                    i.then_inc(f_ks, 1)
                pe.wait_ge(f_r, c + 1)
                for hh in range(BH):
                    i = M(ps[1][0:n, P * hh:P * hh + P], F_Dt[0:n, hh, 0:n], F_R[0:n, hh, :], start=True, stop=True)
                i.then_inc(f_vn, 1)
                if c:
                    for hh in range(BH):
                        M(ps[2][:, P * hh:P * hh + P], qkvT[:, hh, cols], F_S[:, hh, :], start=True, stop=True)
                pe.wait_ge(f_vnc, c + 1)
                if c:
                    for hh in range(BH):
                        i = M(ps[3][:, P * hh:P * hh + P], F_IT[:, hh, :], F_VN[:, hh, :], start=True, stop=True)
                    i.then_inc(f_o, 1)
                for hh in range(BH):
                    i = M(ps[4][:, P * hh:P * hh + P], F_KD[0:n, hh, :], F_VN[0:n, hh, :], start=True, stop=True)
                i.then_inc(f_s, 1)
            pe.wait_ge(f_sc, 5)
            q = 0
            for j in range(1, NT):
                for hh in range(IH):
                    rows = slice(64 * (hh % 2), 64 * (hh % 2) + 64)
                    if q >= 2:
                        pe.wait_ge(i_rel, q - 1)
                    M(ps[q % 2][:, 0:P * (j + 1)], qiT[rows, hh // 2, P * (j - 1):P * j], kiT[rows, 0:P * (j + 1)],
                      start=True, stop=True).then_inc(i_ps, 1)
                    q += 1
            pe.wait_ge(i_rel, q)

            def attn_scores(q):
                j, hh = q // AH, q % AH
                rows = slice(64 * (hh % 2), 64 * (hh % 2) + 64)
                if q >= 2:
                    pe.wait_ge(a_pT, q - 1)
                lhs = qT[rows, hh // 2, P * j:P * j + P]
                M(ps[5 + q % 2][:, 0:META], lhs, kT[rows, hh // 2, 0:META], start=True, stop=True)
                M(ps[q % 2][:, 0:P * (j + 1)], lhs, kT[rows, hh // 2, META:META + P * (j + 1)], start=True, stop=True)\
                    .then_inc(a_sc, 1)

            def attn_transposes(q):
                pe.wait_ge(a_exp, q + 1)
                for b in range(q // AH + 1):
                    TR(ps[2 + q % 2][:, P * b:P * b + P], prob[q % 2][:, META + P * b:META + P * b + P], ident())
                if q:
                    pe.wait_ge(a_pTc, q)
                TR(ps[4][0:META, 0:P], prob[q % 2][:, 0:META], ident()).then_inc(a_pT, 1)

            def attn_outputs(q):
                j, hh = q // AH, q % AH
                pe.wait_ge(a_pTc, q + 1)
                if hh == 0 and j:
                    pe.wait_ge(a_on, j)
                o = ps[7][:, AD * hh:AD * hh + AD]
                for b in range(j + 1):
                    M(o, pT[q % 2][:, P * b:P * b + P], vA[:, b, AD * hh:AD * hh + AD], start=(b == 0), stop=False)
                i = M(o, pT[q % 2][0:META, 512:640], vM[:, AD * hh:AD * hh + AD], start=False, stop=True)
                if hh == AH - 1:
                    i.then_inc(a_o, 1)

            attn_scores(0)
            for q in range(NT * AH):
                if q + 1 < NT * AH:
                    attn_scores(q + 1)
                attn_transposes(q)
                if q:
                    attn_outputs(q - 1)
            attn_outputs(NT * AH - 1)
            pe.wait_ge(a_on, NT)
            pe.wait_ge(slot_in[4], 32)
            pe.wait_ge(slot_in[5], 48)
            pe.wait_ge(wr_in, 16)

            def project_out(t):
                for k in range(KD):
                    if t and k % 4 == 0:
                        pe.wait_ge(g_Tc, 2 * (t - 1) + k // 4 + 1)
                    i = TR(ps[k // 4][:, P * (k % 4):P * (k % 4) + P], oab[:, t, P * k:P * k + P], ident())
                    if k % 4 == 3:
                        i.then_inc(g_T, 1)
                pe.wait_ge(g_Tc, 2 * t + 2)
                if t:
                    pe.wait_ge(g_h, t)
                for half in range(2):
                    for k in range(KD):
                        i = M(ps[2 + half][:, :], oT[:, k, :], w_group(4 + half)[:, k, :], start=(k == 0), stop=(k == KD - 1))
                    i.then_inc(g_ps, 1)

            project_out(0)
            for t in range(NT):
                if t + 1 < NT:
                    project_out(t + 1)
                pe.wait_ge(g_xn, t + 1)
                for k in range(KD):
                    i = TR(ps[4 + k // 4][:, P * (k % 4):P * (k % 4) + P], xraw[:, P * k:P * k + P], ident())
                    if k % 4 == 3:
                        i.then_inc(g_xT, 1)
                pe.wait_ge(g_xTc, 2 * t + 2)
                if t:
                    pe.wait_ge(g_sel, t)
                for k in range(KD):
                    i = M(ps[6][:, 0:NE], xT[:, k, :], wr[:, k, :], start=(k == 0), stop=(k == KD - 1))
                i.then_inc(g_lg, 1)
            pe.wait_ge(g_sel, NT)
            for t in range(NT + 1):
                o = ps[7][:, 32 * t:32 * t + 32]
                for s in range(min(t, NT)):
                    i = M(o, konst_at(K_ONE), selm[:, s, :], start=(s == 0), stop=(t == NT and s == NT - 1))
                if t < NT:
                    i = M(o, konst_at(K_US), selm[:, t, :], start=(t == 0), stop=True)
            i.then_inc(g_rk, NT + 1)
            pe.wait_ge(bias_in, 16 * 5)
            for t in range(NT):
                pe.wait_ge(g_gt, t + 1)
                if t:
                    pe.wait_ge(g_bd, t)
                TR(ps[0][0:NE, 0:P], gtok, ident()).then_inc(g_gtc, 1)
                pe.wait_ge(g_bd, t + 1)
                for half in range(2):
                    M(ps[1 + half][:, :], gT, bdn[:, 512 * half:512 * half + 512], start=True, stop=True).then_inc(g_acc, 1)
            pe.sem_inc(g_rk, 1)

            def gather(i):
                pe.wait_ge(p_built, i + 1)
                for k in range(KD):
                    for t in range(NT):
                        for b, part in enumerate(xn):
                            ins = M(ps[6 + k // 4][:, P * (k % 4):P * (k % 4) + P], part[:, D * t + P * k:D * t + P * k + P],
                                    onehot[:, t, :], start=(t == 0 and b == 0), stop=(t == NT - 1 and b == 2))
                    if k % 4 == 3:
                        ins.then_inc(x_ps, 1)

            def scatter(i, q):
                half, t = q // 4, q % 4
                if q == 0:
                    pe.wait_ge(pt_ready, i + 1)
                if t == 0:
                    pe.wait_ge(y_ready, 2 * i + half + 1)
                if q >= 2:
                    pe.wait_ge(acc_added, 8 * i + q - 1)
                c = slice(512 * half, 512 * half + 512)
                M(ps[6 + q % 2][:, :], onehotT[:, t, :], y_hi[:, c], start=True, stop=False)
                M(ps[6 + q % 2][:, :], onehotT[:, t, :], y_lo[:, c], start=False, stop=True).then_inc(scat_ps, 1)

            def products(i, n, k0, bank, hi, lo):
                pe.wait_ge(w_lo_ready, PIECES * i + n + 1)
                for k in (k0, k0 + 1):
                    kk = slice(P * k, P * k + P)
                    wh, wl = (t[n % RING][:, 512 * (k - k0):512 * (k - k0) + 512] for t in (w_hi, w_lo))
                    last = n + 1 in FIRST or n == PIECES - 1
                    M(ps[bank][:, :], hi[:, kk], wh, start=(n in FIRST[4:] and k == 0), stop=False)
                    M(ps[bank][:, :], hi[:, kk], wl, start=False, stop=False)
                    ins = M(ps[bank][:, :], lo[:, kk], wh, start=False, stop=(last and k > k0))
                ins.then_inc(piece_used, 1)

            def gate_up_bias(n):
                M(ps[n][:, :], sel[n // 2][:, :], bias2[:, 512 * (n % 2):512 * (n % 2) + 512], start=True, stop=False)

            pe.sem_inc(piece_used, RING)
            gather(0)
            pe.wait_ge(table_ready, 1)
            items = pe.value_load(nitems_i[0:1, 0:1], min_val=NE, max_val=ITEMS - 1)
            with pe.Fori(0, items) as i:
                pe.wait_ge(xe_whole_ready, i + 1)
                pe.wait_ge(xe_ready, 2 * i + 2)
                for n in range(4):
                    gate_up_bias(n)
                    for j in range(3):
                        if j == 1:
                            pe.wait_ge(w_lo_ready, PIECES * i + 3 * n + 3)
                            for k in range(2):
                                ins = M(ps[n][:, :], xe[:, P * k:P * k + P], slot(n % 3, 512, 512 * k), start=False, stop=False)
                            ins.then_inc(plain_used, 1)
                        products(i, 3 * n + j, 2 * j, n, xe_hi, xe_lo)
                        if (n, j) in SCATTER_AT:
                            scatter(i, SCATTER_AT.index((n, j)))
                        if n == 3 and j == 1:
                            pe.wait_ge(act_ready, 4 * i + 2)
                            for k in range(4):
                                ins = TR(ps[0][:, P * k:P * k + P], act[:, P * k:P * k + P], ident())
                            ins.then_inc(actT_ps, 1)
                    if n == 2:
                        pe.wait_ge(acc_added, 8 * i + 8)
                        for t in range(NT):
                            ins = M(ps[6][:, P * t:P * t + P], onehot[:, t, :], ident_b[:, :], start=True, stop=True)
                        ins.then_inc(pt_ps, 1)
                pe.wait_ge(pt_ready, i + 2)
                gather(i + 1)
                pe.wait_ge(act_ready, 4 * i + 4)
                for k in range(4, KD):
                    ins = TR(ps[1][:, P * (k - 4):P * (k - 4) + P], act[:, P * k:P * k + P], ident())
                ins.then_inc(actT_ps, 1)
                for half in range(2):
                    for j in range(4):
                        if half == 0 and j % 2 == 0:
                            pe.wait_ge(actT_ready, 2 * i + j // 2 + 1)
                        products(i, 12 + 4 * half + j, 2 * j, 4 + half, actT_hi, actT_lo)
            for q in range(2 * NT):
                scatter(items, q)


_INS = ['x', 'meta_tokens', 'norm_mix_w', 'w_in', 'q_norm_w', 'k_norm_w', 'kv_norm_w', 'w_kv_up', 'conv_w', 'a_log',
        'dt_bias', 'delta_norm_w', 'w_out', 'norm_ffn_w', 'w_router', 'b_router', 'w_gate_up', 'b_gate_up', 'w_down', 'b_down']


def kernel(**inputs):
    import numpy as _np
    import concourse.bacc as _bacc
    from concourse import mybir as _mybir
    from concourse.bass_utils import run_bass_kernel_spmd as _run

    nc = _bacc.Bacc("TRN2", target_bir_lowering=False, num_devices=1)
    arrays = {"in_konst": constants()}
    args = [nc.dram_tensor("in_konst", (P, KONST), F32, kind="ExternalInput").ap()]
    for name in _INS:
        a = _np.ascontiguousarray(inputs[name])
        arrays[f"in_{name}"] = a
        args.append(nc.dram_tensor(f"in_{name}", a.shape, _mybir.dt.from_np(a.dtype), kind="ExternalInput").ap())
    args.append(nc.dram_tensor("out_0", (1, SEQ, D), F32, kind="ExternalOutput").ap())
    hybrid_layer(nc, *args)
    r = _run(nc, [arrays], core_ids=[0])
    return r.results[0]["out_0"]
```

```python
from contextlib import ExitStack

import concourse.bass as bass
import numpy as np
from concourse import mybir

ALU = mybir.AluOpType
ACT = mybir.ActivationFunctionType
AX = mybir.AxisListType
F32 = mybir.dt.float32
I32 = mybir.dt.int32
U32 = mybir.dt.uint32
F32R = mybir.dt.float32r
BF16 = mybir.dt.bfloat16
RING = 5
SCATTER_AT = ((0, 0), (0, 1), (0, 2), (1, 0), (1, 1), (1, 2), (2, 0), (2, 1))
BDOWN = (1, 2, 3, 4, 5, 0, 1, 2)
PIECES = 20
FIRST = (0, 3, 6, 9, 12, 16)

P = 128
D = 1024
KD = D // P
SEQ = 512
NT = SEQ // P
META = 16
T = META + SEQ
AH, AD = 8, 64
AW = AH * AD
RANK = 256
IH = 8
TOPK = 128
BH, BD = 4, 128
CW = 4
PAD = CW - 1
NE = 32
TOPE = 4
EPS = 1e-6
LIMIT = 7.0
ALPHA = 1.702
ITEMS = 48
C_BQKV, C_Z, C_BETA = 1352, 2888, 3400
NPROJ = 336
LOW = -1.0e38
TAKEN = -3.0e38
HIDE = -1.0e30
LEVELS = 7
ROPE_H = 25

K_ID = 0
K_UI = K_ID + P
K_US = K_UI + P
K_LS = K_US + P
K_ONE = K_LS + P
K_LV = K_ONE + P
K_IOTA = K_LV + LEVELS * P
K_ADD = K_IOTA + P
K_LOW = K_ADD + P
K_LI = K_LOW + P
K_TWO = K_LI + P
K_COS = K_TWO + 2 * 32
K_SIN = K_COS + NT * 32
K_MCOS = K_SIN + NT * 32
K_MSIN = K_MCOS + 32
KONST = K_MSIN + 32


def constants():
    k = np.zeros((P, KONST), np.float32)
    r, c = np.meshgrid(np.arange(P), np.arange(P), indexing="ij")
    k[:, K_ID:K_ID + P] = r == c
    k[:, K_UI:K_UI + P] = r <= c
    k[:, K_US:K_US + P] = r < c
    k[:, K_LS:K_LS + P] = r > c
    k[:, K_ONE:K_ONE + P] = 1
    for lv in range(LEVELS):
        at = K_LV + lv * P
        k[:, at:at + P] = (r > c) & (r >> (lv + 1) == c >> (lv + 1)) & (r >> lv != c >> lv)
    k[:, K_IOTA:K_IOTA + P] = c
    k[:, K_ADD:K_ADD + P] = np.where(c <= r, 0, HIDE)
    k[:, K_LOW:K_LOW + P] = np.where(c <= r, 0, LOW)
    k[:, K_LI:K_LI + P] = c <= r
    for half in range(2):
        k[:, K_TWO + NE * half:K_TWO + NE * half + NE] = (r - 64 * half == c)[:, :NE] | (r - 64 * half - NE == c)[:, :NE]
    inv = np.float32(10000.0) ** (-np.arange(0, AD, 2, dtype=np.float32) / np.float32(AD))
    ang = np.arange(T, dtype=np.float32)[:, None] * inv[None, :]
    cos, sin = np.cos(ang).astype(np.float32), np.sin(ang).astype(np.float32)
    for t in range(NT):
        rows = slice(META + P * t, META + P * t + P)
        k[:, K_COS + 32 * t:K_COS + 32 * t + 32] = cos[rows]
        k[:, K_SIN + 32 * t:K_SIN + 32 * t + 32] = sin[rows]
    k[:META, K_MCOS:K_MCOS + 32] = cos[:META]
    k[:META, K_MSIN:K_MSIN + 32] = sin[:META]
    return k


def hybrid_layer(nc, konst, x, meta_tokens, norm_mix_w, w_in, q_norm_w, k_norm_w, kv_norm_w, w_kv_up, conv_w,
                 a_log, dt_bias, delta_norm_w, w_out, norm_ffn_w, w_router, b_router, w_gate_up, b_gate_up,
                 w_down, b_down, out):
    with ExitStack() as ctx:
        def sb(name, cols, dt=F32):
            return ctx.enter_context(nc.sbuf_tensor(name, [P, cols], dt))

        def sem(name):
            return ctx.enter_context(nc.semaphore(name))

        ps = [ctx.enter_context(nc.psum_tensor(f"bank{i}", [P, 512], F32)) for i in range(8)]

        h = sb("h", NT * D)
        kc = sb("kc", KONST)
        ffnw = sb("ffnw", D)
        gains = sb("gains", 64 + 64 + BD + NE + 2 * BH)
        colw = sb("colw", 58)
        small = sb("small", 900)
        N_RING, N_R1, N_R2, N_R3 = 6 * 4096, KD * T, 12 * (T + PAD), 8768
        AT_R1, AT_R2, AT_R3 = N_RING, N_RING + N_R1, N_RING + N_R1 + N_R2 + 4
        arena_tensor = sb("arena", AT_R3 + N_R3)
        arena = nc.lookup_mloc(arena_tensor).addr

        def place(name, where, cols, dt=F32):
            return nc.alloc_sbuf_tensor_at(name, [P, cols], dt, offset=arena + 4 * where)

        ring = place("ring", 0, N_RING)
        r1 = place("r1", AT_R1, N_R1)
        r2 = place("r2", AT_R2, N_R2)
        r3 = place("r3", AT_R3, N_R3)
        xn = [place("xn_b0", 3 * 4096, 4096, BF16), place("xn_b1", 3 * 4096 + 2048, 4096, BF16),
              place("xn_b2", AT_R2, 4096, BF16)]
        w_hi = [place(f"w_hi{b}", 4 * 4096 + 1024 * b if b < 4 else AT_R2 + 2048, 1024, F32R) for b in range(RING)]
        w_lo = [place(f"w_lo{b}", 5 * 4096 + 1024 * b if b < 4 else AT_R2 + 3072, 1024, F32R) for b in range(RING)]
        xe = place("xe", AT_R1 + 3072, 256)
        xe_hi = place("xe_hi", AT_R1 + 3328, 768, F32R)
        x_rest = place("x_rest", AT_R2 + 2048, 1024)
        xe_lo = place("xe_lo", AT_R2 + 5120, 768, F32R)
        actT_hi, actT_lo = place("actT_hi", AT_R3, 1024, F32R), place("actT_lo", AT_R3 + 1024, 1024, F32R)
        y_hi, y_lo = place("y_hi", AT_R3 + 2304, 1024, F32R), place("y_lo", AT_R3 + 3328, 1024, F32R)
        sel = [place("sel0", AT_R1 + 4096, P, F32R), place("sel1", AT_R3 + 6400, P, F32R)]
        onehot_t, onehotT_t = place("onehot", AT_R3 + 6528, 512, BF16), place("onehotT", AT_R3 + 7040, 512, F32R)
        bias2 = place("bias2", AT_R3 + 7552, 1024, F32R)

        def slot(s, n=4096, at=0):
            return ring[:, 4096 * s + at:4096 * s + at + n]

        def konst_at(at, rows=P, n=P):
            return kc[0:rows, at:at + n]

        def ident(n=P):
            return kc[0:n, K_ID:K_ID + n]

        h_t = [h[:, D * t:D * t + D] for t in range(NT)]
        qn_w, kn_w = gains[:, 0:64], gains[:, 64:128]
        dn_w = gains[:, 128:256]
        br_w = gains[:, 256:288]
        alog, dtb = gains[:, 288:292], gains[:, 292:296]
        uT = r1[:, :].rearrange("p (k t) -> p k t", k=KD)
        oab = r1[:, 0:NT * D].rearrange("p (t d) -> p t d", t=NT)
        qkvT = r2[:, :].rearrange("p (m t) -> p m t", m=12)
        qT = r3[:, 0:2048].rearrange("p (a t) -> p a t", a=4)
        kT = r3[:, 2048:4160].rearrange("p (a t) -> p a t", a=4)
        vA = r3[:, 4160:6208].rearrange("p (t d) -> p t d", t=NT)
        vM = r3[0:META, 6208:6720]
        qiT = r3[:, 6720:8256].rearrange("p (a t) -> p a t", a=4)
        kiT = r3[:, 8256:8768]
        utmp = [r3[:, 0:1024], r3[:, 1024:2048]]
        metax = r3[0:META, 2048:3072]
        conv_a = [r3[:, 3072:3600], r3[:, 3600:4128]]
        wrow = r3[0:58, 4128:4256]
        sq = r3[:, 5056:6080]
        convsq = [r3[:, 6080:6608], r3[:, 6608:7136]]
        zs = slot(2, 2048).rearrange("p (t d) -> p t d", t=NT)
        rp = slot(2, 1664, 2048).rearrange("p (a d) -> p a d", a=26)
        pre = slot(1, 1600, 2048).rearrange("p (a d) -> p a d", a=ROPE_H)
        sqC = slot(5, 768, KD * NPROJ)
        ckv = slot(5, 256, KD * NPROJ + 768)
        square_out = r2[:, 5120:6144]
        sm_at = [0]

        def sm(n):
            sm_at[0] += n
            return small[:, sm_at[0] - n:sm_at[0]]

        ssqA, rsA = sm(5), sm(5)
        ba = sm(5 * 8).rearrange("p (t c) -> p t c", t=5)
        beta = sm(20).rearrange("p (t c) -> p t c", t=5)
        gg = sm(20).rearrange("p (t c) -> p t c", t=5)
        rqk = sm(40).rearrange("p (t c) -> p t c", t=5)
        wi = sm(NT * 8).rearrange("p (t c) -> p t c", t=NT)
        st1, st2, st3, st4 = sm(20), sm(20), sm(20), sm(20)
        ea = sm(4)
        ckvT = [sm(P), sm(P)]
        gcc, br = sm(4), sm(4)
        eg, el, ngk = [sm(4), sm(4)], [sm(4), sm(4)], [sm(4), sm(4)]
        mx8, top8 = sm(8), sm(8)
        qmax, qsum, qinv = sm(8), sm(8), sm(8)
        qsums = [sm(8), sm(8)]
        ossq, orstd = sm(16), sm(16)

        konst_in, x_in, gains_in, wrow_in = sem("konst_in"), [sem(f"x_in{i}") for i in range(5)], sem("gains_in"), sem("wrow_in")
        slot_in = [sem(f"slot_in{s}") for s in range(6)]
        wkv_in, wr_in, bias_in = sem("wkv_in"), sem("wr_in"), sem("bias_in")
        colw_T, u_T, u_evac = sem("colw_T"), sem("u_T"), sem("u_evac")
        conv_ps, conv_evac, conv_silu, conv_sq, qk_ssq = (sem("conv_ps"), sem("conv_evac"), sem("conv_silu"),
                                                          sem("conv_sq"), sem("qk_ssq"))
        group_used = sem("group_used")
        proj_ps, ckv_T, kv_ps, rope_T = sem("proj_ps"), sem("ckv_T"), sem("kv_ps"), sem("rope_T")
        act_step = sem("act_step")
        dve_step = sem("dve_step")
        d_u, d_colw, d_conv, d_ckv, d_ckvT, d_rope, d_ropeT = (sem("d_u"), sem("d_colw"), sem("d_conv"), sem("d_ckv"),
                                                               sem("d_ckvT"), sem("d_rope"), sem("d_ropeT"))
        d_ssqc = sem("d_ssqc")
        d_stat, a_stat, a_proj, a_ssq = sem("d_stat"), sem("a_stat"), sem("a_proj"), sem("a_ssq")
        f_in, f_ps, f_dd, f_exp, f_A, f_E, f_lv, f_lvps = (sem("f_in"), sem("f_ps"), sem("f_dd"), sem("f_exp"),
                                                           sem("f_A"), sem("f_E"), sem("f_lv"), sem("f_lvps"))
        f_init, f_rest_ps, f_rest, f_Y = sem("f_init"), sem("f_rest_ps"), sem("f_rest"), sem("f_Y")
        f_ks, f_r, f_vn, f_vnc, f_o, f_oc, f_s, f_sc = (sem("f_ks"), sem("f_r"), sem("f_vn"), sem("f_vnc"), sem("f_o"),
                                                        sem("f_oc"), sem("f_s"), sem("f_sc"))
        i_ps, i_rel, i_add = sem("i_ps"), sem("i_rel"), sem("i_add")
        a_sc, a_msk, a_exp, a_pT, a_pTc, a_o, a_on = (sem("a_sc"), sem("a_msk"), sem("a_exp"), sem("a_pT"), sem("a_pTc"),
                                                      sem("a_o"), sem("a_on"))
        g_T, g_Tc, g_ps, g_h, g_xn, g_xT, g_xTc, g_lg, g_sel, g_rk, g_gt, g_gtc, g_bd, g_acc = (
            sem("g_T"), sem("g_Tc"), sem("g_ps"), sem("g_h"), sem("g_xn"), sem("g_xT"), sem("g_xTc"), sem("g_lg"),
            sem("g_sel"), sem("g_rk"), sem("g_gt"), sem("g_gtc"), sem("g_bd"), sem("g_acc"))
        table_ready = sem("table_ready")
        p_built, x_ps, xe_ready, gm_ready, sg_ready, act_ready = (
            sem("p_built"), sem("x_ps"), sem("xe_ready"), sem("gm_ready"), sem("sg_ready"), sem("act_ready"))
        pt_ps, pt_ready, actT_ps, actT_ready, y_ready, scat_ps, acc_added, loop_step = (
            sem("pt_ps"), sem("pt_ready"), sem("actT_ps"), sem("actT_ready"), sem("y_ready"),
            sem("scat_ps"), sem("acc_added"), sem("loop_step"))
        out_done = sem("out_done")
        raw_in = [sem(f"raw_in{r}") for r in range(3)]
        w_hi_ready, w_lo_ready, piece_used = sem("w_hi_ready"), sem("w_lo_ready"), sem("piece_used")
        plain_used = sem("plain_used")
        actT_hi_ready, y_hi_ready, xe_hi_ready = sem("actT_hi_ready"), sem("y_hi_ready"), sem("xe_hi_ready")
        xe_whole_ready, table_loaded = sem("xe_whole_ready"), sem("table_loaded")

        fs = [slot(s, 512, 512 * i) for s in (0, 1, 3) for i in range(8)]

        def heads(ap):
            return ap.rearrange("p (h c) -> p h c", h=4)

        def chunk_len(c):
            return META if c == 0 else P

        def levels(c):
            return range(1, 4 if c == 0 else LEVELS)

        def lv_count(c):
            return sum(1 + 2 * len(levels(b)) for b in range(c))

        F_GB, F_RK, F_DN, F_DT, F_A, F_D, F_Y, F_S, F_R, F_VN = [heads(a) for a in fs[0:10]]
        F_O = heads(slot(2, 512, 3584))
        F_KD, F_VB, F_IT, F_Dt = [[heads(a) for a in fs[at:at + 2]] for at in (10, 12, 14, 16)]
        F_E = [None] + [heads(a) for a in fs[18:24]]
        isc = slot(2, 1536, 2048).rearrange("p (t c) -> p t c", t=3)
        rel = [slot(0, 512, 1536), slot(0, 512, 2048)]
        prob = [slot(3, T, T * b) for b in range(3)]
        pT = [slot(3, 640, 3 * T), slot(3, 640, 3 * T + 640)]
        oT = r3[:, 0:1024].rearrange("p (k c) -> p k c", k=KD)
        xT = r3[:, 1024:2048].rearrange("p (k c) -> p k c", k=KD)
        wr = r3[:, 2048:2304].rearrange("p (k e) -> p k e", k=KD)
        bias_raw = r3[:, 2304:3328]
        bdn = r3[0:NE, 4352:5376]
        lg = r3[:, 5376:5504].rearrange("p (t e) -> p t e", t=NT)
        selm = r3[:, 5504:5632].rearrange("p (t e) -> p t e", t=NT)
        gate = r3[:, 5632:5760]
        rankm = r3[:, 5760:5888]
        tok_rank = r3[:, 5888:6016].rearrange("p (t e) -> p t e", t=NT)
        etab = r3[:, 6048:6048 + ITEMS]
        shift = r3[:, 6112:6112 + ITEMS]
        cnt, blocks, cum = r3[:, 6176:6208], r3[:, 6208:6240], r3[:, 6240:6272]
        gcol = r3[:, 6304:6308]
        onehot = onehot_t[:, :].rearrange("p (t c) -> p t c", t=NT)
        ident_b = place("ident_b", AT_R3 + 6784, P, BF16)
        onehotT = onehotT_t[:, :].rearrange("p (t c) -> p t c", t=NT)
        xraw = r2[:, 4096:5120]
        gT = r2[0:NE, 4608:5120]
        gm, sg, act = r1[:, 0:1024], r1[:, 1024:2048], r1[:, 2048:3072]

        def f32(ap):
            return ap.bitcast(F32)

        def raw_piece(n):
            s, j = (n // 3, 1 + n % 3) if n < 12 else (n // 4 + 1, n % 4)
            return piece(slot(s % 3), j)

        def piece(t, j):
            return t[:, 1024 * j:1024 * j + 1024]

        eidx = ctx.enter_context(nc.sbuf_tensor("eidx", [P, 8 + 1], U32))
        etab_i = ctx.enter_context(nc.sbuf_tensor("etab_i", [P, ITEMS], I32))
        nitems_i = ctx.enter_context(nc.sbuf_tensor("nitems_i", [P, 1], I32))

        w_in0 = w_in[0].rearrange("(k p) n -> p k n", p=P)
        tok_cols = [(0, META)] + [(META + P * t, P) for t in range(NT)]

        def w_group(s, n=512):
            return slot(s, KD * n).rearrange("p (k n) -> p k n", k=KD)

        gC = w_group(5, NPROJ)
        wkv = slot(1, 2048).rearrange("p (k n) -> p k n", k=2)

        def expert_chunk(e, s):
            if s < 4:
                return w_gate_up[0, bass.ds(e, 1)].rearrange("o (k p) n -> p (o k) n", p=P)[:, :, 512 * s:512 * s + 512]
            return w_down[0, bass.ds(e, 1)].rearrange("o (k p) n -> p (o k) n", p=P)[:, :, 512 * (s - 4):512 * (s - 4) + 512]

        block = ctx.enter_context(nc.Block())

        @block.sync
        def _(sp):
            sp.dma_start(metax, meta_tokens).then_inc(x_in[0], 16)
            for t in range(NT):
                sp.dma_start(h_t[t], x[0, P * t:P * t + P, :]).then_inc(x_in[t + 1], 16)
            sp.dma_start(kc[:, :], konst).then_inc(konst_in, 16)
            for s in range(3):
                sp.dma_start(w_group(s), w_in0[:, :, C_BQKV + 512 * s:C_BQKV + 512 * s + 512]).then_inc(slot_in[s], 16)
            sp.dma_start(w_group(3), w_in0[:, :, 0:512]).then_inc(slot_in[3], 16)
            sp.dma_start(w_group(4), w_in0[:, :, 512:1024]).then_inc(slot_in[4], 16)
            sp.dma_start(gC[:, :, 0:328], w_in0[:, :, 1024:1352]).then_inc(slot_in[5], 16)
            sp.dma_start(gC[:, :, 328:336], w_in0[:, :, C_BETA:C_BETA + 8]).then_inc(slot_in[5], 16)
            sp.wait_ge(group_used, 1)
            sp.dma_start(w_group(0), w_in0[:, :, C_Z:C_Z + 512]).then_inc(slot_in[0], 16)
            sp.wait_ge(group_used, 2)
            sp.dma_start(wkv, w_kv_up[0].rearrange("(k p) n -> p k n", p=P)).then_inc(wkv_in, 16)
            sp.wait_ge(group_used, 4)
            for n in range(2):
                sp.dma_start(w_group(4 + n), w_out[0].rearrange("(k p) n -> p k n", p=P)[:, :, 512 * n:512 * n + 512])\
                  .then_inc(slot_in[4 + n], 16)
            sp.wait_ge(a_on, NT)
            sp.dma_start(wr, w_router[0].rearrange("(k p) e -> p k e", p=P)).then_inc(wr_in, 16)
            sp.dma_start(bdn, b_down[0]).then_inc(bias_in, 16)
            for row in range(4):
                sp.dma_start(bias_raw[NE * row:NE * row + NE, :], b_gate_up[0, :, 1024 * (row // 2):1024 * (row // 2) + 1024])\
                  .then_inc(bias_in, 16)

            def load(e, i, s):
                if s in (1, 2):
                    sp.wait_ge(w_lo_ready, PIECES * i + 4 * s - 8)
                else:
                    sp.wait_ge(plain_used, 4 * i + max(0, s - 2))
                sp.dma_start(w_group(s % 3), expert_chunk(e, s)).then_inc(raw_in[s % 3], 16)

            def load_item(e, e_next, i):
                for s in range(2, 6):
                    load(e, i, s)
                for s in range(2):
                    load(e_next, i + 1, s)

            for s in range(3):
                sp.dma_start(w_group(s), expert_chunk(0, s)).then_inc(raw_in[s], 16)
            for s in range(3, 6):
                load(0, 0, s)
            load(1, 1, 0)
            load(1, 1, 1)
            with sp.Fori(1, NE - 1) as e:
                load_item(e, e + 1, e)
            items = sp.value_load(nitems_i[0:1, 0:1], min_val=NE, max_val=ITEMS - 1)
            with sp.Fori(NE - 1, items) as i:
                e = sp.value_load(etab_i[0:1, bass.ds(i, 1)], min_val=0, max_val=NE - 1)
                e_next = sp.value_load(etab_i[0:1, bass.ds(i + 1, 1)], min_val=0, max_val=NE - 1)
                load_item(e, e_next, i)
            for r in range(2):
                sp.wait_ge(raw_in[r], 32 * items + 16)
            sp.wait_ge(acc_added, 8 * items + 8)
            for t in range(NT):
                sp.dma_start(out[0, P * t:P * t + P, :], h_t[t]).then_inc(out_done, 16)
            sp.wait_ge(out_done, 16 * NT)

        @block.gpsimd
        def _(pool):
            for dst, src in ((qn_w, q_norm_w), (kn_w, k_norm_w), (dn_w, delta_norm_w), (br_w, b_router), (alog, a_log),
                             (dtb, dt_bias), (ffnw[:, :], norm_ffn_w)):
                pool.dma_start(dst, src.partition_broadcast(P)).then_inc(gains_in, 16)
            for c in range(5):
                n = chunk_len(c)
                pool.wait_ge(f_A, c + 1)
                for lv in levels(c):
                    if c and lv in levels(c - 1):
                        pool.wait_ge(f_lvps, lv_count(c - 1) + 2 * lv)
                    m = konst_at(K_LV + lv * P, n, n).unsqueeze(1).to_broadcast([n, 4, n])
                    nc.gpsimd.tensor_tensor(F_E[lv][0:n, :, 0:n], F_A[0:n, :, 0:n], m, ALU.mult).then_inc(f_E, 1)

        @block.scalar
        def _(act_e):
            n_act = [0]

            def own(ins):
                n_act[0] += 1
                ins.then_inc(act_step, 1)
                act_e.wait_ge(act_step, n_act[0])

            A = nc.scalar.activation
            rows = [(norm_mix_w[0].rearrange("(k p) -> k p", p=P), 48, 56), (kv_norm_w[0].rearrange("(k p) -> k p", p=P), 56, 58)]
            for w in range(CW):
                act_e.dma_start(wrow[12 * w:12 * w + 12, :], conv_w[0, w].rearrange("(m p) -> m p", p=P)).then_inc(wrow_in, 16)
            for src, a, b in rows:
                act_e.dma_start(wrow[a:b, :], src).then_inc(wrow_in, 16)
            act_e.wait_ge(d_colw, 1)
            for t in range(5):
                n = tok_cols[t][1]
                src = metax if t == 0 else h_t[t - 1]
                act_e.wait_ge(x_in[t], 16)
                A(sq[0:n, :], src, ACT.Square, accum_out=ssqA[0:n, t:t + 1]).then_inc(a_ssq, 1)
                act_e.wait_ge(a_ssq, t + 1)
            act_e.wait_ge(d_stat, 1)
            A(st1[:, 0:5], rsA, ACT.Sqrt).then_inc(a_stat, 1)
            def silu(m):
                act_e.wait_ge(d_conv, m + 1)
                A(qkvT[:, m, PAD:], qkvT[:, m, PAD:], ACT.Silu).then_inc(conv_silu, 1)
                if m < 8:
                    act_e.wait_ge(conv_silu, m + 1)
                    if m >= 2:
                        act_e.wait_ge(qk_ssq, m - 1)
                    A(convsq[m % 2], qkvT[:, m, PAD:], ACT.Square).then_inc(conv_sq, 1)

            for m in range(12):
                for half in range(2):
                    act_e.wait_ge(conv_ps, 2 * m + half + 1)
                    A(qkvT[:, m, PAD + 264 * half:PAD + 264 * half + 264], ps[4 + 2 * (m % 2) + half][:, 0:264], ACT.Copy)\
                        .then_inc(conv_evac, 1)
                if m:
                    silu(m - 1)
            silu(11)
            for t in range(5):
                n = tok_cols[t][1]
                act_e.wait_ge(proj_ps, 4 * t + 4)
                if t:
                    act_e.wait_ge(d_rope, t)
                    own(A(sqC[:, 0:512], ps[0][:, :], ACT.Square))
                own(A(sqC[0:n, 512:768], ps[1][0:n, 0:256], ACT.Square))
                if t:
                    own(A(pre[:, 16:20, :], ps[1][:, 256:512].rearrange("p (a d) -> p a d", a=4), ACT.Copy))
                    own(A(pre[:, 20:24, :], ps[2][:, 0:256].rearrange("p (a d) -> p a d", a=4), ACT.Copy))
                    own(A(pre[:, 24, :], ps[2][:, 256:320], ACT.Copy))
                    own(A(wi[:, t - 1, :], ps[2][:, 320:328], ACT.Copy, scale=float(IH ** -0.5 * 64 ** -0.5)))
                    own(A(zs[:, t - 1, :], ps[3][:, :], ACT.Copy))
                A(ba[0:n, t, :], ps[2][0:n, 328:336], ACT.Copy).then_inc(a_proj, 1)
                act_e.wait_ge(d_stat, 2 + 2 * t)
                A(st2[0:n, 0:9], st1[0:n, 0:9], ACT.Sqrt).then_inc(a_stat, 1)
                act_e.wait_ge(kv_ps, 2 * t + 2)
                own(A(sqC[0:n, 0:512], ps[5][0:n, :], ACT.Square))
                A(vM if t == 0 else vA[:, t - 1, :], ps[6][0:n, :], ACT.Copy).then_inc(a_proj, 1)
                act_e.wait_ge(d_stat, 3 + 2 * t)
                A(st2[0:n, 0:8], st1[0:n, 0:8], ACT.Sqrt).then_inc(a_stat, 1)
            q = 0
            for j in range(1, NT):
                w = P * (j + 1)
                for hh in range(IH):
                    act_e.wait_ge(i_ps, q + 1)
                    if q >= 2:
                        act_e.wait_ge(i_add, q - 1)
                    A(rel[q % 2][:, 0:w], ps[q % 2][:, 0:w], ACT.Relu).then_inc(i_rel, 1)
                    q += 1
            act_e.wait_ge(d_stat, 12)
            A(rqk[:, :, :], rqk[:, :, :], ACT.Sqrt).then_inc(a_stat, 1)
            act_e.wait_ge(d_stat, 13)
            own(A(zs[:, :, :], zs[:, :, :], ACT.Silu))
            own(A(beta[:, :, :], ba[:, :, 0:4], ACT.Sigmoid))
            own(A(ea, alog, ACT.Exp))
            own(A(st1, st1, ACT.Exp, scale=-1.0))
            A(st3, st1, ACT.Ln, bias=1.0).then_inc(a_stat, 1)
            def decays(c):
                n = chunk_len(c)
                act_e.wait_ge(f_dd, c + 1)
                A(F_DN[0:n, :, 0:n], F_DN[0:n, :, 0:n], ACT.Exp, scale=-1.0).then_inc(act_step, 1)
                A(F_DT[0:n, :, 0:n], F_DT[0:n, :, 0:n], ACT.Exp).then_inc(act_step, 1)
                A(eg[c % 2][0:n, :], gcc[0:n, :], ACT.Exp).then_inc(act_step, 1)
                n_act[0] += 3
                act_e.wait_ge(act_step, n_act[0])
                A(el[c % 2], el[c % 2], ACT.Exp).then_inc(f_exp, 1)

            def copy_values(c):
                n = chunk_len(c)
                act_e.wait_ge(f_vn, c + 1)
                A(F_VN[0:n, :, :], heads(ps[1][0:n, :]), ACT.Copy).then_inc(f_vnc, 1)

            def copy_outputs(c):
                if c:
                    act_e.wait_ge(f_o, c)
                    A(F_O[:, :, :], heads(ps[3][:, :]), ACT.Copy).then_inc(f_oc, 1)

            decays(0)
            for c in range(5):
                n = chunk_len(c)
                for lv in levels(c):
                    act_e.wait_ge(f_lvps, lv_count(c) + 2 * lv)
                    A(F_Y[0:n, :, 0:n], heads(ps[7][0:n, :])[:, :, 0:n], ACT.Copy).then_inc(f_Y, 1)
                    if c and lv == 2:
                        copy_values(c - 1)
                    if c and lv == 3:
                        copy_outputs(c - 1)
                    if c < 4 and lv == (3 if c == 0 else 4):
                        decays(c + 1)
            copy_values(4)
            copy_outputs(4)
            act_e.wait_ge(d_stat, 14)
            A(orstd, ossq, ACT.Sqrt).then_inc(a_stat, 1)
            def attn_exp(q):
                w, hh = META + P * (q // AH + 1), q % AH
                act_e.wait_ge(a_msk, q + 1)
                A(prob[q % 3][:, 0:w], prob[q % 3][:, 0:w], ACT.Exp, bias=qmax[:, hh:hh + 1],
                  accum_out=qsums[q // AH % 2][:, hh:hh + 1]).then_inc(a_exp, 1)

            attn_exp(0)
            for q in range(NT * AH):
                if q + 1 < NT * AH:
                    attn_exp(q + 1)
                w = P * (q // AH + 1)
                act_e.wait_ge(a_pT, q + 1)
                own(A(pT[q % 2][:, 0:w], ps[2 + q % 2][:, 0:w], ACT.Copy))
                A(pT[q % 2][0:META, 512:640], ps[4][0:META, 0:P], ACT.Copy).then_inc(a_pTc, 1)

            def copy_oT(t):
                for half in range(2):
                    act_e.wait_ge(g_T, 2 * t + half + 1)
                    if t:
                        act_e.wait_ge(g_ps, 2 * t)
                    A(oT[:, 4 * half:4 * half + 4, :], ps[half][:, :].rearrange("p (k c) -> p k c", k=4), ACT.Copy)\
                        .then_inc(g_Tc, 1)

            copy_oT(0)
            for t in range(NT):
                if t + 1 < NT:
                    copy_oT(t + 1)
                act_e.wait_ge(g_h, t + 1)
                A(square_out, h_t[t], ACT.Square, accum_out=st1[:, t:t + 1]).then_inc(a_ssq, 1)
                act_e.wait_ge(d_stat, 15 + t)
                A(st3[:, t:t + 1], st2[:, t:t + 1], ACT.Sqrt).then_inc(a_stat, 1)
                for half in range(2):
                    act_e.wait_ge(g_xT, 2 * t + half + 1)
                    A(xT[:, 4 * half:4 * half + 4, :], ps[4 + half][:, :].rearrange("p (k c) -> p k c", k=4), ACT.Copy)\
                        .then_inc(g_xTc, 1)
            act_e.wait_ge(g_sel, NT)
            A(lg, lg, ACT.Exp).then_inc(a_stat, 1)
            act_e.wait_ge(g_ps, 2 * NT)
            A(onehotT, kc[:, 0:512].rearrange("p (t c) -> p t c", t=4), ACT.Copy, scale=0.0).then_inc(pt_ready, 1)

            def round_piece(i, n):
                if n in FIRST:
                    s = FIRST.index(n)
                    act_e.wait_ge(raw_in[s % 3], 32 * i + (16 if s < 3 else 32))
                act_e.wait_ge(piece_used, PIECES * i + n + 1)
                A(w_hi[n % RING][:, :], raw_piece(n), ACT.Copy).then_inc(w_hi_ready, 1)

            def sigmoid(i, n):
                act_e.wait_ge(gm_ready, 4 * i + n + 1)
                A(sg[:, 256 * n:256 * n + 256], gm[:, 256 * n:256 * n + 256], ACT.Sigmoid, scale=ALPHA).then_inc(sg_ready, 1)

            def copy_xe(i):
                act_e.wait_ge(x_ps, 2 * i + 1)
                A(xe[:, :], ps[6][:, 0:256], ACT.Copy).then_inc(xe_whole_ready, 1)
                A(xe_hi[:, 0:256], ps[6][:, 256:512], ACT.Copy).then_inc(xe_hi_ready, 1)
                act_e.wait_ge(x_ps, 2 * i + 2)
                A(xe_hi[:, 256:768], ps[7][:, :], ACT.Copy).then_inc(xe_hi_ready, 1)

            def copy_actT(i, half):
                act_e.wait_ge(actT_ps, 2 * i + half + 1)
                A(actT_hi[:, 512 * half:512 * half + 512], ps[half][:, :], ACT.Copy).then_inc(actT_hi_ready, 1)

            def copy_y(i, half):
                act_e.wait_ge(piece_used, PIECES * i + RING + 16 + 4 * half)
                A(y_hi[:, 512 * half:512 * half + 512], ps[4 + half][:, :], ACT.Copy).then_inc(y_hi_ready, 1)

            for n in range(4):
                round_piece(0, n)
            copy_xe(0)
            act_e.wait_ge(table_ready, 1)
            items = act_e.value_load(nitems_i[0:1, 0:1], min_val=NE, max_val=ITEMS - 1)
            with act_e.Fori(0, items) as i:
                A(sg[:, 0:1], konst_at(K_ONE, P, 1), ACT.Sigmoid).then_inc(table_loaded, 1)
                for s in range(1, 4):
                    for j in range(3):
                        round_piece(i, 3 * s + 1 + j)
                        if j == 1 and s > 1:
                            if s == 2:
                                act_e.wait_ge(table_loaded, i + 1)
                            sigmoid(i, s - 2)
                round_piece(i, 13)
                act_e.wait_ge(pt_ps, i + 1)
                A(onehotT, ps[6][:, :].rearrange("p (t c) -> p t c", t=4), ACT.Copy).then_inc(pt_ready, 1)
                sigmoid(i, 2)
                round_piece(i, 14)
                round_piece(i, 15)
                copy_actT(i, 0)
                sigmoid(i, 3)
                round_piece(i, 16)
                copy_xe(i + 1)
                copy_actT(i, 1)
                for n in range(17, 20):
                    round_piece(i, n)
                round_piece(i + 1, 0)
                copy_y(i, 0)
                for n in range(1, 4):
                    round_piece(i + 1, n)
                copy_y(i, 1)

        @block.vector
        def _(dve):
            V = nc.vector
            counts = {}

            def own(ins, signal=dve_step, wait=True):
                counts[signal.num] = counts.get(signal.num, 0) + 1
                ins.then_inc(signal, 1)
                if wait:
                    dve.wait_ge(signal, counts[signal.num])

            def bc(ap, shape):
                return ap.to_broadcast(shape)

            own(V.memset(small[:, :], 1.0), d_colw)
            own(V.memset(qkvT[:, :, 0:PAD], 0.0))
            dve.wait_ge(a_ssq, 5)
            own(V.tensor_scalar(rsA, ssqA, 1.0 / D, EPS, ALU.mult, ALU.add), d_stat)
            dve.wait_ge(konst_in, 16)
            dve.wait_ge(colw_T, 1)
            own(V.tensor_copy(colw[:, :], ps[7][:, 0:58]))
            dve.wait_ge(a_stat, 1)
            own(V.reciprocal(rsA, st1[:, 0:5]))

            def scale_rows(t):
                n = tok_cols[t][1]
                src = metax if t == 0 else h_t[t - 1]
                if t >= 2:
                    dve.wait_ge(u_T, 2 * (t - 1))
                own(V.tensor_scalar(utmp[t % 2][0:n, :], src, rsA[0:n, t:t + 1], None, ALU.mult), d_u, wait=False)

            scale_rows(0)
            for t in range(5):
                at, n = tok_cols[t]
                if t < 4:
                    scale_rows(t + 1)
                for half in range(2):
                    dve.wait_ge(u_T, 2 * t + half + 1)
                    own(V.tensor_tensor(uT[:, 4 * half:4 * half + 4, at:at + n],
                                        ps[2 * (t % 2) + half][:, :].rearrange("p (k c) -> p k c", k=4)[:, :, 0:n],
                                        bc(colw[:, 48 + 4 * half:52 + 4 * half].unsqueeze(2), [P, 4, n]), ALU.mult), u_evac, wait=False)
            dve.wait_ge(u_evac, 10)
            for m in range(12):
                dve.wait_ge(conv_evac, 2 * m + 2)
                own(V.tensor_scalar(conv_a[0], qkvT[:, m, 0:T], colw[:, m:m + 1], None, ALU.mult))
                for w in range(1, CW - 1):
                    own(V.scalar_tensor_tensor(out=conv_a[w % 2], in0=qkvT[:, m, w:w + T], scalar=colw[:, 12 * w + m:12 * w + m + 1],
                                               in1=conv_a[(w + 1) % 2], op0=ALU.mult, op1=ALU.add))
                w = CW - 1
                own(V.scalar_tensor_tensor(out=qkvT[:, m, PAD:], in0=qkvT[:, m, PAD:], scalar=colw[:, 12 * w + m:12 * w + m + 1],
                                       in1=conv_a[(w + 1) % 2], op0=ALU.mult, op1=ALU.add), d_conv)
            dve.wait_ge(gains_in, 16 * 7)
            dve.wait_ge(qk_ssq, 8)
            own(V.tensor_copy(rqk[0:META, 0, :], ps[3][0:META, 0:8]))
            own(V.tensor_copy(rqk[:, 1:5, :], ps[3][:, 8:40].rearrange("p (t c) -> p t c", t=NT)))
            own(V.tensor_scalar(gcc, gcc, 1.0, None, ALU.mult), d_ssqc)
            for t in range(5):
                at, n = tok_cols[t]
                dve.wait_ge(a_proj, 2 * t + 1)
                if t:
                    own(V.tensor_reduce(st1[:, 0:8], sqC[:, 0:512].rearrange("p (a d) -> p a d", a=8), AX.X, ALU.add))
                    own(V.tensor_scalar(st1[:, 0:8], st1[:, 0:8], 1.0 / AD, EPS, ALU.mult, ALU.add))
                own(V.tensor_reduce(st1[0:n, 8:9], sqC[0:n, 512:768], AX.X, ALU.add))
                own(V.tensor_scalar(st1[0:n, 8:9], st1[0:n, 8:9], 1.0 / RANK, EPS, ALU.mult, ALU.add), d_stat)
                dve.wait_ge(a_stat, 2 + 2 * t)
                own(V.reciprocal(st3[0:n, 0:9], st2[0:n, 0:9]))
                own(V.tensor_scalar(ckv[0:n, :], ps[1][0:n, 0:256], st3[0:n, 8:9], None, ALU.mult), d_ckv)
                if t:
                    own(V.tensor_tensor(pre[:, 0:8, :], ps[0][:, :].rearrange("p (a d) -> p a d", a=8),
                                        bc(st3[:, 0:8].unsqueeze(2), [P, 8, AD]), ALU.mult))
                    own(V.tensor_tensor(pre[:, 0:8, :], pre[:, 0:8, :], bc(qn_w.unsqueeze(1), [P, 8, AD]), ALU.mult))
                dve.wait_ge(ckv_T, t + 1)
                own(V.tensor_scalar(ckvT[0][:, 0:n], ps[4][:, 0:n], colw[:, 56:57], None, ALU.mult))
                own(V.tensor_scalar(ckvT[1][:, 0:n], ps[4][:, P:P + n], colw[:, 57:58], None, ALU.mult), d_ckvT)
                dve.wait_ge(a_proj, 2 * t + 2)
                own(V.tensor_reduce(st1[0:n, 0:8], sqC[0:n, 0:512].rearrange("p (a d) -> p a d", a=8), AX.X, ALU.add))
                own(V.tensor_scalar(st1[0:n, 0:8], st1[0:n, 0:8], 1.0 / AD, EPS, ALU.mult, ALU.add), d_stat)
                dve.wait_ge(a_stat, 3 + 2 * t)
                own(V.reciprocal(st3[0:n, 0:8], st2[0:n, 0:8]))
                own(V.tensor_tensor(pre[0:n, 8:16, :], ps[5][0:n, :].rearrange("p (a d) -> p a d", a=8),
                                    bc(st3[0:n, 0:8].unsqueeze(2), [n, 8, AD]), ALU.mult))
                own(V.tensor_tensor(pre[0:n, 8:16, :], pre[0:n, 8:16, :], bc(kn_w[0:n].unsqueeze(1), [n, 8, AD]), ALU.mult))
                a, b = (8, 16) if t == 0 else (0, ROPE_H)
                cs = K_MCOS if t == 0 else K_COS + 32 * (t - 1)
                sn = K_MSIN if t == 0 else K_SIN + 32 * (t - 1)
                cosb = bc(kc[0:n, cs:cs + 32].unsqueeze(1), [n, b - a, 32])
                sinb = bc(kc[0:n, sn:sn + 32].unsqueeze(1), [n, b - a, 32])
                x1, x2 = pre[0:n, a:b, 0:32], pre[0:n, a:b, 32:64]
                y1, y2 = rp[0:n, a:b, 0:32], rp[0:n, a:b, 32:64]
                if t:
                    dve.wait_ge(rope_T, 4 * t)
                own(V.tensor_tensor(y1, x1, cosb, ALU.mult))
                own(V.tensor_tensor(y2, x2, cosb, ALU.mult))
                own(V.tensor_tensor(x2, x2, sinb, ALU.mult))
                own(V.tensor_tensor(x1, x1, sinb, ALU.mult))
                own(V.tensor_tensor(y1, y1, x2, ALU.subtract))
                own(V.tensor_tensor(y2, y2, x1, ALU.add))
                if t:
                    own(V.tensor_copy(rp[:, 25, :], rp[:, 24, :]))
                own(V.memset(mx8, 0.0), d_rope)
                dve.wait_ge(rope_T, 4 * t + 4)
                if t:
                    own(V.tensor_copy(qT[:, :, P * (t - 1):P * t], heads(ps[7][:, :])))
                    own(V.tensor_copy(kT[:, :, at:at + P], heads(ps[4][:, :])))
                    if t >= 2:
                        own(V.tensor_copy(qiT[:, :, P * (t - 2):P * (t - 1)], heads(ps[5][:, :])))
                    own(V.tensor_copy(kiT[:, P * (t - 1):P * t], ps[6][:, 0:P]))
                else:
                    own(V.tensor_copy(kT[:, :, 0:META], heads(ps[4][:, :])[:, :, 0:META]))
                own(V.memset(mx8, 0.0), d_ropeT)
            q = 0
            for j in range(1, NT):
                w = P * (j + 1)
                row = isc[:, j - 1, 0:w]
                for hh in range(IH):
                    dve.wait_ge(i_rel, q + 1)
                    if hh == 0:
                        own(V.tensor_scalar(row, rel[q % 2][:, 0:w], wi[:, j, 0:1], None, ALU.mult), i_add)
                    else:
                        own(V.scalar_tensor_tensor(out=row, in0=rel[q % 2][:, 0:w], scalar=wi[:, j, hh:hh + 1], in1=row,
                                               op0=ALU.mult, op1=ALU.add), i_add)
                    dve.wait_ge(i_add, q + 1)
                    q += 1
                diag = isc[:, j - 1, P * j:w]
                own(V.tensor_tensor(diag, diag, konst_at(K_LI), ALU.mult))
                own(V.tensor_tensor(diag, diag, konst_at(K_LOW), ALU.add))

            def top_k(step):
                j, at = 1 + step // (TOPK // 8), step % (TOPK // 8)
                row = isc[:, j - 1, 0:P * (j + 1)]
                own(V.max(top8, row))
                own(V.match_replace(row, top8, row, TAKEN))
                if at == TOPK // 8 - 1:
                    own(V.tensor_scalar(row, row, TAKEN, HIDE, ALU.not_equal, ALU.mult))

            own(V.tensor_scalar(rqk[:, :, :], rqk[:, :, :], EPS, None, ALU.add), d_stat)
            y = st4.rearrange("p (t c) -> p t c", t=5)
            own(V.tensor_tensor(y, ba[:, :, 4:8], bc(dtb.unsqueeze(1), [P, 5, 4]), ALU.add))
            own(V.tensor_scalar(st2, st4, -1.0, None, ALU.mult))
            own(V.tensor_tensor(st1, st4, st2, ALU.max), d_stat)
            dve.wait_ge(a_stat, 12)
            own(V.reciprocal(rqk[:, :, :], rqk[:, :, :]))
            dve.wait_ge(a_stat, 13)
            own(V.scalar_tensor_tensor(out=st4, in0=st4, scalar=0.0, in1=st3, op0=ALU.max, op1=ALU.add))
            own(V.tensor_scalar(ea, ea, -1.0, None, ALU.mult))
            own(V.tensor_tensor(gg[:, :, :], y, bc(ea.unsqueeze(1), [P, 5, 4]), ALU.mult))
            def bank(b, n):
                return heads(ps[b][:, :])[0:n]

            def feed(c):
                n = chunk_len(c)
                if c:
                    dve.wait_ge(f_ps, c)
                own(V.tensor_copy(F_GB[0:n, :, :], bc(gg[0:n, c, :].unsqueeze(2), [n, 4, P])), wait=False)
                own(V.tensor_copy(F_RK[0:n, :, 0:n], bc(rqk[0:n, c, 4:8].unsqueeze(2), [n, 4, n])), wait=False)
                dve.wait_ge(dve_step, counts[dve_step.num])
                own(V.memset(mx8, 0.0), f_in)

            def head_decays(c):
                n, R = chunk_len(c), bank(0, P)
                dve.wait_ge(f_ps, c + 1)
                own(V.tensor_copy(gcc[0:n, :], ps[3][0:n, 0:4]))
                for hh in range(BH):
                    own(V.tensor_scalar(F_DT[0:n, hh, 0:n], R[0:n, hh, 0:n], gcc[0:n, hh:hh + 1], 0.0, ALU.subtract, ALU.min), wait=False)
                    own(V.tensor_scalar(F_DN[0:n, hh, 0:n], R[0:n, hh, 0:n], gcc[0:n, hh:hh + 1], 0.0, ALU.subtract, ALU.max), wait=False)
                dve.wait_ge(dve_step, counts[dve_step.num])
                own(V.tensor_copy(el[c % 2].unsqueeze(2), R[:, :, n - 1:n]), f_dd)
                own(V.tensor_tensor(br[0:n, :], beta[0:n, c, :], rqk[0:n, c, 4:8], ALU.mult))

            def head_matrix(c):
                n = chunk_len(c)
                dve.wait_ge(f_exp, c + 1)
                own(V.scalar_tensor_tensor(out=ngk[c % 2][0:n, :], in0=eg[c % 2][0:n, :], scalar=-1.0, in1=br[0:n, :], op0=ALU.mult,
                                           op1=ALU.mult), wait=False)
                own(V.tensor_tensor(F_DN[0:n, :, 0:n], bank(1, n)[:, :, 0:n], F_DN[0:n, :, 0:n], ALU.mult))
                own(V.tensor_tensor(F_DN[0:n, :, 0:n], bank(2, n)[:, :, 0:n], F_DN[0:n, :, 0:n], ALU.mult))
                if c:
                    dve.wait_ge(f_E, sum(len(levels(b)) for b in range(c)))
                for hh in range(BH):
                    own(V.scalar_tensor_tensor(out=F_A[0:n, hh, 0:n], in0=F_DN[0:n, hh, 0:n], scalar=br[0:n, hh:hh + 1],
                                               in1=konst_at(K_LS, n, n), op0=ALU.mult, op1=ALU.mult), wait=False)
                dve.wait_ge(dve_step, counts[dve_step.num])
                own(V.memset(mx8, 0.0), f_A)

            def start_inverse(c):
                n = chunk_len(c)
                own(V.tensor_tensor(F_Y[0:n, :, 0:n], F_A[0:n, :, 0:n], bc(konst_at(K_LV, n, n).unsqueeze(1), [n, 4, n]), ALU.mult))
                own(V.tensor_tensor(F_D[0:n, :, 0:n], bc(ident(n).unsqueeze(1), [n, 4, n]), F_Y[0:n, :, 0:n], ALU.subtract), f_init)

            def transposed_inverse(c):
                n = chunk_len(c)
                dve.wait_ge(f_lvps, lv_count(c) + 1)
                own(V.tensor_tensor(F_Dt[c % 2][0:n, :, 0:n], bc(ident(n).unsqueeze(1), [n, 4, n]), bank(7, n)[:, :, 0:n],
                                    ALU.subtract), f_lv)

            def head_rest(c):
                n, rk = chunk_len(c), rqk[0:chunk_len(c), c, 4:8]
                dve.wait_ge(f_rest_ps, c + 1)
                own(V.tensor_tensor(st2[0:n, 0:4].unsqueeze(2), F_DT[0:n, :, n - 1:n], rk.unsqueeze(2), ALU.mult))
                own(V.tensor_tensor(F_KD[c % 2][0:n, :, :], bank(1, n), bc(st2[0:n, 0:4].unsqueeze(2), [n, 4, P]), ALU.mult), wait=False)
                own(V.tensor_tensor(F_VB[c % 2][0:n, :, :], bank(2, n), bc(beta[0:n, c, :].unsqueeze(2), [n, 4, P]), ALU.mult), wait=False)
                if c:
                    own(V.tensor_tensor(F_DT[:, :, :], bank(0, P), F_DT[:, :, :], ALU.mult))
                    for hh in range(BH):
                        own(V.scalar_tensor_tensor(out=F_IT[c % 2][:, hh, :], in0=F_DT[:, hh, :], scalar=rk[:, hh:hh + 1],
                                                   in1=konst_at(K_UI), op0=ALU.mult, op1=ALU.mult), wait=False)
                dve.wait_ge(dve_step, counts[dve_step.num])
                own(V.memset(mx8, 0.0), f_rest)

            def residual(c):
                n = chunk_len(c)
                if c == 0:
                    own(V.tensor_copy(F_R[0:n, :, :], F_VB[0][0:n, :, :]), f_r)
                    return
                dve.wait_ge(f_ks, c)
                for hh in range(BH):
                    own(V.scalar_tensor_tensor(out=F_R[:, hh, :], in0=bank(0, P)[:, hh, :], scalar=ngk[c % 2][:, hh:hh + 1],
                                               in1=F_VB[c % 2][:, hh, :], op0=ALU.mult, op1=ALU.add), wait=False)
                dve.wait_ge(dve_step, counts[dve_step.num])
                own(V.memset(mx8, 0.0), f_r)

            def new_state(c):
                dve.wait_ge(f_s, c + 1)
                if c == 0:
                    own(V.tensor_copy(F_S[:, :, :], bank(4, P)), f_sc)
                    return
                for hh in range(BH):
                    own(V.scalar_tensor_tensor(out=F_S[:, hh, :], in0=F_S[:, hh, :], scalar=el[c % 2][:, hh:hh + 1],
                                               in1=bank(4, P)[:, hh, :], op0=ALU.mult, op1=ALU.add), wait=False)
                dve.wait_ge(f_oc, c)
                for hh in range(BH):
                    own(V.scalar_tensor_tensor(out=F_O[:, hh, :], in0=bank(2, P)[:, hh, :], scalar=eg[c % 2][:, hh:hh + 1],
                                               in1=F_O[:, hh, :], op0=ALU.mult, op1=ALU.add), wait=False)
                dve.wait_ge(dve_step, counts[dve_step.num])
                own(V.memset(mx8, 0.0), f_sc)

            def outputs(c):
                if c == 0:
                    return
                own(V.tensor_scalar(st2[:, 0:4], rqk[:, c, 0:4], float(BD ** -0.5), None, ALU.mult))
                o = oab[:, c - 1, AW:].rearrange("p (h c) -> p h c", h=4)
                own(V.tensor_tensor(o, F_O[:, :, :], bc(st2[:, 0:4].unsqueeze(2), [P, 4, P]), ALU.mult))
                own(V.tensor_tensor(F_O[:, :, :], o, o, ALU.mult))
                own(V.tensor_reduce(ossq[:, 4 * (c - 1):4 * c], F_O[:, :, :], AX.X, ALU.add))

            steps = 0
            feed(0)
            head_decays(0)
            head_matrix(0)
            start_inverse(0)
            for c in range(5):
                n = chunk_len(c)
                transposed_inverse(c)
                for lv in levels(c):
                    at = lv_count(c) + 2 * lv
                    if lv == 1:
                        head_rest(c)
                    elif c:
                        if lv == 6:
                            outputs(c - 1)
                        top_k(steps)
                        steps += 1
                    dve.wait_ge(f_lvps, at + 1)
                    if lv != levels(c)[-1]:
                        own(V.tensor_tensor(F_D[0:n, :, 0:n], F_D[0:n, :, 0:n], bank(5, n)[:, :, 0:n], ALU.subtract), wait=False)
                    own(V.tensor_tensor(F_Dt[c % 2][0:n, :, 0:n], F_Dt[c % 2][0:n, :, 0:n], bank(6, n)[:, :, 0:n], ALU.subtract), f_lv)
                    dve.wait_ge(dve_step, counts[dve_step.num])
                    if c and lv == 1:
                        residual(c - 1)
                    if c and lv == 3:
                        new_state(c - 1)
                    if c < 4 and lv == 2:
                        feed(c + 1)
                    if c < 4 and lv == (3 if c == 0 else 4):
                        head_decays(c + 1)
                    if c < 4 and lv == (3 if c == 0 else 5):
                        head_matrix(c + 1)
                if c < 4:
                    start_inverse(c + 1)
            residual(4)
            new_state(4)
            outputs(4)
            own(V.tensor_scalar(ossq, ossq, 1.0 / BD, EPS, ALU.mult, ALU.add), d_stat)
            dve.wait_ge(a_stat, 14)
            own(V.reciprocal(orstd, orstd))

            def gated_norm(t):
                o = oab[:, t, AW:].rearrange("p (h c) -> p h c", h=4)
                own(V.tensor_tensor(o, o, bc(orstd[:, 4 * t:4 * t + 4].unsqueeze(2), [P, 4, P]), ALU.mult))
                own(V.tensor_tensor(o, o, bc(dn_w.unsqueeze(1), [P, 4, P]), ALU.mult))
                own(V.tensor_tensor(o, o, zs[:, t, :].rearrange("p (h c) -> p h c", h=4), ALU.mult))

            def normalize(j):
                dve.wait_ge(a_exp, AH * (j + 1))
                own(V.reciprocal(qinv, qsums[j % 2]))
                dve.wait_ge(a_o, j + 1)
                own(V.tensor_tensor(oab[:, j, 0:AW].rearrange("p (a d) -> p a d", a=AH), ps[7][:, :].rearrange("p (a d) -> p a d", a=AH),
                                bc(qinv.unsqueeze(2), [P, AH, AD]), ALU.mult), a_on)

            for j in range(NT):
                w = META + P * (j + 1)
                for hh in range(AH):
                    q = AH * j + hh
                    pr = prob[q % 3]
                    dve.wait_ge(a_sc, q + 1)
                    own(V.tensor_scalar(pr[:, 0:META], ps[5 + q % 2][:, 0:META], AD ** -0.5, None, ALU.mult))
                    mask = konst_at(K_ADD) if j == 0 else isc[:, j - 1, 0:P * (j + 1)]
                    own(V.scalar_tensor_tensor(out=pr[:, META:w], in0=ps[q % 2][:, 0:P * (j + 1)], scalar=AD ** -0.5, in1=mask,
                                               op0=ALU.mult, op1=ALU.add))
                    own(V.tensor_reduce(mx8[:, 0:1], pr[:, 0:w], AX.X, ALU.max))
                    own(V.tensor_scalar(qmax[:, hh:hh + 1], mx8[:, 0:1], -1.0, None, ALU.mult), a_msk)
                    for _ in range(2 if 2 * AH <= q < 2 * AH + 4 else 1):
                        if steps < 3 * TOPK // 8:
                            top_k(steps)
                            steps += 1
                    if j == NT - 1 and hh % 2:
                        gated_norm(hh // 2)
                    if j and hh == 1:
                        normalize(j - 1)
            normalize(NT - 1)

            def add_mixer(t):
                for half in range(2):
                    dve.wait_ge(g_ps, 2 * t + half + 1)
                    hs = h[:, D * t + 512 * half:D * t + 512 * half + 512]
                    own(V.tensor_tensor(hs, hs, ps[2 + half][:, :], ALU.add))
                own(V.memset(mx8, 0.0), g_h)

            def moe_constants():
                own(V.tensor_copy(ident_b[:, :], ident()))
                dve.wait_ge(bias_in, 16 * 5)
                own(V.tensor_copy(bias2[:, :], bias_raw))
                for row in (1, 3):
                    r = slice(NE * row, NE * row + NE)
                    own(V.tensor_tensor(bias2[r, :], bias_raw[r, :], f32(bias2[r, :]), ALU.subtract))
                own(V.memset(f32(y_hi[:, :]), 0.0), y_ready)
                own(V.memset(f32(y_lo[:, :]), 0.0), y_ready)

            add_mixer(0)
            for t in range(NT):
                dve.wait_ge(a_ssq, 6 + t)
                own(V.tensor_scalar(st2[:, t:t + 1], st1[:, t:t + 1], 1.0 / D, EPS, ALU.mult, ALU.add), d_stat)
                dve.wait_ge(a_stat, 15 + t)
                own(V.reciprocal(st4[:, t:t + 1], st3[:, t:t + 1]))
                own(V.scalar_tensor_tensor(out=xraw, in0=h_t[t], scalar=st4[:, t:t + 1], in1=ffnw[:, :], op0=ALU.mult,
                                           op1=ALU.mult), g_xn)
                own(V.tensor_copy(piece(xn[0], t), xraw))
                own(V.tensor_tensor(x_rest[:, :], xraw, piece(xn[0], t), ALU.subtract))
                own(V.tensor_copy(piece(xn[1], t), x_rest[:, :]))
                own(V.tensor_tensor(piece(xn[2], t), x_rest[:, :], piece(xn[1], t), ALU.subtract))
                if t + 1 < NT:
                    add_mixer(t + 1)
                if t == 0:
                    moe_constants()
                dve.wait_ge(g_lg, t + 1)
                own(V.tensor_tensor(lg[:, t, :], ps[6][:, 0:NE], br_w, ALU.add))
                own(V.max(mx8, lg[:, t, :]))
                own(V.max_index(eidx[:, 0:8], mx8, lg[:, t, :]))
                own(V.tensor_copy(qsum, eidx[:, 0:8]))
                own(V.tensor_scalar(selm[:, t, :], konst_at(K_IOTA, P, NE), qsum[:, 0:1], None, ALU.is_equal))
                for k in range(1, TOPE):
                    own(V.scalar_tensor_tensor(out=selm[:, t, :], in0=konst_at(K_IOTA, P, NE), scalar=qsum[:, k:k + 1],
                                               in1=selm[:, t, :], op0=ALU.is_equal, op1=ALU.add))
                own(V.tensor_scalar(lg[:, t, :], lg[:, t, :], mx8[:, 0:1], None, ALU.subtract))
                own(V.memset(mx8, 0.0), g_sel)
            dve.wait_ge(a_stat, 19)
            own(V.tensor_tensor(lg, lg, selm, ALU.mult))
            own(V.tensor_reduce(st1[:, 0:NT], lg, AX.X, ALU.add))
            own(V.reciprocal(st2[:, 0:NT], st1[:, 0:NT]))
            own(V.tensor_tensor(lg, lg, bc(st2[:, 0:NT].unsqueeze(2), [P, NT, NE]), ALU.mult), g_gt)
            own(V.tensor_copy(gate.rearrange("p (e t) -> p t e", t=NT), lg))
            dve.wait_ge(g_gtc, 1)
            own(V.tensor_copy(gT, ps[0][0:NE, :]))
            own(V.memset(mx8, 0.0), g_bd)
            dve.wait_ge(g_rk, NT + 1)
            ranks = ps[7][:, 0:NT * NE].rearrange("p (t e) -> p t e", t=NT)
            own(V.scalar_tensor_tensor(out=tok_rank, in0=ranks, scalar=1.0, in1=selm, op0=ALU.add, op1=ALU.mult))
            own(V.tensor_scalar(rankm.rearrange("p (e t) -> p t e", t=NT), tok_rank, -1.0, None, ALU.add))
            dve.wait_ge(g_rk, NT + 1)
            own(V.tensor_copy(cnt, ps[7][:, 128:160]))
            own(V.tensor_scalar(blocks, cnt, float(P), None, ALU.is_gt))
            for b in range(2, NT):
                own(V.scalar_tensor_tensor(out=blocks, in0=cnt, scalar=float(P * b), in1=blocks, op0=ALU.is_gt, op1=ALU.add))
            own(V.tensor_tensor_scan(cum, konst_at(K_ONE, P, NE), blocks, 0.0, ALU.mult, ALU.add))
            own(V.tensor_copy(etab[:, 0:NE], konst_at(K_IOTA, P, NE)))
            own(V.memset(shift[:, 0:NE], 0.0))
            over = [ITEMS - NE, NE]
            ended = xraw[:, 0:over[0] * NE].rearrange("p (i e) -> p i e", i=over[0])
            own(V.tensor_tensor(ended, bc(cum.unsqueeze(1), [P] + over), bc(konst_at(K_IOTA, P, over[0]).unsqueeze(2), [P] + over),
                                ALU.is_le))
            own(V.tensor_reduce(etab[:, NE:ITEMS], ended, AX.X, ALU.add))
            own(V.tensor_tensor(ended, ended, bc(blocks.unsqueeze(1), [P] + over), ALU.mult))
            own(V.tensor_reduce(shift[:, NE:ITEMS], ended, AX.X, ALU.add))
            own(V.scalar_tensor_tensor(out=shift[:, NE:ITEMS], in0=konst_at(K_IOTA, P, over[0]), scalar=1.0, in1=shift[:, NE:ITEMS],
                                       op0=ALU.add, op1=ALU.subtract))
            own(V.tensor_scalar(shift[:, NE:ITEMS], shift[:, NE:ITEMS], float(P), None, ALU.mult))
            own(V.tensor_scalar(etab, etab, float(NE - 1), None, ALU.min))
            own(V.tensor_copy(etab_i[:, :], etab))
            own(V.tensor_scalar(nitems_i[:, :], cum[:, NE - 1:NE], float(NE), None, ALU.add))
            own(V.memset(gcol, 0.0), table_ready)
            items = dve.value_load(nitems_i[0:1, 0:1], min_val=NE, max_val=ITEMS - 1)

            def build_onehot(e, i):
                for t in range(NT):
                    V.tensor_scalar(onehot[:, t, :], konst_at(K_IOTA), shift[:, bass.ds(i, 1)], rankm[:, bass.ds(4 * e + t, 1)],
                                    ALU.add, ALU.is_equal)
                for half in range(2):
                    ins = V.tensor_copy(sel[half][:, :], kc[:, bass.ds(K_TWO + NE * half + e, 1)].to_broadcast([P, P]))
                ins.then_inc(p_built, 1)

            def split_piece(i, n):
                dve.wait_ge(w_hi_ready, PIECES * i + n + 1)
                V.tensor_tensor(w_lo[n % RING][:, :], raw_piece(n), f32(w_hi[n % RING][:, :]), ALU.subtract).then_inc(w_lo_ready, 1)

            def add_scattered(i, q):
                half, t = q // 4, q % 4
                dve.wait_ge(scat_ps, 8 * i + q + 1)
                hs = h[:, D * t + 512 * half:D * t + 512 * half + 512]
                V.scalar_tensor_tensor(out=hs, in0=ps[6 + q % 2][:, :], scalar=gcol[:, t:t + 1], in1=hs, op0=ALU.mult,
                                       op1=ALU.add).then_inc(acc_added, 1)

            def clamp(i, n):
                c = slice(256 * n, 256 * n + 256)
                gu = ps[n][:, :].rearrange("p (f two) -> p f two", two=2)
                dve.wait_ge(piece_used, PIECES * i + RING + 3 * n + 3)
                V.tensor_scalar(gm[:, c], gu[:, :, 0], LIMIT, None, ALU.min).then_inc(gm_ready, 1)
                V.tensor_scalar(act[:, c], gu[:, :, 1], LIMIT, -LIMIT, ALU.min, ALU.max).then_inc(loop_step, 1)
                dve.wait_ge(loop_step, 8 * i + 2 * n + 1)
                V.scalar_tensor_tensor(out=act[:, c], in0=act[:, c], scalar=1.0, in1=gm[:, c], op0=ALU.add, op1=ALU.mult)\
                    .then_inc(loop_step, 1)

            def times_sigmoid(i, n):
                c = slice(256 * n, 256 * n + 256)
                dve.wait_ge(loop_step, 8 * i + 2 * n + 2)
                dve.wait_ge(sg_ready, 4 * i + n + 1)
                V.tensor_tensor(act[:, c], act[:, c], sg[:, c], ALU.mult).then_inc(act_ready, 1)

            def low_xe(i):
                for half, c in ((0, slice(0, 256)), (1, slice(256, 768))):
                    dve.wait_ge(xe_hi_ready, 2 * i + half + 1)
                    V.tensor_tensor(xe_lo[:, c], ps[6 + half][:, 256 - 256 * half:512], f32(xe_hi[:, c]), ALU.subtract)\
                        .then_inc(xe_ready, 1)

            def low_actT(i, half):
                c = slice(512 * half, 512 * half + 512)
                dve.wait_ge(actT_hi_ready, 2 * i + half + 1)
                V.tensor_tensor(actT_lo[:, c], ps[half][:, :], f32(actT_hi[:, c]), ALU.subtract).then_inc(actT_ready, 1)

            def low_y(i, half):
                c = slice(512 * half, 512 * half + 512)
                dve.wait_ge(y_hi_ready, 2 * i + half + 1)
                V.tensor_tensor(y_lo[:, c], ps[4 + half][:, :], f32(y_hi[:, c]), ALU.subtract).then_inc(y_ready, 1)

            build_onehot(0, 0)
            dve.wait_ge(p_built, 1)
            for n in range(2):
                split_piece(0, n)
            for q in range(2 * NT):
                t, half = q // 2, q % 2
                dve.wait_ge(g_acc, q + 1)
                hs = h[:, D * t + 512 * half:D * t + 512 * half + 512]
                V.tensor_tensor(hs, hs, ps[BDOWN[q]][:, :], ALU.add).then_inc(g_bd, 1)
            for n in range(2, 4):
                split_piece(0, n)
            low_xe(0)
            with dve.Fori(0, items) as i:
                e = dve.value_load(etab_i[0:1, bass.ds(i, 1)], min_val=0, max_val=NE - 1)
                e_next = dve.value_load(etab_i[0:1, bass.ds(i + 1, 1)], min_val=0, max_val=NE - 1)
                for s in range(1, 4):
                    for j in range(3):
                        split_piece(i, 3 * s + 1 + j)
                        if (s - 1, j) in SCATTER_AT:
                            add_scattered(i, SCATTER_AT.index((s - 1, j)))
                        if s > 1 and j == 0:
                            clamp(i, s - 2)
                        if s > 1 and j == 1:
                            times_sigmoid(i, s - 2)
                dve.wait_ge(acc_added, 8 * i + 8)
                V.tensor_copy(gcol, gate[:, bass.ds(4 * e, 4)])
                split_piece(i, 13)
                clamp(i, 2)
                dve.wait_ge(pt_ps, i + 1)
                dve.wait_ge(piece_used, PIECES * i + RING + 10)
                build_onehot(e_next, i + 1)
                dve.wait_ge(p_built, i + 2)
                split_piece(i, 14)
                times_sigmoid(i, 2)
                split_piece(i, 15)
                clamp(i, 3)
                low_actT(i, 0)
                split_piece(i, 16)
                times_sigmoid(i, 3)
                low_xe(i + 1)
                low_actT(i, 1)
                for n in range(17, 20):
                    split_piece(i, n)
                split_piece(i + 1, 0)
                low_y(i, 0)
                for n in range(1, 4):
                    split_piece(i + 1, n)
                low_y(i, 1)
            for q in range(2 * NT):
                add_scattered(items, q)

        @block.tensor
        def _(pe):
            M = nc.tensor.matmul
            TR = nc.tensor.transpose
            pe.wait_ge(konst_in, 16)
            pe.wait_ge(wrow_in, 16 * 6)
            TR(ps[7][:, 0:58], wrow, ident(58)).then_inc(colw_T, 1)
            for t in range(5):
                n = tok_cols[t][1]
                pe.wait_ge(d_u, t + 1)
                if t >= 2:
                    pe.wait_ge(u_evac, 2 * (t - 1))
                for k in range(KD):
                    i = TR(ps[2 * (t % 2) + k // 4][:, P * (k % 4):P * (k % 4) + n], utmp[t % 2][0:n, P * k:P * k + P], ident(n))
                    if k % 4 == 3:
                        i.then_inc(u_T, 1)
            pe.wait_ge(u_evac, 10)
            for m in range(12):
                s = m // 4
                pe.wait_ge(slot_in[s], 16)
                if m >= 2:
                    pe.wait_ge(conv_evac, 2 * (m - 1))
                for half in range(2):
                    for k in range(KD):
                        i = M(ps[4 + 2 * (m % 2) + half][:, 0:264], w_group(s)[:, k, P * (m % 4):P * (m % 4) + P],
                              uT[:, k, 264 * half:264 * half + 264], start=(k == 0), stop=(k == KD - 1))
                    i.then_inc(conv_ps, 1)
                if m % 4 == 3:
                    pe.wait_ge(conv_ps, 2 * m + 2)
                    pe.sem_inc(group_used, 1)
                if 2 <= m < 10:
                    pe.wait_ge(conv_sq, m - 1)
                    for t, (at, n) in enumerate(tok_cols):
                        i = M(ps[3][0:n, 8 * t + m - 2:8 * t + m - 1], convsq[m % 2][:, at:at + n], konst_at(K_ONE)[:, 0:1],
                              start=True, stop=True)
                    i.then_inc(qk_ssq, 1)
            for s in (3, 4):
                pe.wait_ge(slot_in[s], 16)
            pe.wait_ge(slot_in[5], 32)
            pe.wait_ge(slot_in[0], 32)
            pe.wait_ge(wkv_in, 16)

            def project(t):
                at, n = tok_cols[t]
                if t:
                    pe.wait_ge(a_proj, 2 * t - 1)
                    pe.wait_ge(d_ckvT, t)
                for b, (w, c0, c1) in enumerate(((w_group(3), 0, 512), (w_group(4), 0, 512), (gC, 0, NPROJ), (w_group(0), 0, 512))):
                    if t == 0 and b in (0, 3):
                        pe.sem_inc(proj_ps, 1)
                        continue
                    if t == 0:
                        c0, c1 = (0, 256) if b == 1 else (328, 336)
                    for k in range(KD):
                        i = M(ps[b][0:n, c0:c1], uT[:, k, at:at + n], w[:, k, c0:c1], start=(k == 0), stop=(k == KD - 1))
                    i.then_inc(proj_ps, 1)

            project(0)
            pe.wait_ge(conv_evac, 24)
            pe.wait_ge(d_ssqc, 1)
            for t, (at, n) in enumerate(tok_cols):
                pe.wait_ge(d_ckv, t + 1)
                if t:
                    pe.wait_ge(d_ropeT, t)
                for k in range(2):
                    i = TR(ps[4][:, P * k:P * k + n], ckv[0:n, P * k:P * k + P], ident(n))
                i.then_inc(ckv_T, 1)
                pe.wait_ge(d_ckvT, t + 1)
                for b in range(2):
                    for k in range(2):
                        i = M(ps[5 + b][0:n, :], ckvT[k][:, 0:n], wkv[:, k, 512 * b:512 * b + 512], start=(k == 0), stop=(k == 1))
                    i.then_inc(kv_ps, 1)
                if t < NT:
                    project(t + 1)
                pe.wait_ge(d_rope, t + 1)
                pe.wait_ge(a_proj, 2 * t + 2)
                for bank, a in ((7, 0), (4, 8), (5, 16), (6, 24)):
                    pairs = 1 if bank == 6 else 4
                    if t == 0 and bank != 4:
                        pe.sem_inc(rope_T, 1)
                        continue
                    for p in range(pairs):
                        src = rp[0:n, a + 2 * p:a + 2 * p + 2, :].rearrange("p a d -> p (a d)")
                        i = TR(ps[bank][:, P * p:P * p + n], src, ident(n))
                    i.then_inc(rope_T, 1)
            pe.wait_ge(rope_T, 20)
            pe.sem_inc(group_used, 1)
            pe.wait_ge(d_ropeT, 5)
            q = 0
            for j in range(1, NT):
                for hh in range(IH):
                    rows = slice(64 * (hh % 2), 64 * (hh % 2) + 64)
                    if q >= 2:
                        pe.wait_ge(i_rel, q - 1)
                    M(ps[q % 2][:, 0:P * (j + 1)], qiT[rows, hh // 2, P * (j - 1):P * j], kiT[rows, 0:P * (j + 1)],
                      start=True, stop=True).then_inc(i_ps, 1)
                    q += 1
            pe.wait_ge(i_rel, q)
            def head_products(c):
                at, n = tok_cols[c]
                k_ = [qkvT[:, 4 + hh, PAD + at:PAD + at + n] for hh in range(BH)]
                pe.wait_ge(f_in, c + 1)
                if c > 1:
                    pe.wait_ge(f_sc, c - 1)
                elif c:
                    pe.wait_ge(f_rest, c)
                for hh in range(BH):
                    hb = slice(P * hh, P * hh + n)
                    M(ps[0][:, hb], F_GB[0:n, hh, :], konst_at(K_UI, n, n), start=True, stop=True)
                    M(ps[1][0:n, hb], k_[hh], k_[hh], start=True, stop=True)
                    M(ps[2][0:n, hb], F_RK[0:n, hh, 0:n], ident(n), start=True, stop=True)
                M(ps[3][0:n, 0:4], konst_at(K_UI, n, n), gg[0:n, c, :], start=True, stop=True).then_inc(f_ps, 1)

            def rest_products(c):
                at, n = tok_cols[c]
                cols = slice(PAD + at, PAD + at + n)
                pe.wait_ge(f_A, c + 1)
                for hh in range(BH):
                    if c:
                        M(ps[0][0:n, P * hh:P * hh + n], qkvT[:, 4 + hh, cols], qkvT[:, hh, cols], start=True, stop=True)
                    TR(ps[1][0:n, P * hh:P * hh + P], qkvT[:, 4 + hh, cols], ident())
                    i = TR(ps[2][0:n, P * hh:P * hh + P], qkvT[:, 8 + hh, cols], ident())
                i.then_inc(f_rest_ps, 1)

            def key_state(c):
                if c == 0:
                    return
                pe.wait_ge(f_sc, c)
                if c < 4:
                    pe.wait_ge(f_rest, c + 2)
                at = PAD + tok_cols[c][0]
                for hh in range(BH):
                    i = M(ps[0][:, P * hh:P * hh + P], qkvT[:, 4 + hh, at:at + P], F_S[:, hh, :], start=True, stop=True)
                i.then_inc(f_ks, 1)

            def new_values(c):
                at, n = tok_cols[c]
                pe.wait_ge(f_r, c + 1)
                if c == 0:
                    pe.wait_ge(f_rest, 2)
                for hh in range(BH):
                    i = M(ps[1][0:n, P * hh:P * hh + P], F_Dt[c % 2][0:n, hh, 0:n], F_R[0:n, hh, :], start=True, stop=True)
                i.then_inc(f_vn, 1)
                if c:
                    for hh in range(BH):
                        M(ps[2][:, P * hh:P * hh + P], qkvT[:, hh, PAD + at:PAD + at + n], F_S[:, hh, :], start=True, stop=True)

            def outputs_and_state(c):
                n = chunk_len(c)
                pe.wait_ge(f_vnc, c + 1)
                if c:
                    for hh in range(BH):
                        i = M(ps[3][:, P * hh:P * hh + P], F_IT[c % 2][:, hh, :], F_VN[:, hh, :], start=True, stop=True)
                    i.then_inc(f_o, 1)
                for hh in range(BH):
                    i = M(ps[4][:, P * hh:P * hh + P], F_KD[c % 2][0:n, hh, :], F_VN[0:n, hh, :], start=True, stop=True)
                i.then_inc(f_s, 1)

            pe.wait_ge(conv_silu, 12)
            head_products(0)
            rest_products(0)
            lvs, es, ys = 0, 0, 0
            for c in range(5):
                n = chunk_len(c)
                pe.wait_ge(f_init, c + 1)
                pe.wait_ge(f_lv, lvs)
                for hh in range(BH):
                    i = TR(ps[7][0:n, P * hh:P * hh + n], F_Y[0:n, hh, 0:n], ident(n))
                i.then_inc(f_lvps, 1)
                lvs += 1
                for lv in levels(c):
                    last = lv == levels(c)[-1]
                    pe.wait_ge(f_lv, lvs)
                    es += 1
                    pe.wait_ge(f_E, es)
                    ys += 1
                    for hh in range(BH):
                        i = M(ps[7][0:n, P * hh:P * hh + n], F_E[lv][0:n, hh, 0:n], F_Dt[c % 2][0:n, hh, 0:n], start=True, stop=True)
                    i.then_inc(f_lvps, 1)
                    pe.wait_ge(f_Y, ys)
                    for hh in range(BH):
                        if not last:
                            M(ps[5][0:n, P * hh:P * hh + n], F_Y[0:n, hh, 0:n], F_D[0:n, hh, 0:n], start=True, stop=True)
                        i = M(ps[6][0:n, P * hh:P * hh + n], F_D[0:n, hh, 0:n], F_Y[0:n, hh, 0:n], start=True, stop=True)
                    i.then_inc(f_lvps, 1)
                    lvs += 1
                    if c and lv == 1:
                        key_state(c - 1)
                    if c and lv == 2:
                        new_values(c - 1)
                    if c and lv == 3:
                        outputs_and_state(c - 1)
                    if c < 4 and lv == (3 if c == 0 else 4):
                        head_products(c + 1)
                    if c < 4 and last:
                        rest_products(c + 1)
            pe.wait_ge(f_lv, lvs)
            key_state(4)
            new_values(4)
            outputs_and_state(4)
            pe.wait_ge(f_sc, 5)

            def attn_scores(q):
                j, hh = q // AH, q % AH
                rows = slice(64 * (hh % 2), 64 * (hh % 2) + 64)
                if q >= 2:
                    pe.wait_ge(a_exp, q - 1)
                lhs = qT[rows, hh // 2, P * j:P * j + P]
                M(ps[5 + q % 2][:, 0:META], lhs, kT[rows, hh // 2, 0:META], start=True, stop=True)
                M(ps[q % 2][:, 0:P * (j + 1)], lhs, kT[rows, hh // 2, META:META + P * (j + 1)], start=True, stop=True)\
                    .then_inc(a_sc, 1)

            def attn_transposes(q):
                pe.wait_ge(a_exp, q + 1)
                for b in range(q // AH + 1):
                    TR(ps[2 + q % 2][:, P * b:P * b + P], prob[q % 3][:, META + P * b:META + P * b + P], ident())
                if q:
                    pe.wait_ge(a_pTc, q)
                TR(ps[4][0:META, 0:P], prob[q % 3][:, 0:META], ident()).then_inc(a_pT, 1)

            def attn_outputs(q):
                j, hh = q // AH, q % AH
                pe.wait_ge(a_pTc, q + 1)
                if hh == 0 and j:
                    pe.wait_ge(a_on, j)
                o = ps[7][:, AD * hh:AD * hh + AD]
                for b in range(j + 1):
                    M(o, pT[q % 2][:, P * b:P * b + P], vA[:, b, AD * hh:AD * hh + AD], start=(b == 0), stop=False)
                i = M(o, pT[q % 2][0:META, 512:640], vM[:, AD * hh:AD * hh + AD], start=False, stop=True)
                if hh == AH - 1:
                    i.then_inc(a_o, 1)

            attn_scores(0)
            attn_scores(1)
            for q in range(NT * AH):
                if q + 2 < NT * AH:
                    attn_scores(q + 2)
                attn_transposes(q)
                if q:
                    attn_outputs(q - 1)
            attn_outputs(NT * AH - 1)
            pe.wait_ge(a_on, NT)
            pe.wait_ge(slot_in[4], 32)
            pe.wait_ge(slot_in[5], 48)
            pe.wait_ge(wr_in, 16)

            def project_out(t):
                for k in range(KD):
                    if t and k % 4 == 0:
                        pe.wait_ge(g_Tc, 2 * (t - 1) + k // 4 + 1)
                    i = TR(ps[k // 4][:, P * (k % 4):P * (k % 4) + P], oab[:, t, P * k:P * k + P], ident())
                    if k % 4 == 3:
                        i.then_inc(g_T, 1)
                pe.wait_ge(g_Tc, 2 * t + 2)
                if t:
                    pe.wait_ge(g_h, t)
                for half in range(2):
                    for k in range(KD):
                        i = M(ps[2 + half][:, :], oT[:, k, :], w_group(4 + half)[:, k, :], start=(k == 0), stop=(k == KD - 1))
                    i.then_inc(g_ps, 1)

            project_out(0)
            for t in range(NT):
                if t + 1 < NT:
                    project_out(t + 1)
                pe.wait_ge(g_xn, t + 1)
                for k in range(KD):
                    i = TR(ps[4 + k // 4][:, P * (k % 4):P * (k % 4) + P], xraw[:, P * k:P * k + P], ident())
                    if k % 4 == 3:
                        i.then_inc(g_xT, 1)
                pe.wait_ge(g_xTc, 2 * t + 2)
                if t:
                    pe.wait_ge(g_sel, t)
                for k in range(KD):
                    i = M(ps[6][:, 0:NE], xT[:, k, :], wr[:, k, :], start=(k == 0), stop=(k == KD - 1))
                i.then_inc(g_lg, 1)
            pe.sem_inc(piece_used, RING)
            pe.wait_ge(g_sel, NT)
            for t in range(NT + 1):
                o = ps[7][:, 32 * t:32 * t + 32]
                for s in range(min(t, NT)):
                    i = M(o, konst_at(K_ONE), selm[:, s, :], start=(s == 0), stop=(t == NT and s == NT - 1))
                if t < NT:
                    i = M(o, konst_at(K_US), selm[:, t, :], start=(t == 0), stop=True)
            i.then_inc(g_rk, NT + 1)
            pe.wait_ge(bias_in, 16 * 5)
            pe.wait_ge(g_gt, 1)
            for t in range(NT):
                i = TR(ps[0][0:NE, P * t:P * t + P], lg[:, t, :], ident())
            i.then_inc(g_gtc, 1)
            pe.wait_ge(g_bd, 1)
            for t in range(NT):
                for half in range(2):
                    if t == NT - 1:
                        pe.wait_ge(g_bd, 2 + half)
                    M(ps[BDOWN[2 * t + half]][:, :], gT[:, P * t:P * t + P], bdn[:, 512 * half:512 * half + 512],
                      start=True, stop=True).then_inc(g_acc, 1)
            pe.sem_inc(g_rk, 1)

            def gather(i):
                pe.wait_ge(p_built, i + 1)
                for k in range(KD):
                    for t in range(NT):
                        for b, part in enumerate(xn):
                            ins = M(ps[6 + k // 4][:, P * (k % 4):P * (k % 4) + P], part[:, D * t + P * k:D * t + P * k + P],
                                    onehot[:, t, :], start=(t == 0 and b == 0), stop=(t == NT - 1 and b == 2))
                    if k % 4 == 3:
                        ins.then_inc(x_ps, 1)

            def scatter(i, q):
                half, t = q // 4, q % 4
                if q == 0:
                    pe.wait_ge(pt_ready, i + 1)
                if t == 0:
                    pe.wait_ge(y_ready, 2 * i + half + 1)
                if q >= 2:
                    pe.wait_ge(acc_added, 8 * i + q - 1)
                c = slice(512 * half, 512 * half + 512)
                M(ps[6 + q % 2][:, :], onehotT[:, t, :], y_hi[:, c], start=True, stop=False)
                M(ps[6 + q % 2][:, :], onehotT[:, t, :], y_lo[:, c], start=False, stop=True).then_inc(scat_ps, 1)

            def products(i, n, k0, bank, hi, lo):
                pe.wait_ge(w_lo_ready, PIECES * i + n + 1)
                for k in (k0, k0 + 1):
                    kk = slice(P * k, P * k + P)
                    wh, wl = (t[n % RING][:, 512 * (k - k0):512 * (k - k0) + 512] for t in (w_hi, w_lo))
                    last = n + 1 in FIRST or n == PIECES - 1
                    M(ps[bank][:, :], hi[:, kk], wh, start=(n in FIRST[4:] and k == 0), stop=False)
                    M(ps[bank][:, :], hi[:, kk], wl, start=False, stop=False)
                    ins = M(ps[bank][:, :], lo[:, kk], wh, start=False, stop=(last and k > k0))
                ins.then_inc(piece_used, 1)

            def gate_up_bias(n):
                M(ps[n][:, :], sel[n // 2][:, :], bias2[:, 512 * (n % 2):512 * (n % 2) + 512], start=True, stop=False)

            gather(0)
            pe.wait_ge(g_bd, 9)
            pe.wait_ge(table_ready, 1)
            items = pe.value_load(nitems_i[0:1, 0:1], min_val=NE, max_val=ITEMS - 1)
            with pe.Fori(0, items) as i:
                pe.wait_ge(xe_whole_ready, i + 1)
                pe.wait_ge(xe_ready, 2 * i + 2)
                for n in range(4):
                    gate_up_bias(n)
                    for j in range(3):
                        if j == 1:
                            pe.wait_ge(w_lo_ready, PIECES * i + 3 * n + 3)
                            for k in range(2):
                                ins = M(ps[n][:, :], xe[:, P * k:P * k + P], slot(n % 3, 512, 512 * k), start=False, stop=False)
                            ins.then_inc(plain_used, 1)
                        products(i, 3 * n + j, 2 * j, n, xe_hi, xe_lo)
                        if (n, j) in SCATTER_AT:
                            scatter(i, SCATTER_AT.index((n, j)))
                        if n == 3 and j == 1:
                            pe.wait_ge(act_ready, 4 * i + 2)
                            for k in range(4):
                                ins = TR(ps[0][:, P * k:P * k + P], act[:, P * k:P * k + P], ident())
                            ins.then_inc(actT_ps, 1)
                    if n == 2:
                        pe.wait_ge(acc_added, 8 * i + 8)
                        for t in range(NT):
                            ins = M(ps[6][:, P * t:P * t + P], onehot[:, t, :], ident_b[:, :], start=True, stop=True)
                        ins.then_inc(pt_ps, 1)
                pe.wait_ge(pt_ready, i + 2)
                gather(i + 1)
                pe.wait_ge(act_ready, 4 * i + 4)
                for k in range(4, KD):
                    ins = TR(ps[1][:, P * (k - 4):P * (k - 4) + P], act[:, P * k:P * k + P], ident())
                ins.then_inc(actT_ps, 1)
                for half in range(2):
                    for j in range(4):
                        if half == 0 and j % 2 == 0:
                            pe.wait_ge(actT_ready, 2 * i + j // 2 + 1)
                        products(i, 12 + 4 * half + j, 2 * j, 4 + half, actT_hi, actT_lo)
            for q in range(2 * NT):
                scatter(items, q)


_INS = ['x', 'meta_tokens', 'norm_mix_w', 'w_in', 'q_norm_w', 'k_norm_w', 'kv_norm_w', 'w_kv_up', 'conv_w', 'a_log',
        'dt_bias', 'delta_norm_w', 'w_out', 'norm_ffn_w', 'w_router', 'b_router', 'w_gate_up', 'b_gate_up', 'w_down', 'b_down']


def kernel(**inputs):
    import numpy as _np
    import concourse.bacc as _bacc
    from concourse import mybir as _mybir
    from concourse.bass_utils import run_bass_kernel_spmd as _run

    nc = _bacc.Bacc("TRN2", target_bir_lowering=False, num_devices=1)
    arrays = {"in_konst": constants()}
    args = [nc.dram_tensor("in_konst", (P, KONST), F32, kind="ExternalInput").ap()]
    for name in _INS:
        a = _np.ascontiguousarray(inputs[name])
        arrays[f"in_{name}"] = a
        args.append(nc.dram_tensor(f"in_{name}", a.shape, _mybir.dt.from_np(a.dtype), kind="ExternalInput").ap())
    args.append(nc.dram_tensor("out_0", (1, SEQ, D), F32, kind="ExternalOutput").ap())
    hybrid_layer(nc, *args)
    r = _run(nc, [arrays], core_ids=[0])
    return r.results[0]["out_0"]
```
